# Optimizing a Trainium2 kernel written in Bass

```python
import jax, jax.numpy as jnp
from jax import lax
import numpy as np
import math

D_MODEL = 1024
BATCH = 1
SEQ = 256
DEPTH = 1

CHUNK = 64
EPS = 1e-6

LRU_WIDTH = D_MODEL
LRU_HEADS = 8
LRU_HEAD_DIM = LRU_WIDTH // LRU_HEADS
LRU_CONV = 4
LRU_C = 8.0

CONV_WIDTH = D_MODEL
CONV_GROUPS = 8
CONV_K = 3

N_BRANCHES = 2
IN_COLS = 2 * LRU_WIDTH + 3 * CONV_WIDTH + N_BRANCHES * D_MODEL

PEER_HEADS = 8
PEER_NKEYS = 128
PEER_N = PEER_NKEYS * PEER_NKEYS
PEER_DKEY = 256
PEER_HALF = PEER_DKEY // 2
PEER_TOPK = 16
PEER_BLOCK = 128


def rmsnorm(x, g):
    xf = x.astype(jnp.float32)
    y = xf * lax.rsqrt(jnp.mean(xf * xf, axis=-1, keepdims=True) + EPS)
    return (y * g.astype(jnp.float32)).astype(x.dtype)

def causal_dwconv(x, w):
    k, c = w.shape
    return lax.conv_general_dilated(
        x, w[:, None, :].astype(x.dtype), window_strides=(1,), padding=[(k - 1, 0)],
        dimension_numbers=("NWC", "WIO", "NWC"), feature_group_count=c)

def rg_lru(x, w_a, b_a, w_x, b_x, lam):
    b, s, _ = x.shape
    xh = x.reshape(b, s, LRU_HEADS, LRU_HEAD_DIM)
    r = jax.nn.sigmoid(jnp.einsum("bshi,hij->bshj", xh, w_a).reshape(b, s, LRU_WIDTH) + b_a)
    i = jax.nn.sigmoid(jnp.einsum("bshi,hij->bshj", xh, w_x).reshape(b, s, LRU_WIDTH) + b_x)
    log_a = (-LRU_C * r.astype(jnp.float32)) * jax.nn.softplus(-lam.astype(jnp.float32))
    a = jnp.exp(log_a)
    mult = jnp.sqrt(-jnp.expm1(2.0 * log_a))
    u = mult * (i * x).astype(jnp.float32)

    def combine(left, right):
        a1, b1 = left
        a2, b2 = right
        return a1 * a2, a2 * b1 + b2

    _, h = lax.associative_scan(combine, (a, u), axis=1)
    return h.astype(x.dtype)

def token_mixers(xn, w_in, conv_a_w, conv_a_b, w_a, b_a, w_x, b_x, lam, conv_b_w, w_out):
    p = xn @ w_in
    splits = [LRU_WIDTH, 2 * LRU_WIDTH, 2 * LRU_WIDTH + CONV_WIDTH,
              2 * LRU_WIDTH + 2 * CONV_WIDTH, 2 * LRU_WIDTH + 3 * CONV_WIDTH,
              2 * LRU_WIDTH + 3 * CONV_WIDTH + D_MODEL]
    xa, ga, vb, bb, cb, ma, mb = jnp.split(p, splits, axis=-1)
    ya = rg_lru(causal_dwconv(xa, conv_a_w) + conv_a_b, w_a, b_a, w_x, b_x, lam) * jax.nn.gelu(ga)
    yb = bb * causal_dwconv(cb * vb, conv_b_w)
    merged = jax.nn.sigmoid(ma) * ya + jax.nn.sigmoid(mb) * yb
    return merged @ w_out

def peer(xn, w_q, sub_keys, u_tab, v_tab):
    b, s, d = xn.shape
    t = xn.reshape(-1, d)
    n_tok = t.shape[0]
    q = (t @ w_q).reshape(n_tok, PEER_HEADS, 2, PEER_HALF)
    sc = jnp.einsum("thpk,hpnk->thpn", q, sub_keys).astype(jnp.float32)
    s_top, i_top = lax.top_k(sc, PEER_TOPK)
    cand = s_top[:, :, 0, :, None] + s_top[:, :, 1, None, :]
    cand_idx = i_top[:, :, 0, :, None] * PEER_NKEYS + i_top[:, :, 1, None, :]
    kk = PEER_TOPK * PEER_TOPK
    best, pos = lax.top_k(cand.reshape(n_tok, PEER_HEADS, kk), PEER_TOPK)
    idx = jnp.take_along_axis(cand_idx.reshape(n_tok, PEER_HEADS, kk), pos, axis=-1)
    g = jax.nn.softmax(best, axis=-1).astype(xn.dtype)

    nb = n_tok // PEER_BLOCK

    def block(args):
        tb, ib, gb = args
        ue = u_tab[ib]
        act = jax.nn.gelu(jnp.einsum("phkd,pd->phk", ue, tb))
        ve = v_tab[ib]
        return jnp.einsum("phk,phkd->pd", gb * act, ve)

    out = lax.map(block, (t.reshape(nb, PEER_BLOCK, d),
                          idx.reshape(nb, PEER_BLOCK, PEER_HEADS, PEER_TOPK),
                          g.reshape(nb, PEER_BLOCK, PEER_HEADS, PEER_TOPK)))
    return out.reshape(b, s, d)

def first_inputs(seed: int = 0) -> dict:
    key = jax.random.key(seed)
    ks = jax.random.split(key, 20)
    f = jnp.float32
    L = DEPTH

    def nrm(k, shape, scale):
        return jax.random.normal(k, shape, f) * scale

    x = nrm(ks[0], (BATCH, SEQ, D_MODEL), 1.0)
    norm1_g = 1.0 + nrm(ks[1], (L, D_MODEL), 0.02)
    w_in = nrm(ks[2], (L, D_MODEL, IN_COLS), D_MODEL ** -0.5)
    conv_a_w = nrm(ks[3], (L, LRU_CONV, LRU_WIDTH), LRU_CONV ** -0.5)
    conv_a_b = nrm(ks[4], (L, LRU_WIDTH), 0.01)
    w_a = nrm(ks[5], (L, LRU_HEADS, LRU_HEAD_DIM, LRU_HEAD_DIM), LRU_HEAD_DIM ** -0.5)
    b_a = nrm(ks[6], (L, LRU_WIDTH), 0.01)
    w_x = nrm(ks[7], (L, LRU_HEADS, LRU_HEAD_DIM, LRU_HEAD_DIM), LRU_HEAD_DIM ** -0.5)
    b_x = nrm(ks[8], (L, LRU_WIDTH), 0.01)
    a_init = jax.random.uniform(ks[9], (L, LRU_WIDTH), f, 0.9, 0.999)
    sig = a_init ** (1.0 / LRU_C)
    lru_lambda = jnp.log(sig) - jnp.log1p(-sig)
    conv_b_w = nrm(ks[10], (L, CONV_K, CONV_WIDTH), CONV_K ** -0.5)
    w_out = nrm(ks[11], (L, D_MODEL, D_MODEL), D_MODEL ** -0.5)
    norm2_g = 1.0 + nrm(ks[12], (L, D_MODEL), 0.02)
    peer_wq = nrm(ks[13], (L, D_MODEL, PEER_HEADS * PEER_DKEY), D_MODEL ** -0.5)
    peer_subkeys = nrm(ks[14], (L, PEER_HEADS, 2, PEER_NKEYS, PEER_HALF), PEER_HALF ** -0.5)
    peer_u = nrm(ks[15], (L, PEER_N, D_MODEL), D_MODEL ** -0.5)
    peer_v = nrm(ks[16], (L, PEER_N, D_MODEL), PEER_HEADS ** -0.5)
    final_g = 1.0 + nrm(ks[17], (D_MODEL,), 0.02)
    return {"x": x, "norm1_g": norm1_g, "w_in": w_in, "conv_a_w": conv_a_w, "conv_a_b": conv_a_b,
            "w_a": w_a, "b_a": b_a, "w_x": w_x, "b_x": b_x, "lru_lambda": lru_lambda,
            "conv_b_w": conv_b_w, "w_out": w_out, "norm2_g": norm2_g, "peer_wq": peer_wq,
            "peer_subkeys": peer_subkeys, "peer_u": peer_u, "peer_v": peer_v, "final_g": final_g}

def first_block(x, norm1_g, w_in, conv_a_w, conv_a_b, w_a, b_a, w_x, b_x, lru_lambda,
              conv_b_w, w_out, norm2_g, peer_wq, peer_subkeys, peer_u, peer_v, final_g):
    h = x
    for l in range(DEPTH):
        xn = rmsnorm(h, norm1_g[l])
        h = h + token_mixers(xn, w_in[l], conv_a_w[l], conv_a_b[l], w_a[l], b_a[l], w_x[l], b_x[l],
                             lru_lambda[l], conv_b_w[l], w_out[l])
        h = h + peer(rmsnorm(h, norm2_g[l]), peer_wq[l], peer_subkeys[l], peer_u[l], peer_v[l])
    return rmsnorm(h, final_g)


DEPTH_2 = 2

N_MIXERS = 4
ROPE_THETA = 500000.0
Q_BLOCK = 128
LN_EPS = 1e-5
RMS_EPS = 1e-6
MAX_POS_OFFSET = 4096
DIFF_HEADS = 8
DIFF_HEAD_DIM = 64
FOX_HEADS = 16
FOX_HEAD_DIM = 64
MLA_HEADS = 16
MLA_NOPE = 64
MLA_ROPE = 32
MLA_V = 64
MLA_Q_RANK = 384
MLA_KV_RANK = 256
MOBA_HEADS = 16
MOBA_HEAD_DIM = 64
MOBA_BLOCK = 256
MOBA_TOPK = 3
MOBA_Q_CHUNK = 32
PARTIAL_ROT = 64 // 4
D_FF = 2816
CONV_WIDTH_2 = 3
DEEPNORM_ALPHA = (2 * DEPTH_2) ** 0.25
DEEPNORM_BETA = (8 * DEPTH_2) ** -0.25


def _n_uses(m):
    return len(range(m, DEPTH_2, N_MIXERS))

def diff_lambda_init(layer):
    return 0.8 - 0.6 * math.exp(-0.3 * layer)

def layer_norm(x, g, b):
    xf = x.astype(jnp.float32)
    mu = xf.mean(-1, keepdims=True)
    var = jnp.square(xf - mu).mean(-1, keepdims=True)
    y = (xf - mu) * lax.rsqrt(var + LN_EPS) * g.astype(jnp.float32) + b.astype(jnp.float32)
    return y.astype(x.dtype)

def rms_norm(x, g):
    xf = x.astype(jnp.float32)
    y = xf * lax.rsqrt(jnp.mean(xf * xf, -1, keepdims=True) + RMS_EPS) * g.astype(jnp.float32)
    return y.astype(x.dtype)

def rotary_angles(positions, rot_dim):
    inv_freq = ROPE_THETA ** (-jnp.arange(0, rot_dim, 2, dtype=jnp.float32) / rot_dim)
    ang = positions.astype(jnp.float32)[..., None] * inv_freq
    return jnp.cos(ang), jnp.sin(ang)

def apply_rotary(x, cos, sin, rot_dim):
    expand = (1,) * (x.ndim - 3)
    cos = cos.reshape(cos.shape[:2] + expand + cos.shape[-1:])
    sin = sin.reshape(sin.shape[:2] + expand + sin.shape[-1:])
    half = rot_dim // 2
    xr = x[..., :rot_dim].astype(jnp.float32)
    x1, x2 = xr[..., :half], xr[..., half:]
    rot = jnp.concatenate([x1 * cos - x2 * sin, x2 * cos + x1 * sin], -1).astype(x.dtype)
    return jnp.concatenate([rot, x[..., rot_dim:]], -1)

def causal_mask(q_start, q_len, k_len):
    q_idx = q_start + jnp.arange(q_len)
    k_idx = jnp.arange(k_len)
    return k_idx[None, :] <= q_idx[:, None]

def masked_softmax(scores, mask):
    s = jnp.where(mask, scores.astype(jnp.float32), -jnp.inf)
    return jax.nn.softmax(s, axis=-1)

def sweep_query_blocks(block_fn, seq, block):
    starts = jnp.arange(seq // block) * block
    out = lax.map(block_fn, starts)
    n, b, blk, f = out.shape
    return out.transpose(1, 0, 2, 3).reshape(b, n * blk, f)

def diff_attention(x, cos, sin, w_qkv, lam_q1, lam_k1, lam_q2, lam_k2, subln_g, w_o, lambda_init):
    B, S, _ = x.shape
    H, d = DIFF_HEADS, DIFF_HEAD_DIM
    q, k, v = jnp.split(x @ w_qkv, 3, axis=-1)
    q = apply_rotary(q.reshape(B, S, H, 2, d), cos, sin, PARTIAL_ROT).transpose(0, 2, 3, 1, 4)
    k = apply_rotary(k.reshape(B, S, H, 2, d), cos, sin, PARTIAL_ROT).transpose(0, 2, 3, 1, 4)
    v = v.reshape(B, S, H, 2 * d).transpose(0, 2, 1, 3)
    f32 = jnp.float32
    lam = (jnp.exp(jnp.sum(lam_q1.astype(f32) * lam_k1.astype(f32)))
           - jnp.exp(jnp.sum(lam_q2.astype(f32) * lam_k2.astype(f32))) + lambda_init)
    scale = d ** -0.5

    def block(start):
        qb = lax.dynamic_slice_in_dim(q, start, Q_BLOCK, axis=3)
        s = jnp.einsum('bhcqd,bhckd->bhcqk', qb, k) * scale
        p = masked_softmax(s, causal_mask(start, Q_BLOCK, S))
        a = (p[:, :, 0] - lam * p[:, :, 1]).astype(v.dtype)
        o = jnp.einsum('bhqk,bhkd->bqhd', a, v)
        o = rms_norm(o, subln_g) * (1.0 - lambda_init)
        return o.reshape(B, Q_BLOCK, H * 2 * d)

    return sweep_query_blocks(block, S, Q_BLOCK) @ w_o

def forgetting_attention(x, w_in, b_f, w_o):
    B, S, _ = x.shape
    H, d = FOX_HEADS, FOX_HEAD_DIM
    q, k, v, f_logit = jnp.split(x @ w_in, [H * d, 2 * H * d, 3 * H * d], axis=-1)
    q = q.reshape(B, S, H, d).transpose(0, 2, 1, 3)
    k = k.reshape(B, S, H, d).transpose(0, 2, 1, 3)
    v = v.reshape(B, S, H, d).transpose(0, 2, 1, 3)
    log_f = jax.nn.log_sigmoid((f_logit + b_f).astype(jnp.float32))
    c = jnp.cumsum(log_f, axis=1).transpose(0, 2, 1)
    scale = d ** -0.5

    def block(start):
        qb = lax.dynamic_slice_in_dim(q, start, Q_BLOCK, axis=2)
        cb = lax.dynamic_slice_in_dim(c, start, Q_BLOCK, axis=2)
        s = (jnp.einsum('bhqd,bhkd->bhqk', qb, k).astype(jnp.float32) * scale
             + cb[..., :, None] - c[..., None, :])
        p = masked_softmax(s, causal_mask(start, Q_BLOCK, S)).astype(v.dtype)
        o = jnp.einsum('bhqk,bhkd->bqhd', p, v)
        return o.reshape(B, Q_BLOCK, H * d)

    return sweep_query_blocks(block, S, Q_BLOCK) @ w_o

def latent_attention(x, cos, sin, w_down, q_norm_g, kv_norm_g, w_uq, w_ukv, w_o):
    B, S, _ = x.shape
    H = MLA_HEADS
    c_q, c_kv, k_rope = jnp.split(x @ w_down, [MLA_Q_RANK, MLA_Q_RANK + MLA_KV_RANK], axis=-1)
    c_q = rms_norm(c_q, q_norm_g)
    c_kv = rms_norm(c_kv, kv_norm_g)
    q = (c_q @ w_uq).reshape(B, S, H, MLA_NOPE + MLA_ROPE)
    q_nope = q[..., :MLA_NOPE].transpose(0, 2, 1, 3)
    q_rope = apply_rotary(q[..., MLA_NOPE:], cos, sin, MLA_ROPE).transpose(0, 2, 1, 3)
    kv = (c_kv @ w_ukv).reshape(B, S, H, MLA_NOPE + MLA_V)
    k_nope = kv[..., :MLA_NOPE].transpose(0, 2, 1, 3)
    v = kv[..., MLA_NOPE:].transpose(0, 2, 1, 3)
    k_rope = apply_rotary(k_rope, cos, sin, MLA_ROPE)
    scale = (MLA_NOPE + MLA_ROPE) ** -0.5

    def block(start):
        qn = lax.dynamic_slice_in_dim(q_nope, start, Q_BLOCK, axis=2)
        qr = lax.dynamic_slice_in_dim(q_rope, start, Q_BLOCK, axis=2)
        s = (jnp.einsum('bhqd,bhkd->bhqk', qn, k_nope)
             + jnp.einsum('bhqr,bkr->bhqk', qr, k_rope)) * scale
        p = masked_softmax(s, causal_mask(start, Q_BLOCK, S)).astype(v.dtype)
        o = jnp.einsum('bhqk,bhkd->bqhd', p, v)
        return o.reshape(B, Q_BLOCK, H * MLA_V)

    return sweep_query_blocks(block, S, Q_BLOCK) @ w_o

def moba_attention(x, cos, sin, w_qkv, w_o):
    B, S, _ = x.shape
    H, d, BS, QC = MOBA_HEADS, MOBA_HEAD_DIM, MOBA_BLOCK, MOBA_Q_CHUNK
    q, k, v = jnp.split(x @ w_qkv, 3, axis=-1)
    q = apply_rotary(q.reshape(B, S, H, d), cos, sin, PARTIAL_ROT).transpose(0, 2, 1, 3)
    k = apply_rotary(k.reshape(B, S, H, d), cos, sin, PARTIAL_ROT).transpose(0, 2, 1, 3)
    v = v.reshape(B, S, H, d).transpose(0, 2, 1, 3)
    nb = -(-S // BS)
    pad = nb * BS - S
    k_blocks = jnp.pad(k, ((0, 0), (0, 0), (0, pad), (0, 0))).reshape(B, H, nb, BS, d)
    v_blocks = jnp.pad(v, ((0, 0), (0, 0), (0, pad), (0, 0))).reshape(B, H, nb, BS, d)
    k_mean = k_blocks.astype(jnp.float32).mean(axis=3).astype(k.dtype)
    topk = min(MOBA_TOPK, max(nb - 1, 1))
    bidx = jnp.arange(B)[:, None, None, None]
    hidx = jnp.arange(H)[None, :, None, None]
    scale = d ** -0.5

    def chunk(start):
        qc = lax.dynamic_slice_in_dim(q, start, QC, axis=2)
        cur = start // BS
        gate = jnp.einsum('bhqd,bhnd->bhqn', qc, k_mean).astype(jnp.float32)
        gate = jnp.where(jnp.arange(nb) < cur, gate, -jnp.inf)
        _, idx = lax.top_k(gate, topk)
        sel_ok = idx < cur
        k_sel = k_blocks[bidx, hidx, idx]
        v_sel = v_blocks[bidx, hidx, idx]
        s_sel = jnp.einsum('bhqd,bhqnkd->bhqnk', qc, k_sel).reshape(B, H, QC, topk * BS)
        k_own = lax.dynamic_index_in_dim(k_blocks, cur, axis=2, keepdims=False)
        v_own = lax.dynamic_index_in_dim(v_blocks, cur, axis=2, keepdims=False)
        s_own = jnp.einsum('bhqd,bhkd->bhqk', qc, k_own)
        own_mask = (cur * BS + jnp.arange(BS))[None, :] <= (start + jnp.arange(QC))[:, None]
        s = jnp.concatenate([s_sel, s_own], -1) * scale
        mask = jnp.concatenate([jnp.repeat(sel_ok, BS, axis=-1),
                                jnp.broadcast_to(own_mask, (B, H, QC, BS))], -1)
        p = masked_softmax(s, mask).astype(v.dtype)
        p_sel = p[..., :topk * BS].reshape(B, H, QC, topk, BS)
        o = (jnp.einsum('bhqnk,bhqnkd->bqhd', p_sel, v_sel)
             + jnp.einsum('bhqk,bhkd->bqhd', p[..., topk * BS:], v_own))
        return o.reshape(B, QC, H * d)

    return sweep_query_blocks(chunk, S, QC) @ w_o

def conv_ffn(x, w_in, conv_w, conv_b, w_out):
    gate, up = jnp.split(x @ w_in, 2, axis=-1)
    gate = lax.conv_general_dilated(
        gate, conv_w[:, None, :], window_strides=(1,), padding=[(CONV_WIDTH_2 - 1, 0)],
        dimension_numbers=('NWC', 'WIO', 'NWC'), feature_group_count=D_FF) + conv_b
    return (jax.nn.silu(gate) * up) @ w_out

def second_inputs(seed: int = 0) -> dict:
    key = jax.random.key(seed)
    keys = iter(jax.random.split(key, 32))
    f32 = jnp.float32

    def normal(shape, std):
        return std * jax.random.normal(next(keys), shape, f32)

    def gain(shape):
        return 1.0 + normal(shape, 0.02)

    n_diff, n_fox, n_mla, n_moba = [_n_uses(m) for m in range(N_MIXERS)]
    D = D_MODEL
    beta = DEEPNORM_BETA
    x = normal((BATCH, SEQ, D), 1.0)
    offset = jax.random.randint(next(keys), (BATCH, 1), 0, MAX_POS_OFFSET, dtype=jnp.int32)
    positions = jnp.arange(SEQ, dtype=jnp.int32)[None, :] + offset
    diff_w = DIFF_HEADS * 2 * DIFF_HEAD_DIM
    fox_w = FOX_HEADS * FOX_HEAD_DIM
    moba_w = MOBA_HEADS * MOBA_HEAD_DIM
    return {
        'x': x,
        'positions': positions,
        'diff_w_qkv': normal((n_diff, D, 3 * diff_w), D ** -0.5),
        'diff_lambda_q1': normal((n_diff, DIFF_HEAD_DIM), 0.1),
        'diff_lambda_k1': normal((n_diff, DIFF_HEAD_DIM), 0.1),
        'diff_lambda_q2': normal((n_diff, DIFF_HEAD_DIM), 0.1),
        'diff_lambda_k2': normal((n_diff, DIFF_HEAD_DIM), 0.1),
        'diff_subln_g': gain((n_diff, 2 * DIFF_HEAD_DIM)),
        'diff_w_o': normal((n_diff, diff_w, D), beta * diff_w ** -0.5),
        'fox_w_in': normal((n_fox, D, 3 * fox_w + FOX_HEADS), D ** -0.5),
        'fox_b_f': jax.random.uniform(next(keys), (n_fox, FOX_HEADS), f32, 1.0, 5.0),
        'fox_w_o': normal((n_fox, fox_w, D), beta * fox_w ** -0.5),
        'mla_w_down': normal((n_mla, D, MLA_Q_RANK + MLA_KV_RANK + MLA_ROPE), D ** -0.5),
        'mla_q_norm_g': gain((n_mla, MLA_Q_RANK)),
        'mla_kv_norm_g': gain((n_mla, MLA_KV_RANK)),
        'mla_w_uq': normal((n_mla, MLA_Q_RANK, MLA_HEADS * (MLA_NOPE + MLA_ROPE)), MLA_Q_RANK ** -0.5),
        'mla_w_ukv': normal((n_mla, MLA_KV_RANK, MLA_HEADS * (MLA_NOPE + MLA_V)), MLA_KV_RANK ** -0.5),
        'mla_w_o': normal((n_mla, MLA_HEADS * MLA_V, D), beta * (MLA_HEADS * MLA_V) ** -0.5),
        'moba_w_qkv': normal((n_moba, D, 3 * moba_w), D ** -0.5),
        'moba_w_o': normal((n_moba, moba_w, D), beta * moba_w ** -0.5),
        'ffn_w_in': normal((DEPTH_2, D, 2 * D_FF), D ** -0.5),
        'ffn_conv_w': normal((DEPTH_2, CONV_WIDTH_2, D_FF), CONV_WIDTH_2 ** -0.5),
        'ffn_conv_b': normal((DEPTH_2, D_FF), 0.02),
        'ffn_w_out': normal((DEPTH_2, D_FF, D), beta * D_FF ** -0.5),
        'ln1_g': gain((DEPTH_2, D)),
        'ln1_b': normal((DEPTH_2, D), 0.02),
        'ln2_g': gain((DEPTH_2, D)),
        'ln2_b': normal((DEPTH_2, D), 0.02),
    }

def second_block(x, positions, diff_w_qkv, diff_lambda_q1, diff_lambda_k1, diff_lambda_q2, diff_lambda_k2,
              diff_subln_g, diff_w_o, fox_w_in, fox_b_f, fox_w_o, mla_w_down, mla_q_norm_g, mla_kv_norm_g,
              mla_w_uq, mla_w_ukv, mla_w_o, moba_w_qkv, moba_w_o, ffn_w_in, ffn_conv_w, ffn_conv_b,
              ffn_w_out, ln1_g, ln1_b, ln2_g, ln2_b):
    cos_p, sin_p = rotary_angles(positions, PARTIAL_ROT)
    cos_m, sin_m = rotary_angles(positions, MLA_ROPE)
    h = x
    for i in range(DEPTH_2):
        m, u = i % N_MIXERS, i // N_MIXERS
        if m == 0:
            y = diff_attention(h, cos_p, sin_p, diff_w_qkv[u], diff_lambda_q1[u], diff_lambda_k1[u],
                               diff_lambda_q2[u], diff_lambda_k2[u], diff_subln_g[u], diff_w_o[u],
                               diff_lambda_init(i))
        elif m == 1:
            y = forgetting_attention(h, fox_w_in[u], fox_b_f[u], fox_w_o[u])
        elif m == 2:
            y = latent_attention(h, cos_m, sin_m, mla_w_down[u], mla_q_norm_g[u], mla_kv_norm_g[u],
                                 mla_w_uq[u], mla_w_ukv[u], mla_w_o[u])
        else:
            y = moba_attention(h, cos_p, sin_p, moba_w_qkv[u], moba_w_o[u])
        h = layer_norm(DEEPNORM_ALPHA * h + y, ln1_g[i], ln1_b[i])
        f = conv_ffn(h, ffn_w_in[i], ffn_conv_w[i], ffn_conv_b[i], ffn_w_out[i])
        h = layer_norm(DEEPNORM_ALPHA * h + f, ln2_g[i], ln2_b[i])
    return h


def setup_inputs(seed=0):
    out = dict(first_inputs(seed))
    for name, value in second_inputs(seed + 1).items():
        if name != "x":
            out[name + "_2"] = value
    return out


def reference(
    x, norm1_g, w_in, conv_a_w, conv_a_b, w_a, b_a, w_x, b_x, lru_lambda, conv_b_w, w_out,
    norm2_g, peer_wq, peer_subkeys, peer_u, peer_v, final_g, positions_2, diff_w_qkv_2,
    diff_lambda_q1_2, diff_lambda_k1_2, diff_lambda_q2_2, diff_lambda_k2_2, diff_subln_g_2,
    diff_w_o_2, fox_w_in_2, fox_b_f_2, fox_w_o_2, mla_w_down_2, mla_q_norm_g_2, mla_kv_norm_g_2,
    mla_w_uq_2, mla_w_ukv_2, mla_w_o_2, moba_w_qkv_2, moba_w_o_2, ffn_w_in_2, ffn_conv_w_2,
    ffn_conv_b_2, ffn_w_out_2, ln1_g_2, ln1_b_2, ln2_g_2, ln2_b_2,
):
    x = first_block(
        x, norm1_g, w_in, conv_a_w, conv_a_b, w_a, b_a, w_x, b_x, lru_lambda, conv_b_w, w_out,
        norm2_g, peer_wq, peer_subkeys, peer_u, peer_v, final_g,
    )
    return second_block(
        x, positions_2, diff_w_qkv_2, diff_lambda_q1_2, diff_lambda_k1_2, diff_lambda_q2_2,
        diff_lambda_k2_2, diff_subln_g_2, diff_w_o_2, fox_w_in_2, fox_b_f_2, fox_w_o_2,
        mla_w_down_2, mla_q_norm_g_2, mla_kv_norm_g_2, mla_w_uq_2, mla_w_ukv_2, mla_w_o_2,
        moba_w_qkv_2, moba_w_o_2, ffn_w_in_2, ffn_conv_w_2, ffn_conv_b_2, ffn_w_out_2, ln1_g_2,
        ln1_b_2, ln2_g_2, ln2_b_2,
    )


_drawn_inputs = setup_inputs


def setup_inputs(seed=0):
    import zlib

    import numpy as np

    out = dict(_drawn_inputs(seed))
    spreads = {}
    factors = {'b_a': 37.703,
     'b_x': 25.341,
     'diff_lambda_q2_2': 8.0,
     'diff_lambda_k2_2': 8.0,
     'diff_subln_g_2': 86.277,
     'ffn_conv_b_2': 8.0,
     'diff_lambda_q1_2': 64.0,
     'diff_lambda_k1_2': 8.0}
    for name, (base, spread) in spreads.items():
        noise = np.random.default_rng([zlib.crc32(name.encode()), seed]).standard_normal(out[name].shape)
        drawn = base * np.exp(spread * noise) if base else spread * noise
        out[name] = __import__('jax').numpy.asarray(drawn.astype(out[name].dtype))
    for name, factor in factors.items():
        out[name] = (out[name] * factor).astype(out[name].dtype)
    return out
```

```python
import math
from contextlib import ExitStack

import numpy as np

import concourse.bass as bass
from concourse import mybir

F32 = mybir.dt.float32
I32 = mybir.dt.int32
U32 = mybir.dt.uint32
ALU = mybir.AluOpType
ACT = mybir.ActivationFunctionType
AX = mybir.AxisListType

SEQ, D = 256, 1024
PARTS = 128
TB = SEQ // PARTS
KC = D // PARTS
HALF = 512
EPS_RMS, EPS_LN = 1e-6, 1e-5
MIX_GROUPS = 7
HEADS, NKEYS, TOPK = 8, 128, 16
D_FF = 2816
FF_CHUNKS = D_FF // PARTS
ALPHA = 4 ** 0.25
LAMBDA_INIT = 0.8 - 0.6 * math.exp(0.0)
SCALE = 64 ** -0.5
MASKED = -1e30
GELU_C, GELU_A = math.sqrt(2.0 / math.pi), 0.044715
TWO_PI_PARTS = (6.28125, 0.0019350051879882812, 3.019916050561733e-07)
ROUND = 1.5 * 2.0 ** 23
G1, CA, CAB, BA, BX, LAM, CB, G2, SP4, NSP4, HBA, HBX = 0, 1, 5, 6, 7, 8, 9, 12, 13, 14, 15, 16
NP = 17
IDENT, PERM, IOTA, MASK, FREQ, HSEL = 0, 128, 256, 384, 896, 897
NCONST = 913
ARENA = 32768


class Chain:

    def __init__(self, eng, sem):
        self.eng, self.sem, self.base, self.n = eng, sem, 0, 0
        self.it, self.per = None, 0

    def enter(self, it, per, rounds_before=0):
        self.it, self.per = it, per
        self.start, self.first = self.base + self.n, rounds_before
        self.base, self.n = self.start, 0

    def leave(self, rounds):
        assert self.n == self.per, (self.n, self.per)
        self.base, self.n, self.it = self.start + rounds * self.per, 0, None

    def step(self, ins):
        ins.then_inc(self.sem, 1)
        self.n += 1
        return ins

    def wait(self):
        if self.it is None:
            self.eng.wait_ge(self.sem, self.base + self.n)
        else:
            self.eng.wait_ge(self.sem, (self.it - self.first) * self.per + (self.base + self.n))

    def link(self, ins):
        self.step(ins)
        self.wait()


RING_PLAN = [
    ("mix", KC, (0, 1, 2, 3, 4, 5, 6, 7)),
    ("mix_out", 1, (0, 1, 2, 3, 4, 5, 6, 7)),
    ("query", 4, (0, 1, 2, 3)),
    ("expert", 32, (4, 5, 6, 7, 0, 1, 2, 3)),
    ("diff_v", 1, (0, 1, 2, 3, 4, 5, 6, 7)),
    ("diff_qk", 4, (4, 5, 6, 7)),
    ("diff_out", 1, (0, 1, 2, 3, 4, 5, 6, 7)),
    ("ffn0", 11, (0, 1, 2, 3, 4, 5)),
    ("fox_v", 1, (6, 7, 0, 1, 2, 3, 4, 5)),
    ("fox_qk", 4, (4, 5, 6, 7)),
    ("fox_out", 1, (0, 1, 2, 3, 4, 5, 6, 7)),
    ("ffn1", 11, (0, 1, 2, 3, 4, 5)),
]


def uses_before(phase, slot):
    count = 0
    for name, rounds, slots in RING_PLAN:
        if name == phase:
            return count
        count += rounds * slots.count(slot)
    raise KeyError(phase)


def build(nc, x, w_mix, w_gate, w_out, w_query, keys, u_tab, v_tab, diff_qk, diff_v, diff_out,
          fox_qk, fox_v, fox_f, fox_out, ffn_in, ffn_out, consts_in, params_in, ffn_params_in,
          rows_in, subln_in, lambdas_in, forget_bias_in, positions_in, out):
    ctx = ExitStack()
    with ctx:
        def sb(name, shape, dt=F32):
            return ctx.enter_context(nc.sbuf_tensor(name, shape, dt))

        def sem(name):
            return ctx.enter_context(nc.semaphore(name))

        ring = sb("ring", [PARTS, 8 * D])
        h_tok = sb("h_tok", [PARTS, TB * D])
        xT = sb("xT", [PARTS, KC * SEQ])
        tmp = sb("tmp", [PARTS, TB * D])
        rows = sb("rows", [PARTS, 2 * D])
        consts = sb("consts", [PARTS, NCONST])
        params = sb("params", [PARTS, KC * NP])
        ffn_params = sb("ffn_params", [PARTS, 2 * FF_CHUNKS * 4])
        stats = sb("stats", [PARTS, 64])
        arena = sb("arena", [PARTS, ARENA])
        coef = sb("coef", [PARTS, 4 * SEQ])
        chosen = sb("chosen", [PARTS, 3 * SEQ])
        ps = ctx.enter_context(nc.psum_tensor("ps", [PARTS, 8 * HALF], F32))

        def bank(b, lo=0, n=HALF):
            return ps[:, b * HALF + lo:b * HALF + lo + n]

        def slot(s, lo=0, n=D):
            return ring[:, s * D + lo:s * D + lo + n]

        def part(lo, n):
            return arena[:, lo:lo + n]

        def at(t, start, n):
            return t[:, bass.ds(start, n)]

        ident = consts[:, IDENT:IDENT + PARTS]
        perm = consts[:, PERM:PERM + PARTS]
        iota = consts[:, IOTA:IOTA + PARTS]
        mask = consts[:, MASK:MASK + 512]
        freq = consts[:, FREQ:FREQ + 1]
        head_sel = consts[:, HSEL:HSEL + 16]

        M_G1, M_G2, M_A, M_IX, M_M, M_OUT = (2048 * n for n in range(6))
        keysT = part(12288, 16 * PARTS)
        mx = 14336
        xc = part(mx, 256)
        vb_sb, cv, yb, ybb, sq, inner, tg, gg = (part(mx + 256 * n, 256) for n in range(1, 9))
        tm = part(mx + 2304, 512)
        tr, ti, tt, t1, rc = (part(mx + 2816 + 256 * n, 256) for n in range(5))
        pst = part(mx + 4096, NP)
        qs = part(0, 4 * SEQ)
        sc = [part(1024 + 1024 * n, 1024) for n in range(2)]
        rest = part(3072, 1024)
        cand, cand2 = part(4096, 1024), part(5120, 1024)
        eqs = part(6144, 1024)
        top1, idxf = part(7168, 128), part(7296, 128)
        idxu = part(7424, 128).bitcast(U32)
        posu = part(7552, 64).bitcast(U32)
        digit = part(7616, 64).bitcast(U32)
        digitf = part(7680, 64)
        best = part(7744, 64)
        sel = part(7808, 3 * SEQ)
        expsum = part(8576, 32)
        v_tok = part(0, TB * D)
        bias_rows = part(2048, 16 * SEQ)
        o_tok = part(6144, TB * D)
        qk = [part(8192 + 512 * n, 512) for n in range(2)]
        qkr = [part(9216 + 512 * n, 512) for n in range(2)]
        rot = part(10240, 512)
        sm = part(10752, 1024)
        pr = part(11776, 1024)
        pT = part(12800, 768)
        att = part(13568, 512)
        squares = part(14080, 2 * PARTS)
        fz_e = part(14336, SEQ)[0:16, :]
        conv = [part(0 + 256 * n, 256) for n in range(2)]
        act = [part(512 + 256 * n, 256) for n in range(2)]
        hid = [part(1024 + 256 * n, 256) for n in range(2)]
        fpst = [part(1536 + 4 * n, 4) for n in range(2)]
        rope = sb("rope", [PARTS, 2 * SEQ])
        subln = sb("subln", [PARTS, PARTS])
        lambdas = part(21504, 4 * 64)
        wf, fbias = chosen[:, 0:KC * 16], chosen[:, KC * 16:KC * 16 + 1]
        ones256 = sb("ones", [PARTS, SEQ])
        ones = ones256[:, 0:PARTS]
        one_hot = [tmp[:, 512 * n:512 * n + 512] for n in range(4)]
        one_hot_w = [rows[:, 512 * n:512 * n + 512] for n in range(4)]
        halfpow = stats[:, 0:2]
        sumsq, var, rstd, negmean = (stats[:, 2 + 2 * n:4 + 2 * n] for n in range(4))
        sum4 = stats[:, 10:14]
        mx4, nb4, l4, rl4 = (stats[:, 14 + 4 * n:18 + 4 * n] for n in range(4))
        nlam = stats[:, 30:31]
        rl2 = stats[:, 32:34]
        lam2 = stats[:, 34:36]
        osq, ovar, orstd = (stats[:, 36 + 2 * n:38 + 2 * n] for n in range(3))
        halfpow2 = stats[:, 42:44]

        slot_loaded = [sem(f"slot_loaded{s}") for s in range(8)]
        slot_done = [sem(f"slot_done{s}") for s in range(8)]
        x_loaded, consts_loaded, small_loaded = sem("x_loaded"), sem("consts_loaded"), sem("small_loaded")
        keys_loaded, rows_loaded, pos_loaded = sem("keys_loaded"), sem("rows_loaded"), sem("pos_loaded")
        stored, fox_loaded = sem("stored"), sem("fox_loaded")
        dve_steps, act_steps = sem("dve_steps"), sem("act_steps")
        pool_ready = sem("pool_ready")
        h_ready, sumsq_ready, var_ready, rstd_ready = (sem(n) for n in ("h_ready", "sumsq_ready", "var_ready", "rstd_ready"))
        normed, turned, xT_ready = sem("normed"), sem("turned"), sem("xT_ready")
        lam_neg, lam_exp, params_ready = sem("lam_neg"), sem("lam_exp"), sem("params_ready")
        pst_ready, xc_ready, vb_ready, cv_done = (sem(n) for n in ("pst_ready", "xc_ready", "vb_ready", "cv_done"))
        bb_used, sq_ready, inner_ready, tg_ready = (sem(n) for n in ("bb_used", "sq_ready", "inner_ready", "tg_ready"))
        ga_used, tm_ready, tm_used, ri_ready = (sem(n) for n in ("ga_used", "tm_ready", "tm_used", "ri_ready"))
        tt_ready, decay_ready, m_ready, root_ready = (sem(n) for n in ("tt_ready", "decay_ready", "m_ready", "root_ready"))
        merged_ready = sem("merged_ready")
        q_ready, score_done, sc_ready, sc_used = (sem(n) for n in ("q_ready", "score_done", "sc_ready", "sc_used"))
        shifted_ready, exp_ready, sel_ready, sel_turned, chosen_ready = (
            sem(n) for n in ("shifted_ready", "exp_ready", "sel_ready", "sel_turned", "chosen_ready"))
        one_hots_ready, scat_done, w_written = sem("one_hots_ready"), sem("scat_done"), sem("w_written")
        gelu_ready, coef_ready = sem("gelu_ready"), sem("coef_ready")
        angle_ready, rope_ready, lamdot_ready, lamexp_ready = (
            sem(n) for n in ("angle_ready", "rope_ready", "lamdot_ready", "lamexp_ready"))
        att_sems = []
        for kind in ("diff", "fox"):
            att_sems.append({n: sem(f"{kind}_{n}") for n in (
                "v_ready", "qk_ready", "rotated", "rope_done", "scores_done", "max_ready", "probs_ready",
                "mixed_ready", "turned", "turned_ready", "pv_done", "osq_ready", "ovar_ready",
                "orstd_ready", "o_ready", "masked")})
        f_done, fz_ready, fexp_ready, bias_ready = (sem(n) for n in ("f_done", "fz_ready", "fexp_ready", "bias_ready"))
        ffn_sems = [{n: sem(f"ffn{l}_{n}") for n in ("conv_ready", "silu_ready", "hid_ready")} for l in range(2)]
        block = ctx.enter_context(nc.Block())

        def rounds(eng, n, body):
            body(0)
            with eng.Fori(1, n) as it:
                body(it)

        def opening(it):
            return isinstance(it, int) and it == 0

        def following(it, e):
            return (it, 1) if e == 0 else (it + 1, 0)

        def all_pairs(eng, body, n=4, chain=None, steps=0, last_steps=0):
            body(0, 0)
            body(0, 1)
            with eng.Fori(1, n - 1) as it:
                if chain:
                    chain.enter(it, steps, 1)
                body(it, 0)
                body(it, 1)
            if chain:
                chain.leave(n - 2)
            body(n - 1, 0)
            body(n - 1, 1, last=True)

        def phase_slots(phase):
            return {name: slots for name, _, slots in RING_PLAN}[phase]

        @block.sync
        def _(sp):
            def load(phase, s, src, turn=0, cols=D):
                if not (isinstance(turn, int) and turn + uses_before(phase, s) == 0):
                    sp.wait_ge(slot_done[s], turn + uses_before(phase, s))
                sp.dma_start(slot(s, 0, cols), src).then_inc(slot_loaded[s], 16)

            def pick(t, i):
                return t[i] if isinstance(i, int) else t[bass.ds(i, 1)].rearrange("o p n -> (o p) n")

            def mix_round(c):
                for g in range(MIX_GROUPS):
                    load("mix", g, pick(w_mix[g], c), c)
                load("mix", 7, pick(w_gate, c), c, 2 * PARTS)

            rounds(sp, KC, mix_round)
            for k in range(KC):
                load("mix_out", k, w_out[k])
            for it in range(4):
                for q in range(4):
                    load("query", q, w_query[4 * it + q], it)

            def expert_u(q, it):
                load("expert", 4 + q, pick(u_tab, it * 4 + q), it)

            def expert_v(q, it):
                load("expert", q, pick(v_tab, it * 4 + q), it)

            for q in range(4):
                expert_u(q, 0)
            with sp.Fori(0, 31) as it:
                for q in range(4):
                    expert_v(q, it)
                    expert_u(q, it + 1)
            for q in range(4):
                expert_v(q, 31)

            def attention_weights(kind, v_src, qk_src, out_src):
                for k, s in enumerate(dict((n, t) for n, _, t in RING_PLAN)[f"{kind}_v"]):
                    load(f"{kind}_v", s, v_src[k])
                with sp.Fori(0, 4) as it:
                    for n in range(4):
                        load(f"{kind}_qk", 4 + n, pick(qk_src, it * 4 + n), it)
                for k in range(KC):
                    load(f"{kind}_out", k, out_src[k])

            def ffn_weights(l):
                with sp.Fori(0, FF_CHUNKS // 2) as it:
                    for e in range(2):
                        load(f"ffn{l}", 3 * e, pick(ffn_in[l], it * 4 + 2 * e), it)
                        load(f"ffn{l}", 3 * e + 1, pick(ffn_in[l], it * 4 + 2 * e + 1), it)
                        load(f"ffn{l}", 3 * e + 2, pick(ffn_out[l], it * 2 + e), it)

            attention_weights("diff", diff_v, diff_qk, diff_out)
            ffn_weights(0)
            attention_weights("fox", fox_v, fox_qk, fox_out)
            ffn_weights(1)
            sp.wait_ge(normed, 7)
            sp.dma_start(out, h_tok[:, :].rearrange("p (b d) -> p b d", b=TB)).then_inc(stored, 16)
            sp.wait_ge(stored, 16)

        @block.gpsimd
        def _(pool):
            pool.memset(stats[:, :], -0.5).then_inc(pool_ready, 1)
            pool.memset(ones256[:, :], 1.0).then_inc(pool_ready, 1)

            def inverse_roots(first, last):
                for k in range(first, last):
                    pool.wait_ge(var_ready, k + 1)
                    pool.tensor_tensor(rstd, var, halfpow, ALU.pow).then_inc(rstd_ready, 1)

            pool.wait_ge(pool_ready, 1)
            inverse_roots(0, 3)
            s = att_sems[0]
            with pool.Fori(0, HEADS) as it:
                pool.wait_ge(s["ovar_ready"], it + 1)
                pool.tensor_tensor(orstd, ovar, halfpow2, ALU.pow).then_inc(s["orstd_ready"], 1)
            inverse_roots(3, 7)

        @block.scalar
        def _(a):
            chain = Chain(a, act_steps)
            a.dma_start(h_tok[:, :].rearrange("p (b d) -> p b d", b=TB), x).then_inc(x_loaded, 16)
            a.dma_start(consts[:, :], consts_in).then_inc(consts_loaded, 16)
            a.dma_start(params[:, :], params_in).then_inc(small_loaded, 16)
            a.dma_start(rope[:, 0:SEQ].bitcast(I32), positions_in.partition_broadcast(PARTS)).then_inc(pos_loaded, 16)
            a.dma_start(keysT, keys).then_inc(keys_loaded, 16)
            a.dma_start(ffn_params[:, :], ffn_params_in).then_inc(small_loaded, 16)
            a.dma_start(subln[:, :], subln_in.partition_broadcast(PARTS)).then_inc(small_loaded, 16)
            a.dma_start(lambdas, lambdas_in.partition_broadcast(PARTS)).then_inc(small_loaded, 16)

            def load_rows(first, n):
                for r in range(n):
                    a.dma_start(rows[:, r * D:(r + 1) * D], rows_in[first + r:first + r + 1, :].partition_broadcast(PARTS)
                                ).then_inc(rows_loaded, 16)

            def sum_squares(k, centred):
                if k >= 1:
                    a.wait_ge(h_ready, k)
                for b in range(TB):
                    bias = negmean[:, b:b + 1] if centred else 0.0
                    ins = a.activation(tmp[:, b * D:(b + 1) * D], h_tok[:, b * D:(b + 1) * D], ACT.Square,
                                       bias=bias, accum_out=sumsq[:, b:b + 1])
                ins.then_inc(sumsq_ready, 1)

            def evacuate_turned(k, gain=None):
                for b in range(4):
                    a.wait_ge(turned, 4 * k + b + 1)
                    if gain is None:
                        ins = a.activation(xT[:, b * HALF:(b + 1) * HALF], bank(b), ACT.Copy)
                    else:
                        for c in (2 * b, 2 * b + 1):
                            ins = a.activation(xT[:, c * SEQ:(c + 1) * SEQ], bank(b, (c % 2) * SEQ, SEQ), ACT.Copy,
                                               scale=params[:, c * NP + gain:c * NP + gain + 1])
                    ins.then_inc(xT_ready, 1)

            a.wait_ge(x_loaded, 16)
            a.wait_ge(pool_ready, 1)
            sum_squares(0, False)
            a.wait_ge(lam_neg, 1)
            a.activation(part(mx + 4200, KC), part(mx + 4200, KC), ACT.Exp, scale=-1.0).then_inc(lam_exp, 1)
            a.wait_ge(lamdot_ready, 1)
            a.activation(lam2, lam2, ACT.Exp).then_inc(lamexp_ready, 1)
            a.wait_ge(angle_ready, 1)
            a.activation(rope[:, :], part(20480, 512), ACT.Sin).then_inc(rope_ready, 1)
            a.wait_ge(small_loaded, 16 * 4)
            evacuate_turned(0, G1)

            def mix_round(c):
                later = not isinstance(c, int)
                a.wait_ge(slot_done[2], c + 1)
                if later:
                    a.wait_ge(cv_done, c)
                a.activation(vb_sb, bank(1, 0, SEQ), ACT.Copy).then_inc(vb_ready, 1)
                a.wait_ge(slot_done[4], c + 1)
                if later:
                    a.wait_ge(ga_used, c)
                a.activation(sq, bank(3, 0, SEQ), ACT.Square).then_inc(sq_ready, 1)
                a.wait_ge(inner_ready, c + 1)
                a.activation(tg, inner, ACT.Tanh, scale=GELU_C).then_inc(tg_ready, 1)
                a.wait_ge(slot_done[6], c + 1)
                if later:
                    a.wait_ge(tm_used, c)
                a.activation(tm, bank(4), ACT.Tanh, scale=0.5).then_inc(tm_ready, 1)
                a.wait_ge(slot_done[7], c + 1)
                a.wait_ge(pst_ready, c + 1)
                if later:
                    a.wait_ge(m_ready, c)
                a.activation(tr, bank(5, 0, SEQ), ACT.Tanh, scale=0.5, bias=pst[:, HBA:HBA + 1])
                a.activation(ti, bank(5, SEQ, SEQ), ACT.Tanh, scale=0.5, bias=pst[:, HBX:HBX + 1]).then_inc(ri_ready, 1)
                a.wait_ge(ri_ready, c + 1)
                a.activation(tt, tr, ACT.Tanh, scale=pst[:, SP4:SP4 + 1], bias=pst[:, SP4:SP4 + 1]).then_inc(tt_ready, 1)
                a.activation(at(arena, c * SEQ + M_A, SEQ), tr, ACT.Exp, scale=pst[:, NSP4:NSP4 + 1],
                             bias=pst[:, NSP4:NSP4 + 1]).then_inc(decay_ready, 1)

            rounds(a, KC, mix_round)
            a.wait_ge(m_ready, KC)
            for c in range(KC):
                m = part(M_M + c * SEQ, SEQ)
                a.activation(m, m, ACT.Sqrt, scale=0.5).then_inc(root_ready, 1)

            sum_squares(1, False)
            evacuate_turned(1, G2)
            for it in range(4):
                for q in range(4):
                    a.wait_ge(slot_done[q], uses_before("query", q) + it + 1)
                    if it >= 1:
                        a.wait_ge(score_done, it)
                    a.activation(qs[:, q * SEQ:(q + 1) * SEQ], bank(4 + q, 0, SEQ), ACT.Copy).then_inc(q_ready, 1)
                a.wait_ge(score_done, it + 1)
                if it >= 2:
                    a.wait_ge(sc_used, it - 1)
                for b in range(TB):
                    ins = a.activation(sc[it % 2][:, b * HALF:(b + 1) * HALF], bank(2 * (it % 2) + b), ACT.Copy)
                ins.then_inc(sc_ready, 1)
            a.wait_ge(shifted_ready, 1)
            a.activation(sel[:, 0:SEQ], sel[:, 0:SEQ], ACT.Exp).then_inc(exp_ready, 1)
            for b in range(2):
                a.wait_ge(sel_turned, b + 1)
                n = (2 - b) * SEQ
                a.activation(chosen[:, b * HALF:b * HALF + n], bank(4 + b, 0, n), ACT.Copy).then_inc(chosen_ready, 1)

            w3 = arena[:, :].rearrange("p (j t) -> p j t", t=SEQ)
            with a.Fori(0, SEQ // 16) as it:
                for g in range(4):
                    dst = w3[:, :, bass.ds(it * 16 + 4 * g, 4)].rearrange("p j t -> p t j")
                    a.wait_ge(scat_done, it * 4 + (g + 1))
                    a.activation(dst, bank(g).rearrange("p (t j) -> p t j", t=4), ACT.Copy).then_inc(w_written, 1)

            def gelu_block(q, it):
                a.wait_ge(slot_done[4 + q], it + (uses_before("expert", 4 + q) + 1))
                if not opening(it):
                    a.wait_ge(slot_done[q], it + uses_before("expert", q))
                a.activation(coef[:, q * SEQ:(q + 1) * SEQ], bank(4 + q, 0, SEQ), ACT.Gelu_apprx_tanh).then_inc(gelu_ready, 1)

            for q in range(4):
                gelu_block(q, 0)
            load_rows(0, 1)
            a.dma_start(wf, fox_f).then_inc(fox_loaded, 16)
            a.dma_start(fbias[0:16, :], forget_bias_in).then_inc(fox_loaded, 16)
            with a.Fori(1, 32) as it:
                for q in range(4):
                    gelu_block(q, it)

            sum_squares(2, False)
            evacuate_turned(2)
            load_rows(1, 2)

            def attention(kind, s):
                slots = phase_slots(f"{kind}_v")
                a.wait_ge(slot_done[slots[-1]], uses_before(f"{kind}_v", slots[-1]) + 1)
                for b in range(4):
                    ins = a.activation(v_tok[:, b * HALF:(b + 1) * HALF], bank(b), ACT.Copy)
                ins.then_inc(s["v_ready"], 1)
                if kind == "fox":
                    a.wait_ge(fz_ready, 1)
                    a.activation(fz_e, fz_e, ACT.Exp, scale=-1.0).then_inc(fexp_ready, 1)

                def qk_out(it, e):
                    a.wait_ge(slot_done[5 + 2 * e], it + (uses_before(f"{kind}_qk", 5 + 2 * e) + 1))
                    if not opening(it):
                        a.wait_ge(s["rope_done" if kind == "diff" else "scores_done"], it * 2 + (e - 1))
                    a.activation(qk[e], bank(4), ACT.Copy).then_inc(s["qk_ready"], 1)

                def pair(it, e, last=False):
                    n1 = it * 2 + (e + 1)
                    a.wait_ge(s["max_ready"], n1)
                    for m in range(4):
                        ins = a.activation(pr[:, m * SEQ:(m + 1) * SEQ], sm[:, m * SEQ:(m + 1) * SEQ], ACT.Exp,
                                           scale=SCALE, bias=nb4[:, m:m + 1], accum_out=l4[:, m:m + 1])
                    ins.then_inc(s["probs_ready"], 1)
                    if not last:
                        qk_out(*following(it, e))
                    a.wait_ge(s["turned"], n1)
                    if kind == "diff":
                        a.activation(pT[:, 0:384], bank(6, 0, 384), ACT.Copy).then_inc(s["turned_ready"], 1)
                        a.wait_ge(s["pv_done"], n1)
                        for b in range(TB):
                            ins = a.activation(squares[:, b * PARTS:(b + 1) * PARTS], bank(7, b * PARTS, PARTS), ACT.Square, accum_out=osq[:, b:b + 1])
                        ins.then_inc(s["osq_ready"], 1)
                    else:
                        for m in range(2):
                            ins = a.activation(pT[:, m * 384:m * 384 + 384], bank(5 + m, 0, 384), ACT.Copy)
                        ins.then_inc(s["turned_ready"], 1)

                qk_out(0, 0)
                all_pairs(a, pair)

            def ffn(l):
                s = ffn_sems[l]
                with a.Fori(0, FF_CHUNKS // 2) as it:
                    for e in range(2):
                        a.wait_ge(s["conv_ready"], it * 2 + (e + 1))
                        a.activation(act[e], conv[e], ACT.Silu).then_inc(s["silu_ready"], 1)

            attention("diff", att_sems[0])
            evacuate_turned(3)
            sum_squares(3, True)
            evacuate_turned(4)
            load_rows(3, 2)
            ffn(0)
            sum_squares(4, True)
            evacuate_turned(5)
            load_rows(5, 2)
            attention("fox", att_sems[1])
            evacuate_turned(6)
            sum_squares(5, True)
            evacuate_turned(7)
            load_rows(7, 2)
            ffn(1)
            sum_squares(6, True)

        @block.tensor
        def _(pe):
            def loaded(phase, s, turn=0):
                pe.wait_ge(slot_loaded[s], turn * 16 + 16 * (uses_before(phase, s) + 1))

            def turn(k, src):
                for b in range(4):
                    for c in (2 * b, 2 * b + 1):
                        for t in range(TB):
                            ins = pe.transpose(bank(b, (c % 2) * SEQ + t * PARTS, PARTS),
                                               src[:, t * D + c * PARTS:t * D + (c + 1) * PARTS], ident)
                    ins.then_inc(turned, 1)

            def project_in(phase, s, dst, it=0):
                loaded(phase, s, it)
                for k in range(KC):
                    ins = pe.matmul(dst, slot(s, k * PARTS, PARTS), xT[:, k * SEQ:(k + 1) * SEQ],
                                    start=(k == 0), stop=(k == KC - 1))
                ins.then_inc(slot_done[s], 1)

            def project_out(phase, s, src, k, first, last, it=0):
                loaded(phase, s, it)
                for t in range(TB):
                    for half in range(2):
                        ins = pe.matmul(bank(2 * t + half), src[:, k * SEQ + t * PARTS:k * SEQ + (t + 1) * PARTS],
                                        slot(s, half * HALF, HALF), start=first, stop=last)
                ins.then_inc(slot_done[s], 1)

            pe.wait_ge(consts_loaded, 16)
            pe.wait_ge(normed, 1)
            turn(0, tmp)
            pe.wait_ge(xT_ready, 4)

            def mix_round(c):
                later = not isinstance(c, int)
                dsts = [(bank(0, 0, SEQ), xc_ready), (bank(1, 0, SEQ), cv_done), (bank(1, SEQ, SEQ), None),
                        (bank(2, 0, SEQ), bb_used), (bank(3, 0, SEQ), ga_used), (bank(4, 0, SEQ), tm_ready),
                        (bank(4, SEQ, SEQ), None)]
                for g, (dst, free) in enumerate(dsts):
                    if later and free is not None:
                        pe.wait_ge(free, c)
                    project_in("mix", g, dst, c)
                pe.wait_ge(xc_ready, c + 1)
                loaded("mix", 7, c)
                if later:
                    pe.wait_ge(ri_ready, c)
                for n in range(2):
                    ins = pe.matmul(bank(5, n * SEQ, SEQ), slot(7, n * PARTS, PARTS), xc, start=True, stop=True)
                ins.then_inc(slot_done[7], 1)

            rounds(pe, KC, mix_round)
            for k in range(KC):
                pe.wait_ge(merged_ready, k + 1)
                project_out("mix_out", k, part(M_OUT, 2048), k, k == 0, k == KC - 1)

            pe.wait_ge(normed, 2)
            turn(1, tmp)
            pe.wait_ge(xT_ready, 8)
            pe.wait_ge(keys_loaded, 16)
            for it in range(4):
                for q in range(4):
                    if it >= 1:
                        pe.wait_ge(q_ready, 4 * (it - 1) + q + 1)
                    project_in("query", q, bank(4 + q, 0, SEQ), it)
                if it >= 2:
                    pe.wait_ge(sc_ready, it - 1)
                for q in range(4):
                    pe.wait_ge(q_ready, 4 * it + q + 1)
                    for t in range(TB):
                        ins = pe.matmul(bank(2 * (it % 2) + t, q * PARTS, PARTS),
                                        qs[:, q * SEQ + t * PARTS:q * SEQ + (t + 1) * PARTS],
                                        keysT[:, (4 * it + q) * PARTS:(4 * it + q + 1) * PARTS], start=True, stop=True)
                ins.then_inc(score_done, 1)
            pe.wait_ge(sel_ready, 1)
            for n in range(3):
                for t in range(TB):
                    ins = pe.transpose(bank(4 + n // 2, (n % 2) * SEQ + t * PARTS, PARTS),
                                       sel[:, n * SEQ + t * PARTS:n * SEQ + (t + 1) * PARTS], ident)
                if n != 0:
                    ins.then_inc(sel_turned, 1)

            def scatter_round(it):
                for g in range(4):
                    pe.wait_ge(one_hots_ready, it * 4 + (g + 1))
                    if not opening(it):
                        pe.wait_ge(w_written, it * 4 + (g - 3))
                    for u in range(4):
                        ins = pe.matmul(bank(g, u * PARTS, PARTS), one_hot[g][:, u * PARTS:(u + 1) * PARTS],
                                        one_hot_w[g][:, u * PARTS:(u + 1) * PARTS], start=True, stop=True)
                    ins.then_inc(scat_done, 1)

            rounds(pe, SEQ // 16, scatter_round)

            def expert_u(q, it):
                if not opening(it):
                    pe.wait_ge(gelu_ready, it * 4 + (q - 3))
                project_in("expert", 4 + q, bank(4 + q, 0, SEQ), it)

            def expert_v(q, it, first=False, last=False):
                pe.wait_ge(coef_ready, it * 4 + (q + 1))
                loaded("expert", q, it)
                for t in range(TB):
                    for half in range(2):
                        ins = pe.matmul(bank(2 * t + half), coef[:, q * SEQ + t * PARTS:q * SEQ + (t + 1) * PARTS],
                                        slot(q, half * HALF, HALF), start=first, stop=last)
                ins.then_inc(slot_done[q], 1)

            for q in range(4):
                expert_u(q, 0)
            pe.wait_ge(w_written, SEQ // 4)
            for q in range(4):
                expert_v(q, 0, first=(q == 0))
                expert_u(q, 1)
            with pe.Fori(1, 31) as it:
                for q in range(4):
                    expert_v(q, it)
                    expert_u(q, it + 1)
            for q in range(4):
                expert_v(q, 31, last=(q == 3))

            pe.wait_ge(normed, 3)
            turn(2, h_tok)

            def attention(kind, s, k_turn):
                pe.wait_ge(xT_ready, 4 * k_turn)
                for k, sl in enumerate(phase_slots(f"{kind}_v")):
                    project_out(f"{kind}_v", sl, xT, k, k == 0, k == KC - 1)
                if kind == "fox":
                    pe.wait_ge(fox_loaded, 32)
                    for k in range(KC):
                        ins = pe.matmul(bank(7, 0, SEQ)[0:16, :], wf[:, 16 * k:16 * k + 16], xT[:, k * SEQ:(k + 1) * SEQ],
                                        start=(k == 0), stop=(k == KC - 1))
                    ins.then_inc(f_done, 1)

                def project(it, e, n):
                    project_in(f"{kind}_qk", 4 + 2 * e + n, bank(4, n * SEQ, SEQ), it)

                def rotate(it, e):
                    pe.wait_ge(s["qk_ready"], it * 2 + (e + 1))
                    pe.matmul(bank(5), perm, qk[e], start=True, stop=True).then_inc(s["rotated"], 1)

                def pair(it, e, last=False):
                    n1 = it * 2 + (e + 1)
                    src = (qkr if kind == "diff" else qk)[e]
                    pe.wait_ge(s["rope_done" if kind == "diff" else "qk_ready"], n1)
                    if not opening(it):
                        pe.wait_ge(s["max_ready"], it * 2 + (e - 1))
                    elif e == 0:
                        pe.wait_ge(s["v_ready"], 1)
                        if kind == "fox":
                            pe.wait_ge(bias_ready, 1)
                    for m in range(2):
                        for t in range(TB):
                            dst = bank(2 * e + m, t * SEQ, SEQ)
                            if kind == "fox":
                                pe.matmul(dst, ones, at(bias_rows, it * 4 * SEQ + (2 * e + m) * SEQ, SEQ),
                                          start=True, stop=False)
                            ins = pe.matmul(dst, src[64 * m:64 * m + 64, t * PARTS:(t + 1) * PARTS],
                                            src[64 * m:64 * m + 64, SEQ:2 * SEQ], start=(kind == "diff"), stop=True)
                    ins.then_inc(s["scores_done"], 1)
                    nxt = following(it, e)
                    if not last:
                        project(*nxt, 0)
                        project(*nxt, 1)
                    if kind == "diff":
                        if not last:
                            rotate(*nxt)
                        pe.wait_ge(s["mixed_ready"], n1)
                        for n, (t, k) in enumerate(((0, 0), (1, 0), (1, 1))):
                            ins = pe.transpose(bank(6, n * PARTS, PARTS), att[:, t * SEQ + k * PARTS:t * SEQ + (k + 1) * PARTS], ident)
                        ins.then_inc(s["turned"], 1)
                    else:
                        pe.wait_ge(s["probs_ready"], n1)
                        for m in range(2):
                            for n, (t, k) in enumerate(((0, 0), (1, 0), (1, 1))):
                                lo = m * HALF + t * SEQ + k * PARTS
                                ins = pe.transpose(bank(5 + m, n * PARTS, PARTS), pr[:, lo:lo + PARTS], ident)
                        ins.then_inc(s["turned"], 1)
                    pe.wait_ge(s["turned_ready"], n1)
                    if not (opening(it) and e == 0):
                        pe.wait_ge(s["o_ready"], it * 2 + e)
                    if kind == "diff":
                        for t, terms in enumerate((((0, 0),), ((1, 0), (2, 1)))):
                            for n, k in terms:
                                ins = pe.matmul(bank(7, t * PARTS, PARTS), pT[:, n * PARTS:(n + 1) * PARTS],
                                                at(v_tok, it * 2 * PARTS + (k * D + e * PARTS), PARTS),
                                                start=(n < 2), stop=(n != 1))
                    else:
                        for m in range(2):
                            for t, terms in enumerate((((0, 0),), ((1, 0), (2, 1)))):
                                for n, k in terms:
                                    ins = pe.matmul(bank(7, (2 * m + t) * 64, 64), pT[:, m * 384 + n * PARTS:m * 384 + (n + 1) * PARTS],
                                                    at(v_tok, it * 4 * 64 + (k * D + (2 * e + m) * 64), 64),
                                                    start=(n < 2), stop=(n != 1))
                    ins.then_inc(s["pv_done"], 1)

                project(0, 0, 0)
                project(0, 0, 1)
                if kind == "diff":
                    rotate(0, 0)
                all_pairs(pe, pair)
                pe.wait_ge(s["o_ready"], 8)
                turn(k_turn, o_tok)
                pe.wait_ge(xT_ready, 4 * k_turn + 4)
                for k in range(KC):
                    project_out(f"{kind}_out", k, xT, k, k == 0, k == KC - 1)

            def ffn(l, k_turn):
                s = ffn_sems[l]
                pe.wait_ge(normed, 4 + 2 * l)
                turn(k_turn, h_tok)
                pe.wait_ge(xT_ready, 4 * k_turn + 4)

                def ahead(it, e):
                    if not opening(it):
                        pe.wait_ge(s["hid_ready"], it * 2 + (e - 1))
                    project_in(f"ffn{l}", 3 * e, bank(4 + 2 * e, 0, SEQ), it)
                    project_in(f"ffn{l}", 3 * e + 1, bank(5 + 2 * e, 0, SEQ), it)

                def chunk(it, e, last=False):
                    if not last:
                        ahead(*following(it, e))
                    pe.wait_ge(s["hid_ready"], it * 2 + (e + 1))
                    project_out(f"ffn{l}", 3 * e + 2, hid[e], 0, opening(it) and e == 0, last, it)

                ahead(0, 0)
                all_pairs(pe, chunk, FF_CHUNKS // 2)

            attention("diff", att_sems[0], 3)
            ffn(0, 4)
            pe.wait_ge(normed, 5)
            turn(5, h_tok)
            attention("fox", att_sems[1], 6)
            ffn(1, 7)

        @block.vector
        def _(v):
            chain = Chain(v, dve_steps)
            link = chain.link

            def log1p_of_exp(dst, e, t):
                z, z2 = t
                link(v.tensor_scalar(z, e, 2.0, None, ALU.add))
                link(v.reciprocal(z, z))
                link(v.tensor_tensor(z, z, e, ALU.mult))
                link(v.tensor_tensor(z2, z, z, ALU.mult))
                link(v.tensor_scalar(dst, z2, 1.0 / 15.0, None, ALU.mult))
                for n in (13, 11, 9, 7, 5, 3):
                    link(v.scalar_tensor_tensor(out=dst, in0=dst, scalar=1.0 / n, in1=z2, op0=ALU.add, op1=ALU.mult))
                link(v.scalar_tensor_tensor(out=dst, in0=dst, scalar=1.0, in1=z, op0=ALU.add, op1=ALU.mult))
                link(v.tensor_scalar(dst, dst, 2.0, None, ALU.mult))

            def variance(k, eps):
                v.wait_ge(sumsq_ready, k + 1)
                v.tensor_scalar(var, sumsq, 1.0 / D, eps, ALU.mult, ALU.add).then_inc(var_ready, 1)
                v.wait_ge(rstd_ready, k + 1)

            def rms(k):
                variance(k, EPS_RMS)
                for b in range(TB):
                    ins = v.tensor_scalar(tmp[:, b * D:(b + 1) * D], h_tok[:, b * D:(b + 1) * D], rstd[:, b:b + 1], None, ALU.mult)
                ins.then_inc(normed, 1)

            def row(n):
                return rows[:, n * D:(n + 1) * D].unsqueeze(1).to_broadcast([PARTS, TB, D])

            h3 = h_tok[:, :].rearrange("p (b d) -> p b d", b=TB)

            def layer_norm(k, phase, s):
                v.wait_ge(slot_done[s], uses_before(phase, s) + dict((n, r) for n, r, _ in RING_PLAN)[phase])
                for n in range(4):
                    h = h_tok[:, n * HALF:(n + 1) * HALF]
                    ins = v.scalar_tensor_tensor(out=h, in0=h, scalar=ALPHA, in1=bank(n), op0=ALU.mult, op1=ALU.add,
                                                 accum_out=sum4[:, n:n + 1])
                link(ins)
                link(v.tensor_tensor(negmean, sum4[:, 0:4:2], sum4[:, 1:4:2], ALU.add))
                v.tensor_scalar(negmean, negmean, -1.0 / D, None, ALU.mult).then_inc(h_ready, 1)
                variance(k, EPS_LN)
                for b in range(TB):
                    h = h_tok[:, b * D:(b + 1) * D]
                    ins = v.tensor_scalar(h, h, negmean[:, b:b + 1], rstd[:, b:b + 1], ALU.add, ALU.mult)
                link(ins)
                v.wait_ge(rows_loaded, 16 + 32 * (k - 2))
                link(v.tensor_tensor(h3, h3, row(0), ALU.mult))
                v.tensor_tensor(h3, h3, row(1), ALU.add).then_inc(normed, 1)

            v.wait_ge(pool_ready, 2)
            v.wait_ge(small_loaded, 16 * 4)
            p3 = params[:, :].rearrange("p (c n) -> p c n", n=NP)
            lam, small = p3[:, :, LAM], [part(mx + 4200 + 8 * n, KC) for n in range(5)]
            link(v.tensor_scalar(small[1], lam, -1.0, None, ALU.mult))
            v.tensor_tensor(small[0], small[1], lam, ALU.max).then_inc(lam_neg, 1)
            l4v = lambdas.rearrange("p (n w d) -> p n w d", n=2, w=2)
            pairs = part(20480, 128).rearrange("p (n d) -> p n d", n=2)
            link(v.tensor_tensor(pairs, l4v[:, :, 0, :], l4v[:, :, 1, :], ALU.mult))
            v.tensor_reduce(lam2, pairs, AX.X, ALU.add).then_inc(lamdot_ready, 1)
            v.wait_ge(lam_exp, 1)
            log1p_of_exp(small[2], small[0], small[3:5])
            link(v.tensor_scalar(small[1], small[1], 0.0, None, ALU.max))
            link(v.tensor_tensor(small[2], small[2], small[1], ALU.add))
            v.tensor_scalar(p3[:, :, SP4], small[2], 4.0, None, ALU.mult)
            v.tensor_scalar(p3[:, :, NSP4], small[2], -4.0, None, ALU.mult)
            v.tensor_scalar(p3[:, :, HBA], p3[:, :, BA], 0.5, None, ALU.mult)
            link(v.tensor_scalar(p3[:, :, HBX], p3[:, :, BX], 0.5, None, ALU.mult))
            v.wait_ge(x_loaded, 16)
            rms(0)
            v.wait_ge(pos_loaded, 16)
            v.wait_ge(consts_loaded, 16)
            v.wait_ge(lamdot_ready, 1)
            ang, turns, flip = part(20736, SEQ), part(20992, SEQ), part(20480, SEQ)
            link(v.tensor_copy(ang, rope[:, 0:SEQ].bitcast(I32)))
            link(v.tensor_scalar(ang, ang, freq, None, ALU.mult))
            link(v.tensor_scalar(turns, ang, 1.0 / (2.0 * math.pi), ROUND, ALU.mult, ALU.add))
            link(v.tensor_scalar(turns, turns, -ROUND, None, ALU.add))
            for c in TWO_PI_PARTS:
                link(v.scalar_tensor_tensor(out=ang, in0=turns, scalar=-c, in1=ang, op0=ALU.mult, op1=ALU.add))
            link(v.tensor_scalar(ang, ang, 3.1415925, -3.1415925, ALU.min, ALU.max))
            link(v.scalar_tensor_tensor(out=flip, in0=ang, scalar=-1.0, in1=ang, op0=ALU.mult, op1=ALU.max))
            v.tensor_scalar(flip, flip, -1.0, math.pi / 2.0, ALU.mult, ALU.add).then_inc(angle_ready, 1)
            v.wait_ge(lamexp_ready, 1)
            link(v.tensor_tensor(nlam, lam2[:, 1:2], lam2[:, 0:1], ALU.subtract))
            link(v.tensor_scalar(nlam, nlam, -LAMBDA_INIT, None, ALU.add))
            link(v.tensor_scalar(subln[:, :], subln[:, :], 1.0 - LAMBDA_INIT, None, ALU.mult))

            def mix_round(c):
                later = not isinstance(c, int)
                if later:
                    v.wait_ge(decay_ready, c)
                v.tensor_copy(pst, at(params, c * NP, NP)).then_inc(pst_ready, 1)
                v.wait_ge(pst_ready, c + 1)
                v.wait_ge(slot_done[0], c + 1)
                if later:
                    v.wait_ge(slot_done[7], c)
                xa = bank(0, 0, SEQ)
                link(v.tensor_scalar(xc, xa, pst[:, CA + 3:CA + 4], pst[:, CAB:CAB + 1], ALU.mult, ALU.add))
                for k in (1, 2, 3):
                    ins = v.scalar_tensor_tensor(out=xc[:, k:], in0=xa[:, :SEQ - k], scalar=pst[:, CA + 3 - k:CA + 4 - k],
                                                 in1=xc[:, k:], op0=ALU.mult, op1=ALU.add)
                    if k < 3:
                        link(ins)
                ins.then_inc(xc_ready, 1)
                v.wait_ge(vb_ready, c + 1)
                v.tensor_tensor(cv, bank(1, SEQ, SEQ), vb_sb, ALU.mult).then_inc(cv_done, 1)
                v.wait_ge(cv_done, c + 1)
                link(v.tensor_scalar(yb, cv, pst[:, CB + 2:CB + 3], None, ALU.mult))
                for k in (1, 2):
                    link(v.scalar_tensor_tensor(out=yb[:, k:], in0=cv[:, :SEQ - k], scalar=pst[:, CB + 2 - k:CB + 3 - k],
                                                in1=yb[:, k:], op0=ALU.mult, op1=ALU.add))
                v.wait_ge(slot_done[3], c + 1)
                v.tensor_tensor(ybb, bank(2, 0, SEQ), yb, ALU.mult).then_inc(bb_used, 1)
                v.wait_ge(sq_ready, c + 1)
                ga = bank(3, 0, SEQ)
                link(v.tensor_scalar(inner, sq, GELU_A, 1.0, ALU.mult, ALU.add))
                v.tensor_tensor(inner, ga, inner, ALU.mult).then_inc(inner_ready, 1)
                v.wait_ge(tg_ready, c + 1)
                v.scalar_tensor_tensor(out=gg, in0=tg, scalar=1.0, in1=ga, op0=ALU.add, op1=ALU.mult).then_inc(ga_used, 1)
                v.wait_ge(ga_used, c + 1)
                v.wait_ge(bb_used, c + 1)
                v.wait_ge(tm_ready, c + 1)
                v.scalar_tensor_tensor(out=at(arena, c * SEQ + M_G1, SEQ), in0=tm[:, 0:SEQ], scalar=1.0, in1=gg,
                                       op0=ALU.add, op1=ALU.mult)
                v.scalar_tensor_tensor(out=at(arena, c * SEQ + M_G2, SEQ), in0=tm[:, SEQ:], scalar=1.0, in1=ybb,
                                       op0=ALU.add, op1=ALU.mult).then_inc(tm_used, 1)
                v.wait_ge(ri_ready, c + 1)
                v.scalar_tensor_tensor(out=at(arena, c * SEQ + M_IX, SEQ), in0=ti, scalar=1.0, in1=xc,
                                       op0=ALU.add, op1=ALU.mult)
                v.wait_ge(tt_ready, c + 1)
                link(v.tensor_scalar(t1, tt, 1.0, None, ALU.add))
                link(v.reciprocal(rc, t1))
                v.tensor_tensor(at(arena, c * SEQ + M_M, SEQ), tt, rc, ALU.mult).then_inc(m_ready, 1)

            MIX_STEPS = 1 + 2 + 3 + 1 + 2
            chain.enter(0, MIX_STEPS)
            mix_round(0)
            chain.leave(1)
            with v.Fori(1, KC) as it:
                chain.enter(it, MIX_STEPS, 1)
                mix_round(it)
            chain.leave(KC - 1)
            v.wait_ge(m_ready, KC)
            for c in range(KC):
                v.wait_ge(root_ready, c + 1)
                u, m = part(M_IX + c * SEQ, SEQ), part(M_M + c * SEQ, SEQ)
                g1, g2 = part(M_G1 + c * SEQ, SEQ), part(M_G2 + c * SEQ, SEQ)
                link(v.tensor_tensor(u, u, m, ALU.mult))
                if c == 0:
                    v.wait_ge(decay_ready, KC)
                link(v.tensor_tensor_scan(m, part(M_A + c * SEQ, SEQ), u, 0.0, ALU.mult, ALU.add))
                link(v.tensor_tensor(g1, g1, m, ALU.mult))
                v.scalar_tensor_tensor(out=part(M_OUT + c * SEQ, SEQ), in0=g1, scalar=0.5, in1=g2, op0=ALU.mult, op1=ALU.add
                                       ).then_inc(merged_ready, 1)
            v.wait_ge(slot_done[7], uses_before("mix_out", 7) + 1)
            for n in range(4):
                h = h_tok[:, n * HALF:(n + 1) * HALF]
                ins = v.scalar_tensor_tensor(out=h, in0=bank(n), scalar=0.5, in1=h, op0=ALU.mult, op1=ALU.add)
            ins.then_inc(h_ready, 1)
            rms(1)

            top4 = top1.rearrange("p (b q k) -> p b q k", b=TB, q=4)
            idx4 = idxf.rearrange("p (b q k) -> p b q k", b=TB, q=4)
            for it in range(4):
                v.wait_ge(sc_ready, it + 1)
                tiles = [(b, q) for b in range(TB) for q in range(4)]

                def scores(b, q):
                    return sc[it % 2][:, b * HALF + q * PARTS:b * HALF + (q + 1) * PARTS]

                def places(t, b, q, n):
                    return t[:, (b * 4 + q) * 16 + 8 * n:(b * 4 + q) * 16 + 8 * n + 8]

                for b, q in tiles:
                    ins = v.max(places(top1, b, q, 0), scores(b, q))
                link(ins)
                for b, q in tiles:
                    v.max_index(places(idxu, b, q, 0), places(top1, b, q, 0), scores(b, q))
                    ins = v.match_replace(rest[:, (b * 4 + q) * PARTS:(b * 4 + q + 1) * PARTS], places(top1, b, q, 0),
                                          scores(b, q), -3e38)
                ins.then_inc(sc_used, 1)
                v.wait_ge(sc_used, it + 1)
                for b, q in tiles:
                    ins = v.max(places(top1, b, q, 1), rest[:, (b * 4 + q) * PARTS:(b * 4 + q + 1) * PARTS])
                link(ins)
                for b, q in tiles:
                    ins = v.max_index(places(idxu, b, q, 1), places(top1, b, q, 1),
                                      rest[:, (b * 4 + q) * PARTS:(b * 4 + q + 1) * PARTS])
                chain.step(ins)
                c4 = cand.rearrange("p (m a b) -> p m a b", m=4, a=16)
                t4 = top1.rearrange("p (m h k) -> p m h k", m=4, h=2)
                v.tensor_tensor(c4, t4[:, :, 0, :].unsqueeze(3).to_broadcast([PARTS, 4, 16, 16]),
                                t4[:, :, 1, :].unsqueeze(2).to_broadcast([PARTS, 4, 16, 16]), ALU.add)
                chain.wait()
                link(v.tensor_copy(idxf, idxu))

                def cd(t, m):
                    return t[:, m * 256:(m + 1) * 256]

                def bp(t, m, n):
                    return t[:, m * 16 + 8 * n:m * 16 + 8 * n + 8]

                for m in range(4):
                    ins = v.max(bp(best, m, 0), cd(cand, m))
                link(ins)
                for m in range(4):
                    v.max_index(bp(posu, m, 0), bp(best, m, 0), cd(cand, m))
                    ins = v.match_replace(cd(cand2, m), bp(best, m, 0), cd(cand, m), -3e38)
                link(ins)
                for m in range(4):
                    ins = v.max(bp(best, m, 1), cd(cand2, m))
                link(ins)
                for m in range(4):
                    ins = v.max_index(bp(posu, m, 1), bp(best, m, 1), cd(cand2, m))
                link(ins)
                b3 = best.rearrange("p (m k) -> p m k", m=4)
                heads = slice(32 * it, 32 * it + 32)
                sel3 = sel.rearrange("p (n b k) -> p n b k", n=3, b=TB)

                def chosen_of(n):
                    return sel3[:, n, :, heads].rearrange("p b (h k) -> p b h k", h=2)

                b4 = best.rearrange("p (b h k) -> p b h k", b=TB, h=2)
                for b in range(TB):
                    ins = v.tensor_tensor(chosen_of(0)[:, b], b4[:, b], b4[:, b, :, 0:1].to_broadcast([PARTS, 2, 16]), ALU.subtract)
                if it == 3:
                    ins.then_inc(shifted_ready, 1)
                for n, (by, op) in enumerate(((4, ALU.logical_shift_right), (15, ALU.bitwise_and))):
                    link(v.tensor_single_scalar(digit, posu, by, op))
                    link(v.tensor_copy(digitf, digit))
                    e4 = eqs.rearrange("p (m k a) -> p m k a", m=4, k=16)
                    d3 = digitf.rearrange("p (m k) -> p m k", m=4)
                    i4 = idxf.rearrange("p (m h a) -> p m h a", m=4, h=2)
                    link(v.tensor_tensor(e4, d3.unsqueeze(3).to_broadcast([PARTS, 4, 16, 16]),
                                         iota[:, 0:16].unsqueeze(1).unsqueeze(1).to_broadcast([PARTS, 4, 16, 16]), ALU.is_equal))
                    link(v.tensor_tensor(e4, e4, i4[:, :, n, :].unsqueeze(2).to_broadcast([PARTS, 4, 16, 16]), ALU.mult))
                    for b in range(TB):
                        ins = v.tensor_reduce(chosen_of(1 + n)[:, b], e4[:, 2 * b:2 * b + 2], AX.X, ALU.add)
                    chain.step(ins)
            v.wait_ge(exp_ready, 1)
            w3 = sel[:, 0:SEQ].rearrange("p (g k) -> p g k", k=16)
            s16 = expsum[:, 0:16]
            link(v.tensor_reduce(s16, w3, AX.X, ALU.add))
            link(v.reciprocal(s16, s16))
            chain.wait()
            v.tensor_tensor(w3, w3, s16.unsqueeze(2).to_broadcast([PARTS, 16, 16]), ALU.mult).then_inc(sel_ready, 1)

            v.wait_ge(chosen_ready, 2)
            weight, sel_i, sel_j = (chosen[:, n * SEQ:(n + 1) * SEQ] for n in range(3))
            iota4 = iota.unsqueeze(1).to_broadcast([PARTS, 4, PARTS])

            def one_hot_round(it):
                for g in range(4):
                    if not opening(it):
                        v.wait_ge(scat_done, it * 4 + (g - 3))
                    v.tensor_tensor(one_hot[g].rearrange("p (t i) -> p t i", t=4),
                                    at(sel_i, it * 16 + 4 * g, 4).unsqueeze(2).to_broadcast([PARTS, 4, PARTS]),
                                    iota4, ALU.is_equal)
                    for u in range(4):
                        ins = v.tensor_scalar(one_hot_w[g][:, u * PARTS:(u + 1) * PARTS], iota,
                                              at(sel_j, it * 16 + (4 * g + u), 1), at(weight, it * 16 + (4 * g + u), 1),
                                              ALU.is_equal, ALU.mult)
                    ins.then_inc(one_hots_ready, 1)

            rounds(v, SEQ // 16, one_hot_round)

            v.wait_ge(w_written, SEQ // 4)
            with v.Fori(0, 32) as it:
                for q in range(4):
                    c = coef[:, q * SEQ:(q + 1) * SEQ]
                    v.wait_ge(gelu_ready, it * 4 + (q + 1))
                    v.tensor_tensor(c, c, at(arena, it * 4 * SEQ + q * SEQ, SEQ), ALU.mult).then_inc(coef_ready, 1)
            v.wait_ge(slot_done[3], uses_before("expert", 3) + 32)
            for n in range(4):
                h = h_tok[:, n * HALF:(n + 1) * HALF]
                ins = v.tensor_tensor(h, h, bank(n), ALU.add)
            ins.then_inc(h_ready, 1)
            variance(2, EPS_RMS)
            v.wait_ge(rows_loaded, 16)
            for b in range(TB):
                h = h_tok[:, b * D:(b + 1) * D]
                ins = v.scalar_tensor_tensor(out=h, in0=h, scalar=rstd[:, b:b + 1], in1=rows[:, 0:D], op0=ALU.mult, op1=ALU.mult)
            ins.then_inc(normed, 1)

            rope2 = [rope[:, n * SEQ:(n + 1) * SEQ].unsqueeze(1).to_broadcast([PARTS, 2, SEQ]) for n in range(2)]

            def attention(kind, s):
                if kind == "fox":
                    fz, t2, c16 = (part(14592 + 256 * n, SEQ)[0:16, :] for n in range(3))
                    t3 = part(15360, SEQ)[0:16, :]
                    v.wait_ge(f_done, 1)
                    v.wait_ge(fox_loaded, 32)
                    link(v.tensor_scalar(fz, bank(7, 0, SEQ)[0:16, :], fbias[0:16, :], None, ALU.add))
                    v.scalar_tensor_tensor(out=fz_e, in0=fz, scalar=-1.0, in1=fz, op0=ALU.mult, op1=ALU.max).then_inc(fz_ready, 1)
                    v.wait_ge(fexp_ready, 1)
                    log1p_of_exp(c16, fz_e, (t2, t3))
                    link(v.tensor_scalar(fz, fz, 0.0, None, ALU.min))
                    link(v.tensor_tensor(fz, fz, c16, ALU.subtract))
                    link(v.tensor_tensor_scan(c16, ones256[0:16, :], fz, 0.0, ALU.mult, ALU.add))
                    link(v.tensor_scalar(c16, c16, -1.0 / SCALE, None, ALU.mult))
                    link(v.memset(bias_rows, 0.0))
                    b3 = bias_rows[0:16, :].rearrange("p (h t) -> p h t", h=16)
                    v.tensor_tensor(b3, c16.unsqueeze(1).to_broadcast([16, 16, SEQ]),
                                    head_sel[0:16, :].unsqueeze(2).to_broadcast([16, 16, SEQ]), ALU.mult).then_inc(bias_ready, 1)

                def rotary(it, e):
                    v.wait_ge(s["rotated"], it * 2 + (e + 1))
                    if not opening(it):
                        v.wait_ge(s["scores_done"], it * 2 + (e - 1))
                    three = lambda t: t.rearrange("p (n t) -> p n t", n=2)
                    v.tensor_tensor(three(rot), three(bank(5)), rope2[1], ALU.mult)
                    link(v.tensor_tensor(three(qkr[e]), three(qk[e]), rope2[0], ALU.mult))
                    v.tensor_tensor(qkr[e], qkr[e], rot, ALU.add).then_inc(s["rope_done"], 1)

                def pair(it, e, last=False):
                    n1 = it * 2 + (e + 1)
                    v.wait_ge(s["scores_done"], n1)
                    for m in range(2):
                        ins = v.tensor_tensor(sm[:, m * HALF:(m + 1) * HALF], bank(2 * e + m), mask, ALU.add)
                    link(ins)
                    link(v.tensor_reduce(mx4, sm.rearrange("p (m k) -> p m k", m=4), AX.X, ALU.max))
                    v.tensor_scalar(nb4, mx4, -SCALE, None, ALU.mult).then_inc(s["max_ready"], 1)
                    if kind == "diff":
                        v.wait_ge(s["probs_ready"], n1)
                        link(v.reciprocal(rl4, l4))
                        v.tensor_scalar(rl2, rl4[:, 2:4], nlam, None, ALU.mult)
                        for t in range(TB):
                            ins = v.tensor_scalar(att[:, t * SEQ:(t + 1) * SEQ], pr[:, t * SEQ:(t + 1) * SEQ],
                                                  rl4[:, t:t + 1], None, ALU.mult)
                        link(ins)
                        for t in range(TB):
                            a_t = att[:, t * SEQ:(t + 1) * SEQ]
                            ins = v.scalar_tensor_tensor(out=a_t, in0=pr[:, HALF + t * SEQ:HALF + (t + 1) * SEQ],
                                                         scalar=rl2[:, t:t + 1], in1=a_t, op0=ALU.mult, op1=ALU.add)
                        ins.then_inc(s["mixed_ready"], 1)
                        if not last:
                            rotary(*following(it, e))
                        v.wait_ge(s["osq_ready"], n1)
                        v.tensor_scalar(ovar, osq, 1.0 / PARTS, EPS_RMS, ALU.mult, ALU.add).then_inc(s["ovar_ready"], 1)
                        v.wait_ge(s["orstd_ready"], n1)
                        for t in range(TB):
                            ins = v.scalar_tensor_tensor(out=at(o_tok, it * 2 * PARTS + (t * D + e * PARTS), PARTS),
                                                         in0=bank(7, t * PARTS, PARTS), scalar=orstd[:, t:t + 1],
                                                         in1=subln[:, :], op0=ALU.mult, op1=ALU.mult)
                        ins.then_inc(s["o_ready"], 1)
                    else:
                        v.wait_ge(s["probs_ready"], n1)
                        link(v.reciprocal(rl4, l4))
                        v.wait_ge(s["pv_done"], n1)
                        for m in range(2):
                            for t in range(TB):
                                ins = v.tensor_scalar(at(o_tok, it * 4 * 64 + (t * D + (2 * e + m) * 64), 64),
                                                      bank(7, (2 * m + t) * 64, 64), rl4[:, 2 * m + t:2 * m + t + 1], None, ALU.mult)
                        ins.then_inc(s["o_ready"], 1)

                steps = 2 * (5 if kind == "diff" else 3)
                if kind == "diff":
                    v.wait_ge(rope_ready, 1)
                    rotary(0, 0)
                all_pairs(v, pair, chain=chain, steps=steps, last_steps=steps - (1 if kind == "diff" else 0))

            def ffn(l):
                s = ffn_sems[l]

                def chunk(it, e, last=False):
                    gate = bank(4 + 2 * e, 0, SEQ)
                    p = fpst[e]
                    link(v.tensor_copy(p, at(ffn_params, it * 8 + (l * FF_CHUNKS + e) * 4, 4)))
                    v.wait_ge(slot_done[3 * e], it + (uses_before(f"ffn{l}", 3 * e) + 1))
                    link(v.tensor_scalar(conv[e], gate, p[:, 2:3], p[:, 3:4], ALU.mult, ALU.add))
                    for k in (1, 2):
                        ins = v.scalar_tensor_tensor(out=conv[e][:, k:], in0=gate[:, :SEQ - k], scalar=p[:, 2 - k:3 - k],
                                                     in1=conv[e][:, k:], op0=ALU.mult, op1=ALU.add)
                        if k == 1:
                            link(ins)
                    ins.then_inc(s["conv_ready"], 1)
                    v.wait_ge(s["silu_ready"], it * 2 + (e + 1))
                    v.wait_ge(slot_done[3 * e + 1], it + (uses_before(f"ffn{l}", 3 * e + 1) + 1))
                    if not opening(it):
                        v.wait_ge(slot_done[3 * e + 2], it + uses_before(f"ffn{l}", 3 * e + 2))
                    v.tensor_tensor(hid[e], act[e], bank(5 + 2 * e, 0, SEQ), ALU.mult).then_inc(s["hid_ready"], 1)

                all_pairs(v, chunk, FF_CHUNKS // 2, chain=chain, steps=6, last_steps=6)

            attention("diff", att_sems[0])
            layer_norm(3, "diff_out", 7)
            ffn(0)
            layer_norm(4, "ffn0", 5)
            attention("fox", att_sems[1])
            layer_norm(5, "fox_out", 7)
            ffn(1)
            layer_norm(6, "ffn1", 5)


def _in_pieces(w):
    n = w.shape[1] // PARTS
    return w.reshape(KC, PARTS, n, PARTS).transpose(2, 1, 0, 3).reshape(n, PARTS, D)


def _by_feature(v):
    v = v.reshape(-1, v.shape[-1] // PARTS, PARTS)
    return v.transpose(2, 1, 0)


def _constants():
    c = np.zeros((PARTS, NCONST), np.float32)
    c[:, IDENT:IDENT + PARTS] = np.eye(PARTS)
    for m in range(PARTS):
        d = m % 64
        if d < 8:
            c[m + 8, PERM + m] = -1.0
        elif d < 16:
            c[m - 8, PERM + m] = 1.0
    c[:, IOTA:IOTA + PARTS] = np.arange(PARTS)
    q, k = np.arange(PARTS)[:, None], np.arange(SEQ)[None]
    c[:, MASK:MASK + SEQ] = np.where(k <= q, 0.0, MASKED)
    c[:, MASK + SEQ:MASK + 2 * SEQ] = np.where(k <= q + PARTS, 0.0, MASKED)
    inv = np.float32(500000.0) ** (-np.arange(0, 16, 2, dtype=np.float32) / np.float32(16))
    d = np.arange(PARTS) % 64
    c[:, FREQ] = np.where(d < 16, inv[d % 8], 0.0)
    c[:16, HSEL:HSEL + 16] = np.eye(16)
    return c


def kernel(**inputs):
    import concourse.bacc as bacc
    from concourse.bass_utils import run_bass_kernel_spmd

    g = {k: np.asarray(v) for k, v in inputs.items()}
    f = np.ascontiguousarray
    w_in = g["w_in"][0].reshape(KC, PARTS, 7, KC, PARTS).transpose(2, 3, 1, 0, 4).reshape(7, KC, PARTS, D)
    w_in = w_in[[0, 2, 4, 3, 1, 5, 6]]
    params = np.zeros((PARTS, KC, NP), np.float32)
    for lo, name in ((G1, "norm1_g"), (CA, "conv_a_w"), (CAB, "conv_a_b"), (BA, "b_a"), (BX, "b_x"),
                     (LAM, "lru_lambda"), (CB, "conv_b_w"), (G2, "norm2_g")):
        v = _by_feature(g[name][0])
        params[:, :, lo:lo + v.shape[2]] = v
    ffn_params = np.stack([_by_feature(np.concatenate([g["ffn_conv_w_2"][l], g["ffn_conv_b_2"][l][None]]))
                           for l in range(2)], 1)
    diff, fox = g["diff_w_qkv_2"][0], g["fox_w_in_2"][0]

    def qk_pieces(w):
        p = _in_pieces(w[:, :2 * D])
        return p.reshape(2, 8, PARTS, D).transpose(1, 0, 2, 3).reshape(16, PARTS, D)

    ffn_in = []
    for l in range(2):
        p = _in_pieces(g["ffn_w_in_2"][l])
        ffn_in.append(p.reshape(2, FF_CHUNKS, PARTS, D).transpose(1, 0, 2, 3).reshape(2 * FF_CHUNKS, PARTS, D))
    arrays = {
        "x": g["x"][0].reshape(TB, PARTS, D).transpose(1, 0, 2),
        "w_mix": w_in,
        "w_gate": np.concatenate([g["w_a"][0], g["w_x"][0]], axis=2),
        "w_out": g["w_out"][0].reshape(KC, PARTS, D),
        "w_query": _in_pieces(g["peer_wq"][0]),
        "keys": g["peer_subkeys"][0].transpose(3, 0, 1, 2).reshape(PARTS, 16 * PARTS),
        "u_tab": g["peer_u"][0].reshape(PARTS, PARTS, KC, PARTS).transpose(1, 3, 2, 0).reshape(PARTS, PARTS, D),
        "v_tab": g["peer_v"][0].reshape(PARTS, PARTS, D).transpose(1, 0, 2),
        "diff_qk": qk_pieces(diff),
        "diff_v": diff[:, 2 * D:].reshape(KC, PARTS, D),
        "diff_out": g["diff_w_o_2"][0].reshape(KC, PARTS, D),
        "fox_qk": qk_pieces(fox),
        "fox_v": fox[:, 2 * D:3 * D].reshape(KC, PARTS, D),
        "fox_f": fox[:, 3 * D:].reshape(KC, PARTS, 16).transpose(1, 0, 2).reshape(PARTS, KC * 16),
        "fox_out": g["fox_w_o_2"][0].reshape(KC, PARTS, D),
        "ffn_in": np.stack(ffn_in),
        "ffn_out": g["ffn_w_out_2"].reshape(2, FF_CHUNKS, PARTS, D),
        "consts": _constants(),
        "params": params.reshape(PARTS, KC * NP),
        "ffn_params": ffn_params.reshape(PARTS, 2 * FF_CHUNKS * 4),
        "rows": np.stack([g["final_g"]] + [g[f"{n}_2"][l] for l in range(2) for n in ("ln1_g", "ln1_b", "ln2_g", "ln2_b")]),
        "subln": g["diff_subln_g_2"],
        "lambdas": np.stack([g[f"diff_lambda_{n}_2"][0] for n in ("q1", "k1", "q2", "k2")]).reshape(1, 256),
        "forget_bias": g["fox_b_f_2"].reshape(16, 1),
        "positions": g["positions_2"].astype(np.int32),
    }
    nc = bacc.Bacc("TRN2", target_bir_lowering=False, num_devices=1)
    arrays = {f"in_{k}": f(v) for k, v in arrays.items()}
    args = [nc.dram_tensor(k, v.shape, mybir.dt.from_np(v.dtype), kind="ExternalInput").ap() for k, v in arrays.items()]
    out = nc.dram_tensor("out", (PARTS, TB, D), F32, kind="ExternalOutput").ap()
    build(nc, *args, out)
    r = run_bass_kernel_spmd(nc, [arrays], core_ids=[0])
    got = r.results[0]["out"]
    return np.ascontiguousarray(got.transpose(1, 0, 2).reshape(1, SEQ, D))
```

```python
import math
from contextlib import ExitStack

import numpy as np

import concourse.bass as bass
from concourse import mybir

F32 = mybir.dt.float32
F32R = mybir.dt.float32r
I32 = mybir.dt.int32
U32 = mybir.dt.uint32
ALU = mybir.AluOpType
ACT = mybir.ActivationFunctionType
AX = mybir.AxisListType

SEQ, D = 256, 1024
PARTS = 128
TB = SEQ // PARTS
KC = D // PARTS
HALF = 512
EPS_RMS, EPS_LN = 1e-6, 1e-5
MIX_GROUPS = 7
HEADS, NKEYS, TOPK = 8, 128, 16
D_FF = 2816
FF_CHUNKS = D_FF // PARTS
ALPHA = 4 ** 0.25
LAMBDA_INIT = 0.8 - 0.6 * math.exp(0.0)
SCALE = 64 ** -0.5
MASKED = -1e30
GELU_C, GELU_A = math.sqrt(2.0 / math.pi), 0.044715
TWO_PI_PARTS = (6.28125, 0.0019350051879882812, 3.019916050561733e-07)
ROUND = 1.5 * 2.0 ** 23
G1, CA, CAB, BA, BX, LAM, CB, G2, SP4, NSP4, HBA, HBX = 0, 1, 5, 6, 7, 8, 9, 12, 13, 14, 15, 16
NP = 17
IDENT, PERM, IOTA, FREQ, HSEL = 0, 128, 256, 384, 385
NCONST = 401
ARENA = 32768


class Chain:

    def __init__(self, eng, sem):
        self.eng, self.sem, self.base, self.n = eng, sem, 0, 0
        self.it, self.per = None, 0

    def enter(self, it, per, rounds_before=0):
        self.it, self.per = it, per
        self.start, self.first = self.base + self.n, rounds_before
        self.base, self.n = self.start, 0

    def leave(self, rounds):
        assert self.n == self.per, (self.n, self.per)
        self.base, self.n, self.it = self.start + rounds * self.per, 0, None

    def step(self, ins):
        ins.then_inc(self.sem, 1)
        self.n += 1
        return ins

    def wait(self):
        if self.it is None:
            self.eng.wait_ge(self.sem, self.base + self.n)
        else:
            self.eng.wait_ge(self.sem, (self.it - self.first) * self.per + (self.base + self.n))

    def link(self, ins):
        self.step(ins)
        self.wait()


STREAM = [("mix", 8 * KC), ("mix_out", KC), ("query", 16), ("expert", 256),
          ("diff_v", KC), ("diff_qk", 16), ("diff_out", KC), ("ffn0", 3 * FF_CHUNKS),
          ("fox_v", KC), ("fox_f", 1), ("fox_qk", 16), ("fox_out", KC), ("ffn1", 3 * FF_CHUNKS)]
TOTAL = sum(n for _, n in STREAM)
RING = 4


def start_of(phase):
    count = 0
    for name, n in STREAM:
        if name == phase:
            return count
        count += n
    raise KeyError(phase)


class Piece:

    def __init__(self, phase, k, it=0, per=0):
        assert per % RING == 0 or isinstance(it, int)
        self.n = (start_of(phase) if phase else 0) + k
        self.it, self.per = it, per
        if isinstance(it, int):
            self.n, self.it, self.per = self.n + it * per, 0, 0

    @property
    def slot(self):
        return self.n % RING

    @property
    def before(self):
        return self.n // RING if isinstance(self.it, int) else self.it * (self.per // RING) + self.n // RING

    @property
    def count(self):
        return self.n // RING + 1 if isinstance(self.it, int) else self.it * (self.per // RING) + (self.n // RING + 1)

    @property
    def loads(self):
        return 16 * self.count if isinstance(self.it, int) else self.it * (16 * self.per // RING) + 16 * (self.n // RING + 1)

    def later(self, k):
        p = Piece(None, 0)
        p.n, p.it, p.per = self.n + k, self.it, self.per
        return p


def piece_u(j, it=0):
    return Piece("expert", j if j < 3 else 2 * j - 2, it, 8)


def piece_v(j, it=0):
    return Piece("expert", 2 * j + 3 if j < NKEYS - 2 else j + NKEYS, it, 8)


def piece_gate(l, n, it=0):
    return Piece(f"ffn{l}", 3 * n - 1 if n else 0, it, 12)


def piece_up(l, n, it=0):
    return Piece(f"ffn{l}", 3 * n if n else 1, it, 12)


def piece_out(l, n, it=0):
    return Piece(f"ffn{l}", 3 * n + 4 if n < FF_CHUNKS - 1 else 3 * n + 2, it, 12)


def build(nc, x, w_mix, w_gate, w_out, w_query, keys, u_tab, v_tab, diff_qk, diff_v, diff_out,
          fox_qk, fox_v, fox_f, fox_out, mask_in, ffn_in, ffn_out, consts_in, params_in, ffn_params_in,
          rows_in, subln_in, lambdas_in, forget_bias_in, positions_in, h_saved, out):
    ctx = ExitStack()
    with ctx:
        def sb(name, shape, dt=F32):
            return ctx.enter_context(nc.sbuf_tensor(name, shape, dt))

        def sem(name):
            return ctx.enter_context(nc.semaphore(name))

        raw = sb("raw", [PARTS, RING * D])
        high = sb("high", [PARTS, RING * D], F32R)
        low = sb("low", [PARTS, RING * D], F32R)
        h_tok = sb("h_tok", [PARTS, TB * D])
        xh = sb("xh", [PARTS, KC * SEQ], F32R)
        xl = sb("xl", [PARTS, KC * SEQ], F32R)
        yh = sb("yh", [PARTS, 2 * SEQ], F32R)
        yl = sb("yl", [PARTS, 2 * SEQ], F32R)
        consts = sb("consts", [PARTS, NCONST])
        params = sb("params", [PARTS, KC * NP])
        ffn_params = sb("ffn_params", [PARTS, 2 * FF_CHUNKS * 4])
        subln = sb("subln", [PARTS, PARTS])
        stats = sb("stats", [PARTS, 64])
        arena = sb("arena", [PARTS, ARENA])
        ps = ctx.enter_context(nc.psum_tensor("ps", [PARTS, 8 * HALF], F32))

        def bank(b, lo=0, n=HALF):
            return ps[:, b * HALF + lo:b * HALF + lo + n]

        def cols(t, p, lo=0, n=D):
            return t[:, p.slot * D + lo:p.slot * D + lo + n]

        def part(lo, n):
            return arena[:, lo:lo + n]

        def at(t, start, n):
            return t[:, bass.ds(start, n)]

        def chunk_of(t, k):
            return t[:, k * SEQ:(k + 1) * SEQ]

        ident = consts[:, IDENT:IDENT + PARTS]
        perm = consts[:, PERM:PERM + PARTS]
        iota = consts[:, IOTA:IOTA + PARTS]
        freq = consts[:, FREQ:FREQ + 1]
        head_sel = consts[:, HSEL:HSEL + 16]

        one_hot = [h_tok[:, 512 * n:512 * n + 512] for n in range(2)]
        one_hot_w = [h_tok[:, 1024 + 512 * n:1536 + 512 * n] for n in range(2)]
        coef = [h_tok[:, SEQ * n:SEQ * n + SEQ] for n in range(2)]
        chosen = raw[:, (RING - 1) * D:(RING - 1) * D + 3 * SEQ]
        tmp = part(18944, TB * D)
        rows = part(20992, 2 * D)
        mask = part(23040, 512)
        ones256 = part(23552, SEQ)
        ones = part(23552, PARTS)
        rope = part(23808, 2 * SEQ)
        h_back = part(24320, TB * D)
        angles = part(26368, 2 * SEQ)
        turns = part(26880, SEQ)
        lambdas = part(27136, 4 * 64)
        lam_prod = part(27392, 128)
        M_G1, M_G2, M_A, M_IX, M_M = (2048 * n for n in range(5))
        mx = 10240
        xc = part(mx, 256)
        vb_sb, cv, yb, ybb, sq, inner, tg, gg = (part(mx + 256 * n, 256) for n in range(1, 9))
        tm = part(mx + 2304, 512)
        tr, ti, tt, t1, rc = (part(mx + 2816 + 256 * n, 256) for n in range(5))
        pst = part(mx + 4096, NP)
        small = [part(mx + 4200 + 8 * n, KC) for n in range(5)]
        merged = [part(mx + 4352 + 256 * n, 256) for n in range(2)]
        keysT = part(15360, 16 * PARTS)
        qs = part(0, 4 * SEQ)
        sc = [part(1024 + 1024 * n, 1024) for n in range(2)]
        rest = part(3072, 1024)
        cand, cand2 = part(4096, 1024), part(5120, 1024)
        eqs = part(6144, 1024)
        top1, idxf = part(7168, 128), part(7296, 128)
        idxu = part(7424, 128).bitcast(U32)
        posu = part(7552, 64).bitcast(U32)
        digit = part(7616, 64).bitcast(U32)
        digitf = part(7680, 64)
        best = part(7744, 64)
        sel = part(7808, 3 * SEQ)
        expsum = part(8576, 32)
        v_tok = part(0, TB * D)
        bias_rows = part(2048, 16 * SEQ)
        o_tok = part(6144, TB * D)
        qk = [part(8192 + 512 * n, 512) for n in range(2)]
        qkr = [part(9216 + 512 * n, 512) for n in range(2)]
        rot = part(10240, 512)
        sm = part(10752, 1024)
        pr = part(11776, 1024)
        pT = part(12800, 768)
        att = part(13568, 512)
        squares = part(14080, 2 * PARTS)
        fz_e = part(14336, SEQ)[0:16, :]
        conv = [part(0 + 256 * n, 256) for n in range(2)]
        act = [part(512 + 256 * n, 256) for n in range(2)]
        hid = [part(1024 + 256 * n, 256) for n in range(2)]
        fpst = [part(1536 + 4 * n, 4) for n in range(2)]
        fbias = stats[:, 44:45]
        halfpow = stats[:, 0:2]
        sumsq, var, rstd, negmean = (stats[:, 2 + 2 * n:4 + 2 * n] for n in range(4))
        sum4 = stats[:, 10:14]
        mx4, nb4, l4, rl4 = (stats[:, 14 + 4 * n:18 + 4 * n] for n in range(4))
        nlam = stats[:, 30:31]
        rl2 = stats[:, 32:34]
        lam2 = stats[:, 34:36]
        osq, ovar, orstd = (stats[:, 36 + 2 * n:38 + 2 * n] for n in range(3))
        halfpow2 = stats[:, 42:44]

        slot_loaded, slot_high, slot_low, slot_done = (
            [sem(f"slot_{what}{s}") for s in range(RING)] for what in ("loaded", "high", "low", "done"))
        x_loaded, consts_loaded, small_loaded = sem("x_loaded"), sem("consts_loaded"), sem("small_loaded")
        keys_loaded, rows_loaded, pos_loaded = sem("keys_loaded"), sem("rows_loaded"), sem("pos_loaded")
        stored, bias_loaded, mask_loaded = sem("stored"), sem("bias_loaded"), sem("mask_loaded")
        h_kept, h_back_loaded = sem("h_kept"), sem("h_back_loaded")
        turned_high, xc_high, merged_high, coef_high = (
            sem(n) for n in ("turned_high", "xc_high", "merged_high", "coef_high"))
        xc_low, merged_low, coef_low = (sem(n) for n in ("xc_low", "merged_low", "coef_low"))
        dve_steps, act_steps = sem("dve_steps"), sem("act_steps")
        pool_ready = sem("pool_ready")
        h_ready, sumsq_ready, var_ready, rstd_ready = (sem(n) for n in ("h_ready", "sumsq_ready", "var_ready", "rstd_ready"))
        normed, turned, xT_ready = sem("normed"), sem("turned"), sem("xT_ready")
        lam_neg, lam_exp, params_ready = sem("lam_neg"), sem("lam_exp"), sem("params_ready")
        pst_ready, xc_ready, vb_ready, cv_done = (sem(n) for n in ("pst_ready", "xc_ready", "vb_ready", "cv_done"))
        bb_used, sq_ready, inner_ready, tg_ready = (sem(n) for n in ("bb_used", "sq_ready", "inner_ready", "tg_ready"))
        ga_used, tm_ready, tm_used, ri_ready = (sem(n) for n in ("ga_used", "tm_ready", "tm_used", "ri_ready"))
        tt_ready, decay_ready, m_ready, root_ready = (sem(n) for n in ("tt_ready", "decay_ready", "m_ready", "root_ready"))
        merged_ready = sem("merged_ready")
        q_ready, score_done, sc_ready, sc_used = (sem(n) for n in ("q_ready", "score_done", "sc_ready", "sc_used"))
        shifted_ready, exp_ready, sel_ready, sel_turned, chosen_ready = (
            sem(n) for n in ("shifted_ready", "exp_ready", "sel_ready", "sel_turned", "chosen_ready"))
        one_hots_ready, scat_done, w_written = sem("one_hots_ready"), sem("scat_done"), sem("w_written")
        gelu_ready, coef_ready = sem("gelu_ready"), sem("coef_ready")
        angle_ready, rope_ready, lamdot_ready, lamexp_ready = (
            sem(n) for n in ("angle_ready", "rope_ready", "lamdot_ready", "lamexp_ready"))
        att_sems = []
        for kind in ("diff", "fox"):
            att_sems.append({n: sem(f"{kind}_{n}") for n in (
                "v_ready", "qk_ready", "rotated", "rope_done", "scores_done", "max_ready", "probs_ready",
                "mixed_ready", "turned", "turned_ready", "pv_done", "osq_ready", "ovar_ready",
                "orstd_ready", "o_ready", "masked")})
        fz_ready, fexp_ready, bias_ready = (sem(n) for n in ("fz_ready", "fexp_ready", "bias_ready"))
        ffn_sems = [{n: sem(f"ffn{l}_{n}") for n in ("conv_ready", "silu_ready", "hid_ready", "hid_high", "hid_low")} for l in range(2)]
        block = ctx.enter_context(nc.Block())

        def rounds(eng, n, body):
            body(0)
            with eng.Fori(1, n) as it:
                body(it)

        def opening(it):
            return isinstance(it, int) and it == 0

        def following(it, e):
            return (it, 1) if e == 0 else (it + 1, 0)

        def all_pairs(eng, body, n=4, chain=None, steps=0, last_steps=0):
            body(0, 0)
            body(0, 1)
            with eng.Fori(1, n - 1) as it:
                if chain:
                    chain.enter(it, steps, 1)
                body(it, 0)
                body(it, 1)
            if chain:
                chain.leave(n - 2)
            body(n - 1, 0)
            body(n - 1, 1, last=True)

        def expert_steps(eng, step):
            with eng.Fori(0, 31) as it:
                for j in range(1, 5):
                    step(j, it)
            for j in range(NKEYS - 3, NKEYS):
                step(j, 0)

        def ffn_steps(eng, step, chain=None, steps=0):
            step(0, 0)
            with eng.Fori(0, 4) as it:
                if chain:
                    chain.enter(it, 4 * steps)
                for n in range(1, 5):
                    step(n, it)
            if chain:
                chain.leave(4)
            for n in range(17, FF_CHUNKS):
                step(n, 0)

        @block.sync
        def _(sp):
            def load(p, src, n=D):
                if not (isinstance(p.before, int) and p.before == 0):
                    sp.wait_ge(slot_low[p.slot], p.before)
                sp.dma_start(cols(raw, p, 0, n), src).then_inc(slot_loaded[p.slot], 16)

            def pick(t, i):
                return t[i] if isinstance(i, int) else t[bass.ds(i, 1)].rearrange("o p n -> (o p) n")

            def mix_round(c):
                for g in range(MIX_GROUPS):
                    load(Piece("mix", g, c, 8), pick(w_mix[g], c))
                load(Piece("mix", 7, c, 8), pick(w_gate, c), 2 * PARTS)

            rounds(sp, KC, mix_round)
            for k in range(KC):
                load(Piece("mix_out", k), w_out[k])
            for q in range(16):
                if q == 4:
                    sp.wait_ge(h_ready, 1)
                    sp.dma_start(h_saved, h_tok[:, :]).then_inc(h_kept, 16)
                load(Piece("query", q), w_query[q])
            for j in range(3):
                load(piece_u(j), u_tab[j])
            sp.wait_ge(one_hots_ready, SEQ // 4)

            def expert_step(j, it):
                load(piece_v(j, it), pick(v_tab, it * 4 + j))
                if j < NKEYS - 3:
                    load(piece_u(j + 3, it), pick(u_tab, it * 4 + (j + 3)))

            expert_step(0, 0)
            expert_steps(sp, expert_step)
            sp.wait_ge(coef_ready, 120)
            sp.wait_ge(h_kept, 16)
            sp.dma_start(h_back, h_saved).then_inc(h_back_loaded, 16)
            sp.dma_start(rope[:, 0:SEQ].bitcast(I32), positions_in.partition_broadcast(PARTS)).then_inc(pos_loaded, 16)
            sp.dma_start(mask, mask_in).then_inc(mask_loaded, 16)

            def attention_weights(kind, v_src, qk_src, out_src):
                for k in range(KC):
                    load(Piece(f"{kind}_v", k), v_src[k])
                if kind == "fox":
                    load(Piece("fox_f", 0), fox_f)
                with sp.Fori(0, 4) as it:
                    for n in range(4):
                        load(Piece(f"{kind}_qk", n, it, 4), pick(qk_src, it * 4 + n))
                for k in range(KC):
                    load(Piece(f"{kind}_out", k), out_src[k])

            def ffn_weights(l):
                def step(n, it):
                    if n < FF_CHUNKS - 1:
                        load(piece_gate(l, n + 1, it), pick(ffn_in[l], it * 8 + (2 * n + 2)))
                        load(piece_up(l, n + 1, it), pick(ffn_in[l], it * 8 + (2 * n + 3)))
                    load(piece_out(l, n, it), pick(ffn_out[l], it * 4 + n))

                load(piece_gate(l, 0), ffn_in[l][0])
                load(piece_up(l, 0), ffn_in[l][1])
                ffn_steps(sp, step)

            attention_weights("diff", diff_v, diff_qk, diff_out)
            ffn_weights(0)
            attention_weights("fox", fox_v, fox_qk, fox_out)
            ffn_weights(1)
            sp.wait_ge(normed, 7)
            sp.dma_start(out, h_tok[:, :].rearrange("p (b d) -> p b d", b=TB)).then_inc(stored, 16)
            sp.wait_ge(stored, 16)

        @block.gpsimd
        def _(pool):
            pool.memset(stats[:, :], -0.5).then_inc(pool_ready, 1)

            def inverse_roots(first, last):
                for k in range(first, last):
                    pool.wait_ge(var_ready, k + 1)
                    pool.tensor_tensor(rstd, var, halfpow, ALU.pow).then_inc(rstd_ready, 1)

            pool.wait_ge(pool_ready, 1)
            inverse_roots(0, 3)
            pool.memset(ones256, 1.0).then_inc(pool_ready, 1)
            s = att_sems[0]
            with pool.Fori(0, HEADS) as it:
                pool.wait_ge(s["ovar_ready"], it + 1)
                pool.tensor_tensor(orstd, ovar, halfpow2, ALU.pow).then_inc(s["orstd_ready"], 1)
            inverse_roots(3, 7)

        @block.scalar
        def _(a):
            chain = Chain(a, act_steps)
            a.dma_start(h_tok[:, :].rearrange("p (b d) -> p b d", b=TB), x).then_inc(x_loaded, 16)
            a.dma_start(consts[:, :], consts_in).then_inc(consts_loaded, 16)
            a.dma_start(params[:, :], params_in).then_inc(small_loaded, 16)
            a.dma_start(keysT, keys).then_inc(keys_loaded, 16)
            a.dma_start(ffn_params[:, :], ffn_params_in).then_inc(small_loaded, 16)
            a.dma_start(subln[:, :], subln_in.partition_broadcast(PARTS)).then_inc(small_loaded, 16)
            a.dma_start(lambdas, lambdas_in.partition_broadcast(PARTS)).then_inc(small_loaded, 16)

            def load_rows(first, n):
                for r in range(n):
                    a.dma_start(rows[:, r * D:(r + 1) * D], rows_in[first + r:first + r + 1, :].partition_broadcast(PARTS)
                                ).then_inc(rows_loaded, 16)

            def sum_squares(k, centred):
                if k >= 1:
                    a.wait_ge(h_ready, k)
                for b in range(TB):
                    bias = negmean[:, b:b + 1] if centred else 0.0
                    ins = a.activation(tmp[:, b * D:(b + 1) * D], h_tok[:, b * D:(b + 1) * D], ACT.Square,
                                       bias=bias, accum_out=sumsq[:, b:b + 1])
                ins.then_inc(sumsq_ready, 1)

            def take_high(p, n=D):
                a.wait_ge(slot_loaded[p.slot], p.loads)
                if not (isinstance(p.before, int) and p.before == 0):
                    a.wait_ge(slot_done[p.slot], p.before)
                a.activation(cols(high, p, 0, n), cols(raw, p, 0, n), ACT.Copy).then_inc(slot_high[p.slot], 1)

            def ahead(p, n=D):
                if p.n + RING < TOTAL:
                    take_high(p.later(RING), n)

            def evacuate_turned(k, gain=None):
                for b in range(4):
                    a.wait_ge(turned, 4 * k + b + 1)
                    if gain is None:
                        ins = a.activation(xh[:, b * HALF:(b + 1) * HALF], bank(b), ACT.Copy)
                    else:
                        for c in (2 * b, 2 * b + 1):
                            ins = a.activation(chunk_of(xh, c), bank(b, (c % 2) * SEQ, SEQ), ACT.Copy,
                                               scale=params[:, c * NP + gain:c * NP + gain + 1])
                    ins.then_inc(turned_high, 1)

            a.wait_ge(x_loaded, 16)
            a.wait_ge(pool_ready, 1)
            sum_squares(0, False)
            a.wait_ge(lam_neg, 1)
            a.activation(part(mx + 4200, KC), part(mx + 4200, KC), ACT.Exp, scale=-1.0).then_inc(lam_exp, 1)
            a.wait_ge(lamdot_ready, 1)
            a.activation(lam2, lam2, ACT.Exp).then_inc(lamexp_ready, 1)
            for n in range(RING):
                take_high(Piece("mix", n))
            a.wait_ge(small_loaded, 16 * 4)
            evacuate_turned(0, G1)

            def mix_round(c):
                later = not isinstance(c, int)
                piece = [Piece("mix", g, c, 8) for g in range(8)]
                for g in range(3):
                    ahead(piece[g])
                if later:
                    a.wait_ge(cv_done, c)
                a.activation(vb_sb, bank(1, 0, SEQ), ACT.Copy).then_inc(vb_ready, 1)
                a.wait_ge(xc_ready, c + 1)
                if later:
                    a.wait_ge(slot_done[3], piece[7].later(-8).count)
                a.activation(chunk_of(yh, 0), xc, ACT.Copy).then_inc(xc_high, 1)
                ahead(piece[3], 2 * PARTS)
                ahead(piece[4])
                if later:
                    a.wait_ge(ga_used, c)
                a.activation(sq, bank(3, 0, SEQ), ACT.Square).then_inc(sq_ready, 1)
                ahead(piece[5])
                a.wait_ge(inner_ready, c + 1)
                a.activation(tg, inner, ACT.Tanh, scale=GELU_C).then_inc(tg_ready, 1)
                ahead(piece[6])
                if later:
                    a.wait_ge(tm_used, c)
                a.activation(tm, bank(4), ACT.Tanh, scale=0.5).then_inc(tm_ready, 1)
                ahead(piece[7])
                a.wait_ge(pst_ready, c + 1)
                if later:
                    a.wait_ge(m_ready, c)
                a.activation(tr, bank(5, 0, SEQ), ACT.Tanh, scale=0.5, bias=pst[:, HBA:HBA + 1])
                a.activation(ti, bank(5, SEQ, SEQ), ACT.Tanh, scale=0.5, bias=pst[:, HBX:HBX + 1]).then_inc(ri_ready, 1)
                a.wait_ge(ri_ready, c + 1)
                a.activation(tt, tr, ACT.Tanh, scale=pst[:, SP4:SP4 + 1], bias=pst[:, SP4:SP4 + 1]).then_inc(tt_ready, 1)
                a.activation(at(arena, c * SEQ + M_A, SEQ), tr, ACT.Exp, scale=pst[:, NSP4:NSP4 + 1],
                             bias=pst[:, NSP4:NSP4 + 1]).then_inc(decay_ready, 1)

            rounds(a, KC, mix_round)
            a.wait_ge(m_ready, KC)
            for c in range(KC):
                m = part(M_M + c * SEQ, SEQ)
                a.activation(m, m, ACT.Sqrt, scale=0.5).then_inc(root_ready, 1)
            for c in range(KC):
                a.wait_ge(merged_ready, c + 1)
                a.activation(chunk_of(xh, c), merged[c % 2], ACT.Copy).then_inc(merged_high, 1)
                if c >= 2:
                    ahead(Piece("mix_out", c - 2))
            for c in (KC - 2, KC - 1):
                ahead(Piece("mix_out", c))

            sum_squares(1, False)
            evacuate_turned(1, G2)
            for it in range(4):
                for q in range(4):
                    p = Piece("query", 4 * it + q)
                    a.wait_ge(slot_done[p.slot], p.count)
                    if it >= 1:
                        a.wait_ge(score_done, it)
                    a.activation(qs[:, q * SEQ:(q + 1) * SEQ], bank(4 + q, 0, SEQ), ACT.Copy).then_inc(q_ready, 1)
                    if 4 * it + q < 15:
                        ahead(p)
                a.wait_ge(score_done, it + 1)
                if it >= 2:
                    a.wait_ge(sc_used, it - 1)
                for b in range(TB):
                    ins = a.activation(sc[it % 2][:, b * HALF:(b + 1) * HALF], bank(2 * (it % 2) + b), ACT.Copy)
                ins.then_inc(sc_ready, 1)
            a.wait_ge(shifted_ready, 1)
            a.activation(sel[:, 0:SEQ], sel[:, 0:SEQ], ACT.Exp).then_inc(exp_ready, 1)
            for b in range(2):
                a.wait_ge(sel_turned, b + 1)
                n = (2 - b) * SEQ
                a.activation(chosen[:, b * HALF:b * HALF + n], bank(b, 0, n), ACT.Copy).then_inc(chosen_ready, 1)

            w3 = arena[:, :].rearrange("p (j t) -> p j t", t=SEQ)
            with a.Fori(0, SEQ // 16) as it:
                for g in range(4):
                    dst = w3[:, :, bass.ds(it * 16 + 4 * g, 4)].rearrange("p j t -> p t j")
                    a.wait_ge(scat_done, it * 4 + (g + 1))
                    a.activation(dst, bank(g).rearrange("p (t j) -> p t j", t=4), ACT.Copy).then_inc(w_written, 1)

            def gelu_block(j, it=0, first=False):
                p = piece_u(j, it)
                a.wait_ge(slot_done[p.slot], p.count)
                if not first:
                    a.wait_ge(coef_low, it * 4 + (j - 1))
                a.activation(coef[j % 2], bank(4 + j % 4, 0, SEQ), ACT.Gelu_apprx_tanh).then_inc(gelu_ready, 1)

            def coef_high_part(j, it=0, first=False):
                a.wait_ge(coef_ready, it * 4 + (j + 1))
                if not first:
                    p = piece_v(j - 2, it)
                    a.wait_ge(slot_done[p.slot], p.count)
                a.activation(chunk_of(yh, j % 2), coef[j % 2], ACT.Copy).then_inc(coef_high, 1)

            def expert_step(j, it):
                if j + 2 < NKEYS:
                    gelu_block(j + 2, it)
                ahead(piece_v(j, it))
                if j + 2 < NKEYS:
                    coef_high_part(j + 2, it)
                if j + 3 < NKEYS:
                    ahead(piece_u(j + 3, it))

            a.wait_ge(scat_done, SEQ // 4)
            gelu_block(0, first=True)
            gelu_block(1, first=True)
            take_high(piece_v(0))
            coef_high_part(0, first=True)
            coef_high_part(1, first=True)
            for j in range(3):
                ahead(piece_u(j))
            expert_step(0, 0)
            expert_steps(a, expert_step)
            load_rows(0, 1)
            a.dma_start(fbias[0:16, :], forget_bias_in).then_inc(bias_loaded, 16)

            sum_squares(2, False)
            evacuate_turned(2)
            load_rows(1, 2)
            a.wait_ge(angle_ready, 1)
            a.activation(rope, angles, ACT.Sin).then_inc(rope_ready, 1)

            def attention(kind, s):
                for k in range(KC):
                    ahead(Piece(f"{kind}_v", k))
                for b in range(4):
                    ins = a.activation(v_tok[:, b * HALF:(b + 1) * HALF], bank(b), ACT.Copy)
                ins.then_inc(s["v_ready"], 1)
                if kind == "fox":
                    ahead(Piece("fox_f", 0))
                    a.wait_ge(fz_ready, 1)
                    a.activation(fz_e, fz_e, ACT.Exp, scale=-1.0).then_inc(fexp_ready, 1)

                def qk_out(it, e):
                    k_piece = Piece(f"{kind}_qk", 2 * e + 1, it, 4)
                    a.wait_ge(slot_done[k_piece.slot], k_piece.count)
                    if not opening(it):
                        a.wait_ge(s["rope_done" if kind == "diff" else "scores_done"], it * 2 + (e - 1))
                    a.activation(qk[e], bank(4), ACT.Copy).then_inc(s["qk_ready"], 1)

                def pair(it, e, last=False):
                    n1 = it * 2 + (e + 1)
                    for n in range(2):
                        ahead(Piece(f"{kind}_qk", 2 * e + n, it, 4))
                    a.wait_ge(s["max_ready"], n1)
                    for m in range(4):
                        ins = a.activation(pr[:, m * SEQ:(m + 1) * SEQ], sm[:, m * SEQ:(m + 1) * SEQ], ACT.Exp,
                                           scale=SCALE, bias=nb4[:, m:m + 1], accum_out=l4[:, m:m + 1])
                    ins.then_inc(s["probs_ready"], 1)
                    if not last:
                        qk_out(*following(it, e))
                    a.wait_ge(s["turned"], n1)
                    if kind == "diff":
                        a.activation(pT[:, 0:384], bank(6, 0, 384), ACT.Copy).then_inc(s["turned_ready"], 1)
                        a.wait_ge(s["pv_done"], n1)
                        for b in range(TB):
                            ins = a.activation(squares[:, b * PARTS:(b + 1) * PARTS], bank(7, b * PARTS, PARTS), ACT.Square, accum_out=osq[:, b:b + 1])
                        ins.then_inc(s["osq_ready"], 1)
                    else:
                        for m in range(2):
                            ins = a.activation(pT[:, m * 384:m * 384 + 384], bank(5 + m, 0, 384), ACT.Copy)
                        ins.then_inc(s["turned_ready"], 1)

                qk_out(0, 0)
                all_pairs(a, pair)

            def output(kind, k_turn):
                evacuate_turned(k_turn)
                for k in range(KC):
                    ahead(Piece(f"{kind}_out", k))

            def ffn(l):
                s = ffn_sems[l]

                def hidden(n, it=0, first=False):
                    ahead(piece_gate(l, n, it))
                    a.wait_ge(s["conv_ready"], it * 4 + (n + 1))
                    a.activation(act[n % 2], conv[n % 2], ACT.Silu).then_inc(s["silu_ready"], 1)
                    ahead(piece_up(l, n, it))
                    a.wait_ge(s["hid_ready"], it * 4 + (n + 1))
                    if not first:
                        p = piece_out(l, n - 2, it)
                        a.wait_ge(slot_done[p.slot], p.count)
                    a.activation(chunk_of(yh, n % 2), hid[n % 2], ACT.Copy).then_inc(s["hid_high"], 1)

                def step(n, it):
                    if n + 1 < FF_CHUNKS:
                        hidden(n + 1, it, first=(opening(it) and n == 0))
                    ahead(piece_out(l, n, it))

                hidden(0, first=True)
                ffn_steps(a, step)

            attention("diff", att_sems[0])
            output("diff", 3)
            sum_squares(3, True)
            evacuate_turned(4)
            load_rows(3, 2)
            ffn(0)
            sum_squares(4, True)
            evacuate_turned(5)
            load_rows(5, 2)
            attention("fox", att_sems[1])
            output("fox", 6)
            sum_squares(5, True)
            evacuate_turned(7)
            load_rows(7, 2)
            ffn(1)
            sum_squares(6, True)

        @block.tensor
        def _(pe):
            def turn(k, src):
                for b in range(4):
                    for c in (2 * b, 2 * b + 1):
                        for t in range(TB):
                            ins = pe.transpose(bank(b, (c % 2) * SEQ + t * PARTS, PARTS),
                                               src[:, t * D + c * PARTS:t * D + (c + 1) * PARTS], ident)
                    ins.then_inc(turned, 1)

            def products(dst, left, right, start, stop):
                pe.matmul(dst, left[1], right[0], start=start, stop=False)
                pe.matmul(dst, left[0], right[1], start=False, stop=False)
                return pe.matmul(dst, left[0], right[0], start=False, stop=stop)

            def project_in(p, dst):
                pe.wait_ge(slot_low[p.slot], p.count)
                for k in range(KC):
                    ins = products(dst, (cols(high, p, k * PARTS, PARTS), cols(low, p, k * PARTS, PARTS)),
                                   (chunk_of(xh, k), chunk_of(xl, k)), k == 0, k == KC - 1)
                ins.then_inc(slot_done[p.slot], 1)

            def project_out(p, src_high, src_low, k, first, last):
                pe.wait_ge(slot_low[p.slot], p.count)
                for t in range(TB):
                    xs = slice(k * SEQ + t * PARTS, k * SEQ + (t + 1) * PARTS)
                    for half in range(2):
                        pe.matmul(bank(2 * t + half), src_low[:, xs], cols(high, p, half * HALF, HALF), start=first, stop=False)
                    for half in range(2):
                        pe.matmul(bank(2 * t + half), src_high[:, xs], cols(low, p, half * HALF, HALF), start=False, stop=False)
                    for half in range(2):
                        ins = pe.matmul(bank(2 * t + half), src_high[:, xs], cols(high, p, half * HALF, HALF), start=False, stop=last)
                ins.then_inc(slot_done[p.slot], 1)

            pe.wait_ge(consts_loaded, 16)
            pe.wait_ge(normed, 1)
            turn(0, tmp)
            pe.wait_ge(xT_ready, 4)

            def mix_round(c):
                later = not isinstance(c, int)
                dsts = [(bank(0, 0, SEQ), xc_ready), (bank(1, 0, SEQ), cv_done), (bank(1, SEQ, SEQ), None),
                        (bank(2, 0, SEQ), bb_used), (bank(3, 0, SEQ), ga_used), (bank(4, 0, SEQ), tm_ready),
                        (bank(4, SEQ, SEQ), None)]
                for g, (dst, free) in enumerate(dsts):
                    if later and free is not None:
                        pe.wait_ge(free, c)
                    project_in(Piece("mix", g, c, 8), dst)
                gate = Piece("mix", 7, c, 8)
                pe.wait_ge(xc_low, c + 1)
                pe.wait_ge(slot_low[gate.slot], gate.count)
                if later:
                    pe.wait_ge(ri_ready, c)
                for n in range(2):
                    ins = products(bank(5, n * SEQ, SEQ), (cols(high, gate, n * PARTS, PARTS), cols(low, gate, n * PARTS, PARTS)),
                                   (chunk_of(yh, 0), chunk_of(yl, 0)), True, True)
                ins.then_inc(slot_done[gate.slot], 1)

            rounds(pe, KC, mix_round)
            for k in range(KC):
                pe.wait_ge(merged_low, k + 1)
                project_out(Piece("mix_out", k), xh, xl, k, k == 0, k == KC - 1)

            pe.wait_ge(normed, 2)
            turn(1, tmp)
            pe.wait_ge(xT_ready, 8)
            pe.wait_ge(keys_loaded, 16)
            for it in range(4):
                for q in range(4):
                    if it >= 1:
                        pe.wait_ge(q_ready, 4 * (it - 1) + q + 1)
                    project_in(Piece("query", 4 * it + q), bank(4 + q, 0, SEQ))
                if it >= 2:
                    pe.wait_ge(sc_ready, it - 1)
                for q in range(4):
                    pe.wait_ge(q_ready, 4 * it + q + 1)
                    for t in range(TB):
                        ins = pe.matmul(bank(2 * (it % 2) + t, q * PARTS, PARTS),
                                        qs[:, q * SEQ + t * PARTS:q * SEQ + (t + 1) * PARTS],
                                        keysT[:, (4 * it + q) * PARTS:(4 * it + q + 1) * PARTS], start=True, stop=True)
                ins.then_inc(score_done, 1)
            for j in range(3):
                if j == 0:
                    pe.wait_ge(q_ready, 16)
                project_in(piece_u(j), bank(4 + j, 0, SEQ))
            pe.wait_ge(sel_ready, 1)
            for n in range(3):
                for t in range(TB):
                    ins = pe.transpose(bank(n // 2, (n % 2) * SEQ + t * PARTS, PARTS),
                                       sel[:, n * SEQ + t * PARTS:n * SEQ + (t + 1) * PARTS], ident)
                if n != 0:
                    ins.then_inc(sel_turned, 1)

            def scatter_round(it):
                for g in range(4):
                    pe.wait_ge(one_hots_ready, it * 4 + (g + 1))
                    if not opening(it):
                        pe.wait_ge(w_written, it * 4 + (g - 3))
                    for u in range(4):
                        ins = pe.matmul(bank(g, u * PARTS, PARTS), one_hot[g % 2][:, u * PARTS:(u + 1) * PARTS],
                                        one_hot_w[g % 2][:, u * PARTS:(u + 1) * PARTS], start=True, stop=True)
                    ins.then_inc(scat_done, 1)

            rounds(pe, SEQ // 16, scatter_round)

            def expert_step(j, it):
                pe.wait_ge(coef_low, it * 4 + (j + 1))
                project_out(piece_v(j, it), chunk_of(yh, j % 2), chunk_of(yl, j % 2), 0,
                            first=(opening(it) and j == 0), last=(j == NKEYS - 1))
                if j + 3 < NKEYS:
                    if not (opening(it) and j == 0):
                        pe.wait_ge(gelu_ready, it * 4 + j)
                    project_in(piece_u(j + 3, it), bank(4 + (j + 3) % 4, 0, SEQ))

            pe.wait_ge(w_written, SEQ // 4)
            expert_step(0, 0)
            expert_steps(pe, expert_step)

            pe.wait_ge(normed, 3)
            turn(2, h_tok)

            def attention(kind, s, k_turn):
                pe.wait_ge(xT_ready, 4 * k_turn)
                for k in range(KC):
                    project_out(Piece(f"{kind}_v", k), xh, xl, k, k == 0, k == KC - 1)
                if kind == "fox":
                    project_in(Piece("fox_f", 0), bank(7, 0, SEQ))

                def project(it, e, n):
                    project_in(Piece(f"{kind}_qk", 2 * e + n, it, 4), bank(4, n * SEQ, SEQ))

                def rotate(it, e):
                    pe.wait_ge(s["qk_ready"], it * 2 + (e + 1))
                    pe.matmul(bank(5), perm, qk[e], start=True, stop=True).then_inc(s["rotated"], 1)

                def pair(it, e, last=False):
                    n1 = it * 2 + (e + 1)
                    src = (qkr if kind == "diff" else qk)[e]
                    pe.wait_ge(s["rope_done" if kind == "diff" else "qk_ready"], n1)
                    if not opening(it):
                        pe.wait_ge(s["max_ready"], it * 2 + (e - 1))
                    elif e == 0:
                        pe.wait_ge(s["v_ready"], 1)
                        if kind == "fox":
                            pe.wait_ge(bias_ready, 1)
                    for m in range(2):
                        for t in range(TB):
                            dst = bank(2 * e + m, t * SEQ, SEQ)
                            if kind == "fox":
                                pe.matmul(dst, ones, at(bias_rows, it * 4 * SEQ + (2 * e + m) * SEQ, SEQ),
                                          start=True, stop=False)
                            ins = pe.matmul(dst, src[64 * m:64 * m + 64, t * PARTS:(t + 1) * PARTS],
                                            src[64 * m:64 * m + 64, SEQ:2 * SEQ], start=(kind == "diff"), stop=True)
                    ins.then_inc(s["scores_done"], 1)
                    nxt = following(it, e)
                    if not last:
                        project(*nxt, 0)
                        project(*nxt, 1)
                    if kind == "diff":
                        if not last:
                            rotate(*nxt)
                        pe.wait_ge(s["mixed_ready"], n1)
                        for n, (t, k) in enumerate(((0, 0), (1, 0), (1, 1))):
                            ins = pe.transpose(bank(6, n * PARTS, PARTS), att[:, t * SEQ + k * PARTS:t * SEQ + (k + 1) * PARTS], ident)
                        ins.then_inc(s["turned"], 1)
                    else:
                        pe.wait_ge(s["probs_ready"], n1)
                        for m in range(2):
                            for n, (t, k) in enumerate(((0, 0), (1, 0), (1, 1))):
                                lo = m * HALF + t * SEQ + k * PARTS
                                ins = pe.transpose(bank(5 + m, n * PARTS, PARTS), pr[:, lo:lo + PARTS], ident)
                        ins.then_inc(s["turned"], 1)
                    pe.wait_ge(s["turned_ready"], n1)
                    if not (opening(it) and e == 0):
                        pe.wait_ge(s["o_ready"], it * 2 + e)
                    if kind == "diff":
                        for t, terms in enumerate((((0, 0),), ((1, 0), (2, 1)))):
                            for n, k in terms:
                                ins = pe.matmul(bank(7, t * PARTS, PARTS), pT[:, n * PARTS:(n + 1) * PARTS],
                                                at(v_tok, it * 2 * PARTS + (k * D + e * PARTS), PARTS),
                                                start=(n < 2), stop=(n != 1))
                    else:
                        for m in range(2):
                            for t, terms in enumerate((((0, 0),), ((1, 0), (2, 1)))):
                                for n, k in terms:
                                    ins = pe.matmul(bank(7, (2 * m + t) * 64, 64), pT[:, m * 384 + n * PARTS:m * 384 + (n + 1) * PARTS],
                                                    at(v_tok, it * 4 * 64 + (k * D + (2 * e + m) * 64), 64),
                                                    start=(n < 2), stop=(n != 1))
                    ins.then_inc(s["pv_done"], 1)

                project(0, 0, 0)
                project(0, 0, 1)
                if kind == "diff":
                    rotate(0, 0)
                all_pairs(pe, pair)
                pe.wait_ge(s["o_ready"], 8)
                turn(k_turn, o_tok)
                pe.wait_ge(xT_ready, 4 * k_turn + 4)
                for k in range(KC):
                    project_out(Piece(f"{kind}_out", k), xh, xl, k, k == 0, k == KC - 1)

            def ffn(l, k_turn):
                s = ffn_sems[l]
                pe.wait_ge(normed, 4 + 2 * l)
                turn(k_turn, h_tok)
                pe.wait_ge(xT_ready, 4 * k_turn + 4)

                def gate_and_up(n, it=0):
                    project_in(piece_gate(l, n, it), bank(4 + 2 * (n % 2), 0, SEQ))
                    project_in(piece_up(l, n, it), bank(5 + 2 * (n % 2), 0, SEQ))

                def step(n, it):
                    if n + 1 < FF_CHUNKS:
                        if not (opening(it) and n == 0):
                            pe.wait_ge(s["hid_ready"], it * 4 + n)
                        gate_and_up(n + 1, it)
                    pe.wait_ge(s["hid_low"], it * 4 + (n + 1))
                    project_out(piece_out(l, n, it), chunk_of(yh, n % 2), chunk_of(yl, n % 2), 0,
                                first=(opening(it) and n == 0), last=(n == FF_CHUNKS - 1))

                gate_and_up(0)
                ffn_steps(pe, step)

            attention("diff", att_sems[0], 3)
            ffn(0, 4)
            pe.wait_ge(normed, 5)
            turn(5, h_tok)
            attention("fox", att_sems[1], 6)
            ffn(1, 7)

        @block.vector
        def _(v):
            chain = Chain(v, dve_steps)
            link = chain.link

            def take_low(p, n=D):
                v.wait_ge(slot_high[p.slot], p.count)
                v.tensor_tensor(cols(low, p, 0, n), cols(raw, p, 0, n), cols(high, p, 0, n).bitcast(F32), ALU.subtract
                                ).then_inc(slot_low[p.slot], 1)

            def ahead(p, n=D):
                if p.n + RING < TOTAL:
                    take_low(p.later(RING), n)

            def low_of(dst, src, src_high):
                return v.tensor_tensor(dst, src, src_high.bitcast(F32), ALU.subtract)

            def evacuate_turned(k, gain=None):
                for b in range(4):
                    v.wait_ge(turned_high, 4 * k + b + 1)
                    if gain is None:
                        ins = low_of(xl[:, b * HALF:(b + 1) * HALF], bank(b), xh[:, b * HALF:(b + 1) * HALF])
                    else:
                        for c in (2 * b, 2 * b + 1):
                            ins = v.scalar_tensor_tensor(out=chunk_of(xl, c), in0=bank(b, (c % 2) * SEQ, SEQ),
                                                         scalar=params[:, c * NP + gain:c * NP + gain + 1],
                                                         in1=chunk_of(xh, c).bitcast(F32), op0=ALU.mult, op1=ALU.subtract)
                    ins.then_inc(xT_ready, 1)

            def log1p_of_exp(dst, e, t):
                z, z2 = t
                link(v.tensor_scalar(z, e, 2.0, None, ALU.add))
                link(v.reciprocal(z, z))
                link(v.tensor_tensor(z, z, e, ALU.mult))
                link(v.tensor_tensor(z2, z, z, ALU.mult))
                link(v.tensor_scalar(dst, z2, 1.0 / 15.0, None, ALU.mult))
                for n in (13, 11, 9, 7, 5, 3):
                    link(v.scalar_tensor_tensor(out=dst, in0=dst, scalar=1.0 / n, in1=z2, op0=ALU.add, op1=ALU.mult))
                link(v.scalar_tensor_tensor(out=dst, in0=dst, scalar=1.0, in1=z, op0=ALU.add, op1=ALU.mult))
                link(v.tensor_scalar(dst, dst, 2.0, None, ALU.mult))

            def variance(k, eps):
                v.wait_ge(sumsq_ready, k + 1)
                v.tensor_scalar(var, sumsq, 1.0 / D, eps, ALU.mult, ALU.add).then_inc(var_ready, 1)
                v.wait_ge(rstd_ready, k + 1)

            def rms(k):
                variance(k, EPS_RMS)
                for b in range(TB):
                    ins = v.tensor_scalar(tmp[:, b * D:(b + 1) * D], h_tok[:, b * D:(b + 1) * D], rstd[:, b:b + 1], None, ALU.mult)
                ins.then_inc(normed, 1)

            def row(n):
                return rows[:, n * D:(n + 1) * D].unsqueeze(1).to_broadcast([PARTS, TB, D])

            h3 = h_tok[:, :].rearrange("p (b d) -> p b d", b=TB)

            def layer_norm(k, last):
                v.wait_ge(slot_done[last.slot], last.count)
                for n in range(4):
                    h = h_tok[:, n * HALF:(n + 1) * HALF]
                    ins = v.scalar_tensor_tensor(out=h, in0=h, scalar=ALPHA, in1=bank(n), op0=ALU.mult, op1=ALU.add,
                                                 accum_out=sum4[:, n:n + 1])
                link(ins)
                link(v.tensor_tensor(negmean, sum4[:, 0:4:2], sum4[:, 1:4:2], ALU.add))
                v.tensor_scalar(negmean, negmean, -1.0 / D, None, ALU.mult).then_inc(h_ready, 1)
                variance(k, EPS_LN)
                for b in range(TB):
                    h = h_tok[:, b * D:(b + 1) * D]
                    ins = v.tensor_scalar(h, h, negmean[:, b:b + 1], rstd[:, b:b + 1], ALU.add, ALU.mult)
                link(ins)
                v.wait_ge(rows_loaded, 16 + 32 * (k - 2))
                link(v.tensor_tensor(h3, h3, row(0), ALU.mult))
                v.tensor_tensor(h3, h3, row(1), ALU.add).then_inc(normed, 1)

            v.wait_ge(pool_ready, 1)
            v.wait_ge(small_loaded, 16 * 4)
            p3 = params[:, :].rearrange("p (c n) -> p c n", n=NP)
            lam, small = p3[:, :, LAM], [part(mx + 4200 + 8 * n, KC) for n in range(5)]
            link(v.tensor_scalar(small[1], lam, -1.0, None, ALU.mult))
            v.tensor_tensor(small[0], small[1], lam, ALU.max).then_inc(lam_neg, 1)
            l4v = lambdas.rearrange("p (n w d) -> p n w d", n=2, w=2)
            pairs = lam_prod.rearrange("p (n d) -> p n d", n=2)
            link(v.tensor_tensor(pairs, l4v[:, :, 0, :], l4v[:, :, 1, :], ALU.mult))
            v.tensor_reduce(lam2, pairs, AX.X, ALU.add).then_inc(lamdot_ready, 1)
            v.wait_ge(lam_exp, 1)
            log1p_of_exp(small[2], small[0], small[3:5])
            link(v.tensor_scalar(small[1], small[1], 0.0, None, ALU.max))
            link(v.tensor_tensor(small[2], small[2], small[1], ALU.add))
            v.tensor_scalar(p3[:, :, SP4], small[2], 4.0, None, ALU.mult)
            v.tensor_scalar(p3[:, :, NSP4], small[2], -4.0, None, ALU.mult)
            v.tensor_scalar(p3[:, :, HBA], p3[:, :, BA], 0.5, None, ALU.mult)
            link(v.tensor_scalar(p3[:, :, HBX], p3[:, :, BX], 0.5, None, ALU.mult))
            v.wait_ge(x_loaded, 16)
            rms(0)
            v.wait_ge(lamexp_ready, 1)
            link(v.tensor_tensor(nlam, lam2[:, 1:2], lam2[:, 0:1], ALU.subtract))
            link(v.tensor_scalar(nlam, nlam, -LAMBDA_INIT, None, ALU.add))
            link(v.tensor_scalar(subln[:, :], subln[:, :], 1.0 - LAMBDA_INIT, None, ALU.mult))
            for n in range(RING):
                take_low(Piece("mix", n))
            evacuate_turned(0, G1)

            def mix_round(c):
                later = not isinstance(c, int)
                if later:
                    v.wait_ge(decay_ready, c)
                v.tensor_copy(pst, at(params, c * NP, NP)).then_inc(pst_ready, 1)
                v.wait_ge(pst_ready, c + 1)
                piece = [Piece("mix", g, c, 8) for g in range(8)]
                v.wait_ge(slot_done[0], piece[0].count)
                xa = bank(0, 0, SEQ)
                link(v.tensor_scalar(xc, xa, pst[:, CA + 3:CA + 4], pst[:, CAB:CAB + 1], ALU.mult, ALU.add))
                for k in (1, 2, 3):
                    ins = v.scalar_tensor_tensor(out=xc[:, k:], in0=xa[:, :SEQ - k], scalar=pst[:, CA + 3 - k:CA + 4 - k],
                                                 in1=xc[:, k:], op0=ALU.mult, op1=ALU.add)
                    if k < 3:
                        link(ins)
                ins.then_inc(xc_ready, 1)
                for g in range(3):
                    ahead(piece[g])
                v.wait_ge(xc_high, c + 1)
                low_of(chunk_of(yl, 0), xc, chunk_of(yh, 0)).then_inc(xc_low, 1)
                v.wait_ge(vb_ready, c + 1)
                v.tensor_tensor(cv, bank(1, SEQ, SEQ), vb_sb, ALU.mult).then_inc(cv_done, 1)
                v.wait_ge(cv_done, c + 1)
                link(v.tensor_scalar(yb, cv, pst[:, CB + 2:CB + 3], None, ALU.mult))
                for k in (1, 2):
                    link(v.scalar_tensor_tensor(out=yb[:, k:], in0=cv[:, :SEQ - k], scalar=pst[:, CB + 2 - k:CB + 3 - k],
                                                in1=yb[:, k:], op0=ALU.mult, op1=ALU.add))
                ahead(piece[3], 2 * PARTS)
                v.wait_ge(slot_done[3], piece[3].count)
                v.tensor_tensor(ybb, bank(2, 0, SEQ), yb, ALU.mult).then_inc(bb_used, 1)
                ahead(piece[4])
                v.wait_ge(sq_ready, c + 1)
                ga = bank(3, 0, SEQ)
                link(v.tensor_scalar(inner, sq, GELU_A, 1.0, ALU.mult, ALU.add))
                v.tensor_tensor(inner, ga, inner, ALU.mult).then_inc(inner_ready, 1)
                ahead(piece[5])
                v.wait_ge(tg_ready, c + 1)
                v.scalar_tensor_tensor(out=gg, in0=tg, scalar=1.0, in1=ga, op0=ALU.add, op1=ALU.mult).then_inc(ga_used, 1)
                ahead(piece[6])
                v.wait_ge(ga_used, c + 1)
                v.wait_ge(bb_used, c + 1)
                v.wait_ge(tm_ready, c + 1)
                v.scalar_tensor_tensor(out=at(arena, c * SEQ + M_G1, SEQ), in0=tm[:, 0:SEQ], scalar=1.0, in1=gg,
                                       op0=ALU.add, op1=ALU.mult)
                v.scalar_tensor_tensor(out=at(arena, c * SEQ + M_G2, SEQ), in0=tm[:, SEQ:], scalar=1.0, in1=ybb,
                                       op0=ALU.add, op1=ALU.mult).then_inc(tm_used, 1)
                ahead(piece[7])
                v.wait_ge(ri_ready, c + 1)
                v.scalar_tensor_tensor(out=at(arena, c * SEQ + M_IX, SEQ), in0=ti, scalar=1.0, in1=xc,
                                       op0=ALU.add, op1=ALU.mult)
                v.wait_ge(tt_ready, c + 1)
                link(v.tensor_scalar(t1, tt, 1.0, None, ALU.add))
                link(v.reciprocal(rc, t1))
                v.tensor_tensor(at(arena, c * SEQ + M_M, SEQ), tt, rc, ALU.mult).then_inc(m_ready, 1)

            MIX_STEPS = 1 + 2 + 3 + 1 + 2
            chain.enter(0, MIX_STEPS)
            mix_round(0)
            chain.leave(1)
            with v.Fori(1, KC) as it:
                chain.enter(it, MIX_STEPS, 1)
                mix_round(it)
            chain.leave(KC - 1)
            v.wait_ge(m_ready, KC)
            for c in range(KC):
                v.wait_ge(root_ready, c + 1)
                u, m = part(M_IX + c * SEQ, SEQ), part(M_M + c * SEQ, SEQ)
                g1, g2 = part(M_G1 + c * SEQ, SEQ), part(M_G2 + c * SEQ, SEQ)
                link(v.tensor_tensor(u, u, m, ALU.mult))
                if c == 0:
                    v.wait_ge(decay_ready, KC)
                link(v.tensor_tensor_scan(m, part(M_A + c * SEQ, SEQ), u, 0.0, ALU.mult, ALU.add))
                link(v.tensor_tensor(g1, g1, m, ALU.mult))
                v.scalar_tensor_tensor(out=merged[c % 2], in0=g1, scalar=0.5, in1=g2, op0=ALU.mult, op1=ALU.add
                                       ).then_inc(merged_ready, 1)
                v.wait_ge(merged_high, c + 1)
                low_of(chunk_of(xl, c), merged[c % 2], chunk_of(xh, c)).then_inc(merged_low, 1)
                if c >= 2:
                    ahead(Piece("mix_out", c - 2))
            for c in (KC - 2, KC - 1):
                ahead(Piece("mix_out", c))
            last = Piece("mix_out", KC - 1)
            v.wait_ge(slot_done[last.slot], last.count)
            for n in range(4):
                h = h_tok[:, n * HALF:(n + 1) * HALF]
                ins = v.scalar_tensor_tensor(out=h, in0=bank(n), scalar=0.5, in1=h, op0=ALU.mult, op1=ALU.add)
            ins.then_inc(h_ready, 1)
            rms(1)
            evacuate_turned(1, G2)

            top4 = top1.rearrange("p (b q k) -> p b q k", b=TB, q=4)
            idx4 = idxf.rearrange("p (b q k) -> p b q k", b=TB, q=4)
            for it in range(4):
                v.wait_ge(sc_ready, it + 1)
                for q in range(4 * it, min(4 * it + 4, 15)):
                    ahead(Piece("query", q))
                tiles = [(b, q) for b in range(TB) for q in range(4)]

                def scores(b, q):
                    return sc[it % 2][:, b * HALF + q * PARTS:b * HALF + (q + 1) * PARTS]

                def places(t, b, q, n):
                    return t[:, (b * 4 + q) * 16 + 8 * n:(b * 4 + q) * 16 + 8 * n + 8]

                for b, q in tiles:
                    ins = v.max(places(top1, b, q, 0), scores(b, q))
                link(ins)
                for b, q in tiles:
                    v.max_index(places(idxu, b, q, 0), places(top1, b, q, 0), scores(b, q))
                    ins = v.match_replace(rest[:, (b * 4 + q) * PARTS:(b * 4 + q + 1) * PARTS], places(top1, b, q, 0),
                                          scores(b, q), -3e38)
                ins.then_inc(sc_used, 1)
                v.wait_ge(sc_used, it + 1)
                for b, q in tiles:
                    ins = v.max(places(top1, b, q, 1), rest[:, (b * 4 + q) * PARTS:(b * 4 + q + 1) * PARTS])
                link(ins)
                for b, q in tiles:
                    ins = v.max_index(places(idxu, b, q, 1), places(top1, b, q, 1),
                                      rest[:, (b * 4 + q) * PARTS:(b * 4 + q + 1) * PARTS])
                chain.step(ins)
                c4 = cand.rearrange("p (m a b) -> p m a b", m=4, a=16)
                t4 = top1.rearrange("p (m h k) -> p m h k", m=4, h=2)
                v.tensor_tensor(c4, t4[:, :, 0, :].unsqueeze(3).to_broadcast([PARTS, 4, 16, 16]),
                                t4[:, :, 1, :].unsqueeze(2).to_broadcast([PARTS, 4, 16, 16]), ALU.add)
                chain.wait()
                link(v.tensor_copy(idxf, idxu))

                def cd(t, m):
                    return t[:, m * 256:(m + 1) * 256]

                def bp(t, m, n):
                    return t[:, m * 16 + 8 * n:m * 16 + 8 * n + 8]

                for m in range(4):
                    ins = v.max(bp(best, m, 0), cd(cand, m))
                link(ins)
                for m in range(4):
                    v.max_index(bp(posu, m, 0), bp(best, m, 0), cd(cand, m))
                    ins = v.match_replace(cd(cand2, m), bp(best, m, 0), cd(cand, m), -3e38)
                link(ins)
                for m in range(4):
                    ins = v.max(bp(best, m, 1), cd(cand2, m))
                link(ins)
                for m in range(4):
                    ins = v.max_index(bp(posu, m, 1), bp(best, m, 1), cd(cand2, m))
                link(ins)
                b3 = best.rearrange("p (m k) -> p m k", m=4)
                heads = slice(32 * it, 32 * it + 32)
                sel3 = sel.rearrange("p (n b k) -> p n b k", n=3, b=TB)

                def chosen_of(n):
                    return sel3[:, n, :, heads].rearrange("p b (h k) -> p b h k", h=2)

                b4 = best.rearrange("p (b h k) -> p b h k", b=TB, h=2)
                for b in range(TB):
                    ins = v.tensor_tensor(chosen_of(0)[:, b], b4[:, b], b4[:, b, :, 0:1].to_broadcast([PARTS, 2, 16]), ALU.subtract)
                if it == 3:
                    ins.then_inc(shifted_ready, 1)
                for n, (by, op) in enumerate(((4, ALU.logical_shift_right), (15, ALU.bitwise_and))):
                    link(v.tensor_single_scalar(digit, posu, by, op))
                    link(v.tensor_copy(digitf, digit))
                    e4 = eqs.rearrange("p (m k a) -> p m k a", m=4, k=16)
                    d3 = digitf.rearrange("p (m k) -> p m k", m=4)
                    i4 = idxf.rearrange("p (m h a) -> p m h a", m=4, h=2)
                    link(v.tensor_tensor(e4, d3.unsqueeze(3).to_broadcast([PARTS, 4, 16, 16]),
                                         iota[:, 0:16].unsqueeze(1).unsqueeze(1).to_broadcast([PARTS, 4, 16, 16]), ALU.is_equal))
                    link(v.tensor_tensor(e4, e4, i4[:, :, n, :].unsqueeze(2).to_broadcast([PARTS, 4, 16, 16]), ALU.mult))
                    for b in range(TB):
                        ins = v.tensor_reduce(chosen_of(1 + n)[:, b], e4[:, 2 * b:2 * b + 2], AX.X, ALU.add)
                    chain.step(ins)
            v.wait_ge(exp_ready, 1)
            w3 = sel[:, 0:SEQ].rearrange("p (g k) -> p g k", k=16)
            s16 = expsum[:, 0:16]
            link(v.tensor_reduce(s16, w3, AX.X, ALU.add))
            link(v.reciprocal(s16, s16))
            chain.wait()
            v.tensor_tensor(w3, w3, s16.unsqueeze(2).to_broadcast([PARTS, 16, 16]), ALU.mult).then_inc(sel_ready, 1)

            v.wait_ge(chosen_ready, 2)
            v.wait_ge(h_kept, 16)
            weight, sel_i, sel_j = (chosen[:, n * SEQ:(n + 1) * SEQ] for n in range(3))
            iota4 = iota.unsqueeze(1).to_broadcast([PARTS, 4, PARTS])

            def one_hot_round(it):
                for g in range(4):
                    if not (opening(it) and g < 2):
                        v.wait_ge(scat_done, it * 4 + (g - 1))
                    v.tensor_tensor(one_hot[g % 2].rearrange("p (t i) -> p t i", t=4),
                                    at(sel_i, it * 16 + 4 * g, 4).unsqueeze(2).to_broadcast([PARTS, 4, PARTS]),
                                    iota4, ALU.is_equal)
                    for u in range(4):
                        ins = v.tensor_scalar(one_hot_w[g % 2][:, u * PARTS:(u + 1) * PARTS], iota,
                                              at(sel_j, it * 16 + (4 * g + u), 1), at(weight, it * 16 + (4 * g + u), 1),
                                              ALU.is_equal, ALU.mult)
                    ins.then_inc(one_hots_ready, 1)

            rounds(v, SEQ // 16, one_hot_round)

            def weigh(j, it=0):
                v.wait_ge(gelu_ready, it * 4 + (j + 1))
                v.tensor_tensor(coef[j % 2], coef[j % 2], at(arena, it * 4 * SEQ + j * SEQ, SEQ), ALU.mult).then_inc(coef_ready, 1)

            def coef_low_part(j, it=0):
                v.wait_ge(coef_high, it * 4 + (j + 1))
                low_of(chunk_of(yl, j % 2), coef[j % 2], chunk_of(yh, j % 2)).then_inc(coef_low, 1)

            def expert_step(j, it):
                if j + 2 < NKEYS:
                    weigh(j + 2, it)
                ahead(piece_v(j, it))
                if j + 2 < NKEYS:
                    coef_low_part(j + 2, it)
                if j + 3 < NKEYS:
                    ahead(piece_u(j + 3, it))

            v.wait_ge(w_written, SEQ // 4)
            weigh(0)
            weigh(1)
            take_low(piece_v(0))
            coef_low_part(0)
            coef_low_part(1)
            for j in range(3):
                ahead(piece_u(j))
            expert_step(0, 0)
            expert_steps(v, expert_step)
            v.wait_ge(h_back_loaded, 16)
            for n in range(4):
                cs = slice(n * HALF, (n + 1) * HALF)
                ins = v.tensor_tensor(h_tok[:, cs], h_back[:, cs], bank(n), ALU.add)
            ins.then_inc(h_ready, 1)
            variance(2, EPS_RMS)
            v.wait_ge(rows_loaded, 16)
            for b in range(TB):
                h = h_tok[:, b * D:(b + 1) * D]
                ins = v.scalar_tensor_tensor(out=h, in0=h, scalar=rstd[:, b:b + 1], in1=rows[:, 0:D], op0=ALU.mult, op1=ALU.mult)
            ins.then_inc(normed, 1)
            evacuate_turned(2)
            v.wait_ge(pos_loaded, 16)
            v.wait_ge(consts_loaded, 16)
            ang, flip = angles[:, SEQ:], angles[:, 0:SEQ]
            link(v.tensor_copy(ang, rope[:, 0:SEQ].bitcast(I32)))
            link(v.tensor_scalar(ang, ang, freq, None, ALU.mult))
            link(v.tensor_scalar(turns, ang, 1.0 / (2.0 * math.pi), ROUND, ALU.mult, ALU.add))
            link(v.tensor_scalar(turns, turns, -ROUND, None, ALU.add))
            for c in TWO_PI_PARTS:
                link(v.scalar_tensor_tensor(out=ang, in0=turns, scalar=-c, in1=ang, op0=ALU.mult, op1=ALU.add))
            link(v.tensor_scalar(ang, ang, 3.1415925, -3.1415925, ALU.min, ALU.max))
            link(v.scalar_tensor_tensor(out=flip, in0=ang, scalar=-1.0, in1=ang, op0=ALU.mult, op1=ALU.max))
            v.tensor_scalar(flip, flip, -1.0, math.pi / 2.0, ALU.mult, ALU.add).then_inc(angle_ready, 1)

            rope2 = [rope[:, n * SEQ:(n + 1) * SEQ].unsqueeze(1).to_broadcast([PARTS, 2, SEQ]) for n in range(2)]

            def attention(kind, s):
                for k in range(KC):
                    ahead(Piece(f"{kind}_v", k))
                if kind == "diff":
                    v.wait_ge(mask_loaded, 16)
                if kind == "fox":
                    ahead(Piece("fox_f", 0))
                    fz, t2, c16 = (part(14592 + 256 * n, SEQ)[0:16, :] for n in range(3))
                    t3 = part(15360, SEQ)[0:16, :]
                    v.wait_ge(slot_done[Piece("fox_f", 0).slot], Piece("fox_f", 0).count)
                    v.wait_ge(bias_loaded, 16)
                    v.wait_ge(pool_ready, 2)
                    link(v.tensor_scalar(fz, bank(7, 0, SEQ)[0:16, :], fbias[0:16, :], None, ALU.add))
                    v.scalar_tensor_tensor(out=fz_e, in0=fz, scalar=-1.0, in1=fz, op0=ALU.mult, op1=ALU.max).then_inc(fz_ready, 1)
                    v.wait_ge(fexp_ready, 1)
                    log1p_of_exp(c16, fz_e, (t2, t3))
                    link(v.tensor_scalar(fz, fz, 0.0, None, ALU.min))
                    link(v.tensor_tensor(fz, fz, c16, ALU.subtract))
                    link(v.tensor_tensor_scan(c16, ones256[0:16, :], fz, 0.0, ALU.mult, ALU.add))
                    link(v.tensor_scalar(c16, c16, -1.0 / SCALE, None, ALU.mult))
                    link(v.memset(bias_rows, 0.0))
                    b3 = bias_rows[0:16, :].rearrange("p (h t) -> p h t", h=16)
                    v.tensor_tensor(b3, c16.unsqueeze(1).to_broadcast([16, 16, SEQ]),
                                    head_sel[0:16, :].unsqueeze(2).to_broadcast([16, 16, SEQ]), ALU.mult).then_inc(bias_ready, 1)

                def rotary(it, e):
                    v.wait_ge(s["rotated"], it * 2 + (e + 1))
                    if not opening(it):
                        v.wait_ge(s["scores_done"], it * 2 + (e - 1))
                    three = lambda t: t.rearrange("p (n t) -> p n t", n=2)
                    v.tensor_tensor(three(rot), three(bank(5)), rope2[1], ALU.mult)
                    link(v.tensor_tensor(three(qkr[e]), three(qk[e]), rope2[0], ALU.mult))
                    v.tensor_tensor(qkr[e], qkr[e], rot, ALU.add).then_inc(s["rope_done"], 1)

                def pair(it, e, last=False):
                    n1 = it * 2 + (e + 1)
                    v.wait_ge(s["scores_done"], n1)
                    for m in range(2):
                        ins = v.tensor_tensor(sm[:, m * HALF:(m + 1) * HALF], bank(2 * e + m), mask, ALU.add)
                    link(ins)
                    link(v.tensor_reduce(mx4, sm.rearrange("p (m k) -> p m k", m=4), AX.X, ALU.max))
                    v.tensor_scalar(nb4, mx4, -SCALE, None, ALU.mult).then_inc(s["max_ready"], 1)
                    for n in range(2):
                        ahead(Piece(f"{kind}_qk", 2 * e + n, it, 4))
                    if kind == "diff":
                        v.wait_ge(s["probs_ready"], n1)
                        link(v.reciprocal(rl4, l4))
                        v.tensor_scalar(rl2, rl4[:, 2:4], nlam, None, ALU.mult)
                        for t in range(TB):
                            ins = v.tensor_scalar(att[:, t * SEQ:(t + 1) * SEQ], pr[:, t * SEQ:(t + 1) * SEQ],
                                                  rl4[:, t:t + 1], None, ALU.mult)
                        link(ins)
                        for t in range(TB):
                            a_t = att[:, t * SEQ:(t + 1) * SEQ]
                            ins = v.scalar_tensor_tensor(out=a_t, in0=pr[:, HALF + t * SEQ:HALF + (t + 1) * SEQ],
                                                         scalar=rl2[:, t:t + 1], in1=a_t, op0=ALU.mult, op1=ALU.add)
                        ins.then_inc(s["mixed_ready"], 1)
                        if not last:
                            rotary(*following(it, e))
                        v.wait_ge(s["osq_ready"], n1)
                        v.tensor_scalar(ovar, osq, 1.0 / PARTS, EPS_RMS, ALU.mult, ALU.add).then_inc(s["ovar_ready"], 1)
                        v.wait_ge(s["orstd_ready"], n1)
                        for t in range(TB):
                            ins = v.scalar_tensor_tensor(out=at(o_tok, it * 2 * PARTS + (t * D + e * PARTS), PARTS),
                                                         in0=bank(7, t * PARTS, PARTS), scalar=orstd[:, t:t + 1],
                                                         in1=subln[:, :], op0=ALU.mult, op1=ALU.mult)
                        ins.then_inc(s["o_ready"], 1)
                    else:
                        v.wait_ge(s["probs_ready"], n1)
                        link(v.reciprocal(rl4, l4))
                        v.wait_ge(s["pv_done"], n1)
                        for m in range(2):
                            for t in range(TB):
                                ins = v.tensor_scalar(at(o_tok, it * 4 * 64 + (t * D + (2 * e + m) * 64), 64),
                                                      bank(7, (2 * m + t) * 64, 64), rl4[:, 2 * m + t:2 * m + t + 1], None, ALU.mult)
                        ins.then_inc(s["o_ready"], 1)

                steps = 2 * (5 if kind == "diff" else 3)
                if kind == "diff":
                    v.wait_ge(rope_ready, 1)
                    rotary(0, 0)
                all_pairs(v, pair, chain=chain, steps=steps, last_steps=steps - (1 if kind == "diff" else 0))

            def ffn(l):
                s = ffn_sems[l]

                def hidden(n, it=0):
                    e = n % 2
                    gate = bank(4 + 2 * e, 0, SEQ)
                    p = fpst[e]
                    link(v.tensor_copy(p, at(ffn_params, it * 16 + (l * FF_CHUNKS + n) * 4, 4)))
                    v.wait_ge(slot_done[piece_gate(l, n, it).slot], piece_gate(l, n, it).count)
                    link(v.tensor_scalar(conv[e], gate, p[:, 2:3], p[:, 3:4], ALU.mult, ALU.add))
                    for k in (1, 2):
                        ins = v.scalar_tensor_tensor(out=conv[e][:, k:], in0=gate[:, :SEQ - k], scalar=p[:, 2 - k:3 - k],
                                                     in1=conv[e][:, k:], op0=ALU.mult, op1=ALU.add)
                        if k == 1:
                            link(ins)
                    ins.then_inc(s["conv_ready"], 1)
                    ahead(piece_gate(l, n, it))
                    v.wait_ge(s["silu_ready"], it * 4 + (n + 1))
                    v.wait_ge(slot_done[piece_up(l, n, it).slot], piece_up(l, n, it).count)
                    v.tensor_tensor(hid[e], act[e], bank(5 + 2 * e, 0, SEQ), ALU.mult).then_inc(s["hid_ready"], 1)
                    ahead(piece_up(l, n, it))
                    v.wait_ge(s["hid_high"], it * 4 + (n + 1))
                    low_of(chunk_of(yl, e), hid[e], chunk_of(yh, e)).then_inc(s["hid_low"], 1)

                def step(n, it):
                    if n + 1 < FF_CHUNKS:
                        hidden(n + 1, it)
                    ahead(piece_out(l, n, it))

                hidden(0)
                ffn_steps(v, step, chain, 3)

            def output(kind, k_turn):
                evacuate_turned(k_turn)
                for k in range(KC):
                    ahead(Piece(f"{kind}_out", k))

            attention("diff", att_sems[0])
            output("diff", 3)
            layer_norm(3, Piece("diff_out", KC - 1))
            evacuate_turned(4)
            ffn(0)
            layer_norm(4, piece_out(0, FF_CHUNKS - 1))
            evacuate_turned(5)
            attention("fox", att_sems[1])
            output("fox", 6)
            layer_norm(5, Piece("fox_out", KC - 1))
            evacuate_turned(7)
            ffn(1)
            layer_norm(6, piece_out(1, FF_CHUNKS - 1))


def _in_pieces(w):
    n = w.shape[1] // PARTS
    return w.reshape(KC, PARTS, n, PARTS).transpose(2, 1, 0, 3).reshape(n, PARTS, D)


def _by_feature(v):
    v = v.reshape(-1, v.shape[-1] // PARTS, PARTS)
    return v.transpose(2, 1, 0)


def _constants():
    c = np.zeros((PARTS, NCONST), np.float32)
    c[:, IDENT:IDENT + PARTS] = np.eye(PARTS)
    for m in range(PARTS):
        d = m % 64
        if d < 8:
            c[m + 8, PERM + m] = -1.0
        elif d < 16:
            c[m - 8, PERM + m] = 1.0
    c[:, IOTA:IOTA + PARTS] = np.arange(PARTS)
    inv = np.float32(500000.0) ** (-np.arange(0, 16, 2, dtype=np.float32) / np.float32(16))
    d = np.arange(PARTS) % 64
    c[:, FREQ] = np.where(d < 16, inv[d % 8], 0.0)
    c[:16, HSEL:HSEL + 16] = np.eye(16)
    return c


def _causal_mask():
    q, k = np.arange(PARTS)[:, None], np.arange(SEQ)[None]
    return np.concatenate([np.where(k <= q + b * PARTS, 0.0, MASKED) for b in range(TB)], 1).astype(np.float32)


def kernel(**inputs):
    import concourse.bacc as bacc
    from concourse.bass_utils import run_bass_kernel_spmd

    g = {k: np.asarray(v) for k, v in inputs.items()}
    f = np.ascontiguousarray
    w_in = g["w_in"][0].reshape(KC, PARTS, 7, KC, PARTS).transpose(2, 3, 1, 0, 4).reshape(7, KC, PARTS, D)
    w_in = w_in[[0, 2, 4, 3, 1, 5, 6]]
    params = np.zeros((PARTS, KC, NP), np.float32)
    for lo, name in ((G1, "norm1_g"), (CA, "conv_a_w"), (CAB, "conv_a_b"), (BA, "b_a"), (BX, "b_x"),
                     (LAM, "lru_lambda"), (CB, "conv_b_w"), (G2, "norm2_g")):
        v = _by_feature(g[name][0])
        params[:, :, lo:lo + v.shape[2]] = v
    ffn_params = np.stack([_by_feature(np.concatenate([g["ffn_conv_w_2"][l], g["ffn_conv_b_2"][l][None]]))
                           for l in range(2)], 1)
    diff, fox = g["diff_w_qkv_2"][0], g["fox_w_in_2"][0]

    def qk_pieces(w):
        p = _in_pieces(w[:, :2 * D])
        return p.reshape(2, 8, PARTS, D).transpose(1, 0, 2, 3).reshape(16, PARTS, D)

    ffn_in = []
    for l in range(2):
        p = _in_pieces(g["ffn_w_in_2"][l])
        ffn_in.append(p.reshape(2, FF_CHUNKS, PARTS, D).transpose(1, 0, 2, 3).reshape(2 * FF_CHUNKS, PARTS, D))
    arrays = {
        "x": g["x"][0].reshape(TB, PARTS, D).transpose(1, 0, 2),
        "w_mix": w_in,
        "w_gate": np.concatenate([g["w_a"][0], g["w_x"][0]], axis=2),
        "w_out": g["w_out"][0].reshape(KC, PARTS, D),
        "w_query": _in_pieces(g["peer_wq"][0]),
        "keys": g["peer_subkeys"][0].transpose(3, 0, 1, 2).reshape(PARTS, 16 * PARTS),
        "u_tab": g["peer_u"][0].reshape(PARTS, PARTS, KC, PARTS).transpose(1, 3, 2, 0).reshape(PARTS, PARTS, D),
        "v_tab": g["peer_v"][0].reshape(PARTS, PARTS, D).transpose(1, 0, 2),
        "diff_qk": qk_pieces(diff),
        "diff_v": diff[:, 2 * D:].reshape(KC, PARTS, D),
        "diff_out": g["diff_w_o_2"][0].reshape(KC, PARTS, D),
        "fox_qk": qk_pieces(fox),
        "fox_v": fox[:, 2 * D:3 * D].reshape(KC, PARTS, D),
        "fox_f": _in_pieces(np.pad(fox[:, 3 * D:], ((0, 0), (0, PARTS - 16))))[0],
        "fox_out": g["fox_w_o_2"][0].reshape(KC, PARTS, D),
        "mask": _causal_mask(),
        "ffn_in": np.stack(ffn_in),
        "ffn_out": g["ffn_w_out_2"].reshape(2, FF_CHUNKS, PARTS, D),
        "consts": _constants(),
        "params": params.reshape(PARTS, KC * NP),
        "ffn_params": ffn_params.reshape(PARTS, 2 * FF_CHUNKS * 4),
        "rows": np.stack([g["final_g"]] + [g[f"{n}_2"][l] for l in range(2) for n in ("ln1_g", "ln1_b", "ln2_g", "ln2_b")]),
        "subln": g["diff_subln_g_2"],
        "lambdas": np.stack([g[f"diff_lambda_{n}_2"][0] for n in ("q1", "k1", "q2", "k2")]).reshape(1, 256),
        "forget_bias": g["fox_b_f_2"].reshape(16, 1),
        "positions": g["positions_2"].astype(np.int32),
    }
    nc = bacc.Bacc("TRN2", target_bir_lowering=False, num_devices=1)
    arrays = {f"in_{k}": f(v) for k, v in arrays.items()}
    args = [nc.dram_tensor(k, v.shape, mybir.dt.from_np(v.dtype), kind="ExternalInput").ap() for k, v in arrays.items()]
    out = nc.dram_tensor("out", (PARTS, TB, D), F32, kind="ExternalOutput").ap()
    h_saved = nc.dram_tensor("h_saved", (PARTS, TB * D), F32, kind="Internal").ap()
    build(nc, *args, h_saved, out)
    r = run_bass_kernel_spmd(nc, [arrays], core_ids=[0])
    got = r.results[0]["out"]
    return np.ascontiguousarray(got.transpose(1, 0, 2).reshape(1, SEQ, D))
```

```python
import math
from contextlib import ExitStack

import numpy as np

import concourse.bass as bass
from concourse import mybir

F32 = mybir.dt.float32
F32R = mybir.dt.float32r
I32 = mybir.dt.int32
U32 = mybir.dt.uint32
ALU = mybir.AluOpType
ACT = mybir.ActivationFunctionType
AX = mybir.AxisListType

SEQ, D = 256, 1024
PARTS = 128
TB = SEQ // PARTS
KC = D // PARTS
HALF = 512
EPS_RMS, EPS_LN = 1e-6, 1e-5
MIX_GROUPS = 7
HEADS, NKEYS = 8, 128
D_FF = 2816
FF_CHUNKS = D_FF // PARTS
ALPHA = 4 ** 0.25
LAMBDA_INIT = 0.8 - 0.6 * math.exp(0.0)
SCALE = 64 ** -0.5
MASKED = -1e30
GELU_C, GELU_A = math.sqrt(2.0 / math.pi), 0.044715
TWO_PI_PARTS = (6.28125, 0.0019350051879882812, 3.019916050561733e-07)
ROUND = 1.5 * 2.0 ** 23
G1, CA, CAB, BA, BX, LAM, CB, G2, SP4, NSP4, HBA, HBX = 0, 1, 5, 6, 7, 8, 9, 12, 13, 14, 15, 16
NP = 17
IDENT, PERM, IOTA, FREQ, HSEL = 0, 128, 256, 384, 385
NCONST = 401
EARLY_OF_ROUND = (4, 4, 4, 12)
EARLY = sum(EARLY_OF_ROUND)
LATE = NKEYS - EARLY
ARENA = 32768


class Chain:

    def __init__(self, eng, sem):
        self.eng, self.sem, self.base, self.n = eng, sem, 0, 0
        self.it, self.per = None, 0

    def enter(self, it, per, rounds_before=0):
        self.it, self.per = it, per
        self.start, self.first = self.base + self.n, rounds_before
        self.base, self.n = self.start, 0

    def leave(self, rounds):
        assert self.n == self.per, (self.n, self.per)
        self.base, self.n, self.it = self.start + rounds * self.per, 0, None

    def step(self, ins):
        ins.then_inc(self.sem, 1)
        self.n += 1
        return ins

    def wait(self):
        if self.it is None:
            self.eng.wait_ge(self.sem, self.base + self.n)
        else:
            self.eng.wait_ge(self.sem, (self.it - self.first) * self.per + (self.base + self.n))

    def link(self, ins):
        self.step(ins)
        self.wait()


STREAM = [("mix", 8 * KC), ("mix_out", KC), ("query", 16), ("expert", NKEYS + LATE),
          ("diff_v", KC), ("diff_qk", 16), ("diff_out", KC), ("ffn0", 3 * FF_CHUNKS),
          ("fox_f", 1), ("fox_v", KC), ("fox_qk", 16), ("fox_out", KC), ("ffn1", 3 * FF_CHUNKS)]
TOTAL = sum(n for _, n in STREAM)
RING = 4


def start_of(phase):
    count = 0
    for name, n in STREAM:
        if name == phase:
            return count
        count += n
    raise KeyError(phase)


class Piece:

    def __init__(self, phase, k, it=0, per=0):
        assert per % RING == 0 or isinstance(it, int)
        self.n = (start_of(phase) if phase else 0) + k
        self.it, self.per = it, per
        if isinstance(it, int):
            self.n, self.it, self.per = self.n + it * per, 0, 0

    @property
    def slot(self):
        return self.n % RING

    @property
    def before(self):
        return self.n // RING if isinstance(self.it, int) else self.it * (self.per // RING) + self.n // RING

    @property
    def count(self):
        return self.n // RING + 1 if isinstance(self.it, int) else self.it * (self.per // RING) + (self.n // RING + 1)

    @property
    def loads(self):
        return 16 * self.count if isinstance(self.it, int) else self.it * (16 * self.per // RING) + 16 * (self.n // RING + 1)

    def later(self, k):
        p = Piece(None, 0)
        p.n, p.it, p.per = self.n + k, self.it, self.per
        return p


def piece_u(j, it=0):
    return Piece("expert", j if j < 3 else 2 * j - 2, it, 8)


def piece_v(j, it=0):
    return Piece("expert", 2 * j + 3, it, 8) if j < LATE - 3 else Piece("expert", j + LATE, it, 4)


def piece_gate(l, n, it=0):
    return Piece(f"ffn{l}", 3 * n - 1 if n else 0, it, 12)


def piece_up(l, n, it=0):
    return Piece(f"ffn{l}", 3 * n if n else 1, it, 12)


def piece_out(l, n, it=0):
    return Piece(f"ffn{l}", 3 * n + 4 if n < FF_CHUNKS - 1 else 3 * n + 2, it, 12)


def build(nc, x, w_mix, w_gate, w_out, w_query, keys, u_tab, v_tab, diff_qk, diff_v, diff_out,
          fox_qk, fox_v, fox_f, fox_out, mask_in, ffn_in, ffn_out, consts_in, params_in, ffn_params_in,
          rows_in, subln_in, lambdas_in, forget_bias_in, positions_in, h_saved, out):
    ctx = ExitStack()
    with ctx:
        def sb(name, shape, dt=F32):
            return ctx.enter_context(nc.sbuf_tensor(name, shape, dt))

        def sem(name):
            return ctx.enter_context(nc.semaphore(name))

        raw = sb("raw", [PARTS, RING * D])
        high = sb("high", [PARTS, RING * D], F32R)
        low = sb("low", [PARTS, RING * D], F32R)
        h_tok = sb("h_tok", [PARTS, TB * D])
        xh = sb("xh", [PARTS, KC * SEQ], F32R)
        xl = sb("xl", [PARTS, KC * SEQ], F32R)
        yh = sb("yh", [PARTS, 2 * SEQ], F32R)
        yl = sb("yl", [PARTS, 2 * SEQ], F32R)
        consts = sb("consts", [PARTS, NCONST])
        params = sb("params", [PARTS, KC * NP])
        ffn_params = sb("ffn_params", [PARTS, 2 * FF_CHUNKS * 4])
        subln = sb("subln", [PARTS, PARTS])
        stats = sb("stats", [PARTS, 64])
        arena = sb("arena", [PARTS, ARENA])
        ps = ctx.enter_context(nc.psum_tensor("ps", [PARTS, 8 * HALF], F32))

        def bank(b, lo=0, n=HALF):
            return ps[:, b * HALF + lo:b * HALF + lo + n]

        def cols(t, p, lo=0, n=D):
            return t[:, p.slot * D + lo:p.slot * D + lo + n]

        def part(lo, n):
            return arena[:, lo:lo + n]

        def at(t, start, n):
            return t[:, bass.ds(start, n)]

        def chunk_of(t, k):
            return t[:, k * SEQ:(k + 1) * SEQ]

        def weights_of(token, j, j_end):
            return arena[:, :].rearrange("p (j t) -> p j t", t=SEQ)[:, j:j_end, bass.ds(token, 4)].rearrange("p j t -> p t j")

        def coefficients(j, it):
            return coef[j % 2] if j < LATE else at(arena, it * (4 * SEQ) + j * SEQ, SEQ)

        def act_tokens(g):
            return (3,) if g % 2 == 0 else (2, 3)

        def scattered(g):
            return bank(g).rearrange("p (t j) -> p t j", t=4)

        def turned_part(t, n):
            return t[:, :].rearrange("p (c t) -> p c t", c=KC)[:, 4 * (n % 2):4 * (n % 2) + 4, n // 2 * PARTS:(n // 2 + 1) * PARTS]

        ident = consts[:, IDENT:IDENT + PARTS]
        perm = consts[:, PERM:PERM + PARTS]
        iota = consts[:, IOTA:IOTA + PARTS]
        freq = consts[:, FREQ:FREQ + 1]
        head_sel = consts[:, HSEL:HSEL + 16]

        one_hot = [h_tok[:, 512 * n:512 * n + 512] for n in range(2)]
        one_hot_w = [h_tok[:, 1024 + 512 * n:1536 + 512 * n] for n in range(2)]
        coef = [h_tok[:, SEQ * n:SEQ * n + SEQ] for n in range(2)]
        chosen = raw[:, 2 * D:2 * D + 3 * SEQ]
        minus_weight = raw[:, 2 * D + 3 * SEQ:3 * D]
        distance = [ps[:, 7 * HALF + PARTS * n:7 * HALF + PARTS * (n + 1)] for n in range(4)]
        tmp = part(18944, TB * D)
        rows = part(20992, 2 * D)
        mask = part(23040, 512)
        ones256 = part(23552, SEQ)
        ones = part(23552, PARTS)
        rope = part(23808, 2 * SEQ)
        h_back = part(24320, TB * D)
        angles = part(26368, 2 * SEQ)
        turns = part(26880, SEQ)
        lambdas = part(27136, 4 * 64)
        lam_prod = part(27392, 128)
        M_OUT = 0
        gate_a, gate_b, decay, ix, msq, root = (part(2048 + 256 * n, 256) for n in range(6))
        mx = 10240
        xc = part(mx, 256)
        vb_sb, cv, yb, ybb, sq, inner, tg, gg = (part(mx + 256 * n, 256) for n in range(1, 9))
        tm = part(mx + 2304, 512)
        tr, ti, tt, t1 = (part(mx + 2816 + 256 * n, 256) for n in range(4))
        pst = part(mx + 4096, NP)
        small = [part(mx + 4200 + 8 * n, KC) for n in range(5)]
        keysT = part(15360, 16 * PARTS)
        qs = part(0, 4 * SEQ)
        sc = [part(1024 + 1024 * n, 1024) for n in range(2)]
        rest = part(3072, 1024)
        cand, cand2 = part(4096, 1024), part(5120, 1024)
        eqs = part(6144, 1024)
        top1, idxf = part(7168, 128), part(7296, 128)
        idxu = part(7424, 128).bitcast(U32)
        posu = part(7552, 64).bitcast(U32)
        digit = part(7616, 64).bitcast(U32)
        digitf = part(7680, 64)
        best = part(7744, 64)
        sel = part(7808, 3 * SEQ)
        expsum = part(8576, 32)
        early_u = [part(9216 + D * n, D) for n in range(4)]
        xf = part(13312, KC * SEQ)
        v_tok = part(0, TB * D)
        bias_rows = part(2048, 16 * SEQ)
        o_tok = part(6144, TB * D)
        qk = [part(8192 + 512 * n, 512) for n in range(2)]
        qkr = [part(9216 + 512 * n, 512) for n in range(2)]
        rot = part(10240, 512)
        sm = part(10752, 1024)
        pr = part(11776, 1024)
        pT = part(12800, 768)
        att = part(13568, 512)
        squares = part(14080, 2 * PARTS)
        fz_e = part(14336, SEQ)[0:16, :]
        conv = [part(0 + 256 * n, 256) for n in range(2)]
        act = [part(512 + 256 * n, 256) for n in range(2)]
        hid = [part(1024 + 256 * n, 256) for n in range(2)]
        fpst = [part(1536 + 4 * n, 4) for n in range(2)]
        fbias = stats[:, 44:45]
        halfpow = stats[:, 0:2]
        sumsq, var, rstd, negmean = (stats[:, 2 + 2 * n:4 + 2 * n] for n in range(4))
        sum4 = stats[:, 10:14]
        mx4, nb4, l4, rl4 = (stats[:, 14 + 4 * n:18 + 4 * n] for n in range(4))
        nlam = stats[:, 30:31]
        rl2 = stats[:, 32:34]
        lam2 = stats[:, 34:36]
        osq, ovar, orstd = (stats[:, 36 + 2 * n:38 + 2 * n] for n in range(3))
        halfpow2 = stats[:, 42:44]

        slot_loaded, slot_high, slot_low, slot_done = (
            [sem(f"slot_{what}{s}") for s in range(RING)] for what in ("loaded", "high", "low", "done"))
        x_loaded = [sem(f"x_loaded{b}") for b in range(TB)]
        ffn_params_loaded = sem("ffn_params_loaded")
        consts_loaded, small_loaded = sem("consts_loaded"), sem("small_loaded")
        keys_loaded, rows_loaded, pos_loaded = sem("keys_loaded"), sem("rows_loaded"), sem("pos_loaded")
        stored, bias_loaded, mask_loaded = sem("stored"), sem("bias_loaded"), sem("mask_loaded")
        h_kept, h_back_loaded = sem("h_kept"), sem("h_back_loaded")
        turned_high, xc_high, merged_high, coef_high = (
            sem(n) for n in ("turned_high", "xc_high", "merged_high", "coef_high"))
        xc_low, merged_low, coef_low = (sem(n) for n in ("xc_low", "merged_low", "coef_low"))
        dve_steps, act_steps = sem("dve_steps"), sem("act_steps")
        pool_ready = sem("pool_ready")
        h_ready, sumsq_ready, var_ready, rstd_ready = (sem(n) for n in ("h_ready", "sumsq_ready", "var_ready", "rstd_ready"))
        first_tile_done = sem("first_tile_done")
        normed, turned, xT_ready = sem("normed"), sem("turned"), sem("xT_ready")
        lam_neg, lam_exp = sem("lam_neg"), sem("lam_exp")
        pst_ready, xc_ready, vb_ready, cv_done = (sem(n) for n in ("pst_ready", "xc_ready", "vb_ready", "cv_done"))
        bb_used, sq_ready, inner_ready, tg_ready = (sem(n) for n in ("bb_used", "sq_ready", "inner_ready", "tg_ready"))
        ga_used, tm_ready, tm_used, ri_ready = (sem(n) for n in ("ga_used", "tm_ready", "tm_used", "ri_ready"))
        tt_ready, decay_ready, m_ready, root_ready = (sem(n) for n in ("tt_ready", "decay_ready", "m_ready", "root_ready"))
        merged_ready = sem("merged_ready")
        q_ready, score_done, sc_ready, sc_used = (sem(n) for n in ("q_ready", "score_done", "sc_ready", "sc_used"))
        shifted_ready, exp_ready, sel_ready, sel_turned, chosen_ready = (
            sem(n) for n in ("shifted_ready", "exp_ready", "sel_ready", "sel_turned", "chosen_ready"))
        one_hots_ready, act_one_hots_ready = sem("one_hots_ready"), sem("act_one_hots_ready")
        distance_ready, scat_done, w_written = sem("distance_ready"), sem("scat_done"), sem("w_written")
        gelu_ready, coef_ready = sem("gelu_ready"), sem("coef_ready")
        xf_ready, early_done, early_gelu, early_weighed = (
            sem(n) for n in ("xf_ready", "early_done", "early_gelu", "early_weighed"))
        early_loaded = [sem(f"early_loaded{n}") for n in range(4)]
        angle_ready, rope_ready, lamdot_ready, lamexp_ready = (
            sem(n) for n in ("angle_ready", "rope_ready", "lamdot_ready", "lamexp_ready"))
        att_sems = []
        for kind in ("diff", "fox"):
            att_sems.append({n: sem(f"{kind}_{n}") for n in (
                "v_ready", "qk_ready", "rotated", "rope_done", "scores_done", "max_ready", "probs_ready",
                "mixed_ready", "turned", "turned_ready", "pv_done", "osq_ready", "ovar_ready",
                "orstd_ready", "o_ready", "masked")})
        fz_ready, fexp_ready, bias_ready = (sem(n) for n in ("fz_ready", "fexp_ready", "bias_ready"))
        ffn_sems = [{n: sem(f"ffn{l}_{n}") for n in ("conv_ready", "silu_ready", "hid_ready", "hid_high", "hid_low")} for l in range(2)]
        block = ctx.enter_context(nc.Block())

        def rounds(eng, n, body):
            body(0)
            with eng.Fori(1, n) as it:
                body(it)

        def opening(it):
            return isinstance(it, int) and it == 0

        def following(it, e):
            return (it, 1) if e == 0 else (it + 1, 0)

        GROUP_BANKS = (4, 0, 1, 4)

        def two_left(it):
            return not (isinstance(it, int) and it == HEADS // 2 - 1)

        def all_pairs(eng, body, n=4, chain=None, steps=0):
            body(0, 0)
            body(0, 1)
            with eng.Fori(1, n - 1) as it:
                if chain:
                    chain.enter(it, steps, 1)
                body(it, 0)
                body(it, 1)
            if chain:
                chain.leave(n - 2)
            body(n - 1, 0)
            body(n - 1, 1, last=True)

        def expert_steps(eng, step):
            step(0, 0)
            with eng.Fori(0, (LATE - 4) // 4) as it:
                for j in range(1, 5):
                    step(j, it)
            step(LATE - 3, 0)
            with eng.Fori(0, EARLY // 4) as it:
                for j in range(LATE - 2, LATE + 2):
                    step(j, it)
            for j in range(NKEYS - 2, NKEYS):
                step(j, 0)

        def ffn_steps(eng, step, chain=None, steps=0):
            step(0, 0)
            with eng.Fori(0, 4) as it:
                if chain:
                    chain.enter(it, 4 * steps)
                for n in range(1, 5):
                    step(n, it)
            if chain:
                chain.leave(4)
            for n in range(17, FF_CHUNKS):
                step(n, 0)

        @block.sync
        def _(sp):
            def load(p, src, n=D):
                if not (isinstance(p.before, int) and p.before == 0):
                    sp.wait_ge(slot_low[p.slot], p.before)
                sp.dma_start(cols(raw, p, 0, n), src).then_inc(slot_loaded[p.slot], 16)

            def pick(t, i):
                return t[i] if isinstance(i, int) else t[bass.ds(i, 1)].rearrange("o p n -> (o p) n")

            def mix_round(c):
                for g in range(MIX_GROUPS):
                    if opening(c) and g == 2:
                        sp.dma_start(params[:, :], params_in).then_inc(small_loaded, 16)
                        sp.dma_start(lambdas, lambdas_in.partition_broadcast(PARTS)).then_inc(small_loaded, 16)
                        sp.dma_start(subln[:, :], subln_in.partition_broadcast(PARTS)).then_inc(small_loaded, 16)
                    load(Piece("mix", g, c, 8), pick(w_mix[g], c))
                load(Piece("mix", 7, c, 8), pick(w_gate, c), 2 * PARTS)

            sp.dma_start(h_tok[:, D:2 * D], x[:, 1, :]).then_inc(x_loaded[1], 16)
            rounds(sp, KC, mix_round)
            sp.dma_start(ffn_params[:, :], ffn_params_in).then_inc(ffn_params_loaded, 16)
            sp.dma_start(keysT, keys).then_inc(keys_loaded, 16)
            for k in range(KC):
                load(Piece("mix_out", k), w_out[k])
            p = 0
            for it, early in enumerate(EARLY_OF_ROUND):
                for q in range(4 * it, 4 * it + 4):
                    load(Piece("query", q), w_query[q])
                if it == 3:
                    for j in range(3):
                        load(piece_u(j), u_tab[j])
                if it == 0:
                    sp.wait_ge(merged_ready, KC)
                for p in range(p, p + early):
                    if p >= 4:
                        sp.wait_ge(early_done, p - 3)
                    sp.dma_start(early_u[p % 4], u_tab[LATE + p]).then_inc(early_loaded[p % 4], 16)
                p += 1
                if it == 0:
                    sp.wait_ge(h_ready, TB)
                    sp.dma_start(h_saved, h_tok[:, :]).then_inc(h_kept, 16)
            def expert_step(j, it):
                if j == NKEYS - 2:
                    sp.wait_ge(coef_low, LATE)
                    sp.wait_ge(h_kept, 16)
                    sp.dma_start(h_back, h_saved).then_inc(h_back_loaded, 16)
                    sp.dma_start(rope[:, 0:SEQ].bitcast(I32), positions_in.partition_broadcast(PARTS)).then_inc(pos_loaded, 16)
                    sp.dma_start(mask, mask_in).then_inc(mask_loaded, 16)
                load(piece_v(j, it), pick(v_tab, it * 4 + j))
                if j < LATE - 3:
                    load(piece_u(j + 3, it), pick(u_tab, it * 4 + (j + 3)))
                if opening(it) and j == 0:
                    sp.wait_ge(one_hots_ready, SEQ // 4)
                    sp.wait_ge(act_one_hots_ready, SEQ // 4)

            expert_steps(sp, expert_step)

            def attention_weights(kind, v_src, qk_src, out_src):
                if kind == "fox":
                    load(Piece("fox_f", 0), fox_f)
                for k in range(KC):
                    load(Piece(f"{kind}_v", k), v_src[k])
                with sp.Fori(0, 4) as it:
                    for n in range(4):
                        load(Piece(f"{kind}_qk", n, it, 4), pick(qk_src, it * 4 + n))
                for k in range(KC):
                    load(Piece(f"{kind}_out", k), out_src[k])

            def ffn_weights(l):
                def step(n, it):
                    if n < FF_CHUNKS - 1:
                        load(piece_gate(l, n + 1, it), pick(ffn_in[l], it * 8 + (2 * n + 2)))
                        load(piece_up(l, n + 1, it), pick(ffn_in[l], it * 8 + (2 * n + 3)))
                    load(piece_out(l, n, it), pick(ffn_out[l], it * 4 + n))

                load(piece_gate(l, 0), ffn_in[l][0])
                load(piece_up(l, 0), ffn_in[l][1])
                ffn_steps(sp, step)

            attention_weights("diff", diff_v, diff_qk, diff_out)
            ffn_weights(0)
            attention_weights("fox", fox_v, fox_qk, fox_out)
            ffn_weights(1)
            for b in range(TB):
                sp.wait_ge(normed, 6 * TB + b + 1)
                sp.dma_start(out[:, b, :], h_tok[:, b * D:(b + 1) * D]).then_inc(stored, 16)
            sp.wait_ge(stored, 16 * TB)

        @block.gpsimd
        def _(pool):
            pool.memset(stats[:, :], -0.5).then_inc(pool_ready, 1)

            def inverse_roots(first, last):
                for n in range(TB * first, TB * last):
                    b = slice(n % TB, n % TB + 1)
                    pool.wait_ge(var_ready, n + 1)
                    pool.tensor_tensor(rstd[:, b], var[:, b], halfpow[:, b], ALU.pow).then_inc(rstd_ready, 1)

            pool.wait_ge(pool_ready, 1)
            inverse_roots(0, 3)
            pool.memset(ones256, 1.0).then_inc(pool_ready, 1)
            s = att_sems[0]
            with pool.Fori(0, HEADS) as it:
                pool.wait_ge(s["ovar_ready"], it + 1)
                pool.tensor_tensor(orstd, ovar, halfpow2, ALU.pow).then_inc(s["orstd_ready"], 1)
            inverse_roots(3, 4)
            pool.memset(bias_rows, 0.0).then_inc(pool_ready, 1)
            inverse_roots(4, 7)

        @block.scalar
        def _(a):
            chain = Chain(a, act_steps)
            a.dma_start(h_tok[:, 0:D], x[:, 0, :]).then_inc(x_loaded[0], 16)
            a.dma_start(consts[:, :], consts_in).then_inc(consts_loaded, 16)

            def load_rows(first, n):
                for r in range(n):
                    a.dma_start(rows[:, r * D:(r + 1) * D], rows_in[first + r:first + r + 1, :].partition_broadcast(PARTS)
                                ).then_inc(rows_loaded, 16)

            def sum_squares(k, centred):
                for b in range(TB):
                    if k >= 1:
                        a.wait_ge(h_ready, TB * (k - 1) + b + 1)
                    else:
                        a.wait_ge(x_loaded[b], 16)
                    bias = negmean[:, b:b + 1] if centred else 0.0
                    squares_of_h = tmp if k < 2 else part(15360, TB * D)
                    a.activation(squares_of_h[:, b * D:(b + 1) * D], h_tok[:, b * D:(b + 1) * D], ACT.Square,
                                 bias=bias, accum_out=sumsq[:, b:b + 1]).then_inc(sumsq_ready, 1)

            def take_high(p, n=D):
                a.wait_ge(slot_loaded[p.slot], p.loads)
                if not (isinstance(p.before, int) and p.before == 0):
                    a.wait_ge(slot_done[p.slot], p.before)
                a.activation(cols(high, p, 0, n), cols(raw, p, 0, n), ACT.Copy).then_inc(slot_high[p.slot], 1)

            def ahead(p, n=D):
                if p.n + RING < TOTAL:
                    take_high(p.later(RING), n)

            def evacuate_turned(k, gain=None):
                for n in range(4):
                    a.wait_ge(turned, 4 * k + n + 1)
                    if gain is None:
                        ins = a.activation(turned_part(xh, n), bank(n).rearrange("p (c t) -> p c t", c=4), ACT.Copy)
                    else:
                        for i in range(4):
                            c = 4 * (n % 2) + i
                            ins = a.activation(turned_part(xh, n)[:, i], bank(n, i * PARTS, PARTS), ACT.Copy,
                                               scale=params[:, c * NP + gain:c * NP + gain + 1])
                    ins.then_inc(turned_high, 1)

            a.wait_ge(pool_ready, 1)
            a.activation(stats[:, 60:61], stats[:, 61:62], ACT.Square)
            sum_squares(0, False)
            take_high(Piece("mix", 0))
            a.wait_ge(small_loaded, 16 * 3)
            evacuate_turned(0, G1)
            for n in range(1, RING):
                take_high(Piece("mix", n))
            a.wait_ge(lam_neg, 1)
            a.activation(part(mx + 4200, KC), part(mx + 4200, KC), ACT.Exp, scale=-1.0).then_inc(lam_exp, 1)
            a.wait_ge(lamdot_ready, 1)
            a.activation(lam2, lam2, ACT.Exp).then_inc(lamexp_ready, 1)

            def take_root(n):
                a.wait_ge(m_ready, n)
                a.activation(root, msq, ACT.Sqrt, scale=0.25).then_inc(root_ready, 1)

            def merged_high_part(c):
                a.wait_ge(merged_ready, c + 1)
                a.activation(chunk_of(xh, c), part(M_OUT + c * SEQ, SEQ), ACT.Copy).then_inc(merged_high, 1)

            def mix_round(c, last=False):
                later = not opening(c)
                piece = [Piece("mix", g, c, 8) for g in range(8)]
                for g in range(3):
                    ahead(piece[g])
                if later:
                    take_root(c)
                    a.wait_ge(cv_done, c)
                a.activation(vb_sb, bank(1, 0, SEQ), ACT.Copy).then_inc(vb_ready, 1)
                a.wait_ge(xc_ready, c + 1)
                if later:
                    a.wait_ge(slot_done[3], piece[7].later(-8).count)
                a.activation(chunk_of(yh, 0), xc, ACT.Copy).then_inc(xc_high, 1)
                ahead(piece[3], 2 * PARTS)
                ahead(piece[4])
                if later:
                    a.wait_ge(ga_used, c)
                a.activation(sq, bank(3, 0, SEQ), ACT.Square).then_inc(sq_ready, 1)
                ahead(piece[5])
                a.wait_ge(inner_ready, c + 1)
                a.activation(tg, inner, ACT.Tanh, scale=GELU_C).then_inc(tg_ready, 1)
                ahead(piece[6])
                if later:
                    a.wait_ge(tm_used, c)
                a.activation(tm, bank(4), ACT.Tanh, scale=0.5).then_inc(tm_ready, 1)
                if last:
                    for k in range(KC - 1):
                        merged_high_part(k)
                ahead(piece[7])
                a.wait_ge(pst_ready, c + 1)
                if later:
                    a.wait_ge(merged_ready, c)
                a.activation(tr, bank(5, 0, SEQ), ACT.Tanh, scale=0.5, bias=pst[:, HBA:HBA + 1])
                a.activation(ti, bank(5, SEQ, SEQ), ACT.Tanh, scale=0.5, bias=pst[:, HBX:HBX + 1]).then_inc(ri_ready, 1)
                a.wait_ge(ri_ready, c + 1)
                a.activation(tt, tr, ACT.Tanh, scale=pst[:, SP4:SP4 + 1], bias=pst[:, SP4:SP4 + 1]).then_inc(tt_ready, 1)
                a.activation(decay, tr, ACT.Exp, scale=pst[:, NSP4:NSP4 + 1],
                             bias=pst[:, NSP4:NSP4 + 1]).then_inc(decay_ready, 1)

            mix_round(0)
            with a.Fori(1, KC - 1) as it:
                mix_round(it)
            mix_round(KC - 1, last=True)
            take_root(KC)
            merged_high_part(KC - 1)
            for c in range(KC):
                ahead(Piece("mix_out", c))

            sum_squares(1, False)
            evacuate_turned(1, G2)
            early = 0
            for it in range(4):
                for q in range(4):
                    p = Piece("query", 4 * it + q)
                    a.wait_ge(slot_done[p.slot], p.count)
                    if it >= 1:
                        a.wait_ge(score_done, it)
                    a.activation(qs[:, q * SEQ:(q + 1) * SEQ], bank(4 + q, 0, SEQ), ACT.Copy).then_inc(q_ready, 1)
                    if 4 * it + q < 15:
                        ahead(p)
                a.wait_ge(score_done, it + 1)
                if it >= 2:
                    a.wait_ge(sc_used, it - 1)
                for b in range(TB):
                    ins = a.activation(sc[it % 2][:, b * HALF:(b + 1) * HALF], bank(2 * (it % 2) + b), ACT.Copy)
                ins.then_inc(sc_ready, 1)
                for early in range(early, early + EARLY_OF_ROUND[it]):
                    if early == EARLY - 4:
                        a.wait_ge(shifted_ready, 1)
                        a.activation(sel[:, 0:SEQ], sel[:, 0:SEQ], ACT.Exp).then_inc(exp_ready, 1)
                    a.wait_ge(early_done, early + 1)
                    a.activation(part((LATE + early) * SEQ, SEQ), bank(4 + early % 4, 0, SEQ), ACT.Gelu_apprx_tanh
                                 ).then_inc(early_gelu, 1)
                early += 1
            v0, u0 = piece_v(0), piece_u(0)
            take_high(v0)
            ahead(u0)
            for b in range(2):
                a.wait_ge(sel_turned, b + 1)
                n = (2 - b) * SEQ
                a.activation(chosen[:, b * HALF:b * HALF + n], bank(b, 0, n), ACT.Copy).then_inc(chosen_ready, 1)

            a.activation(minus_weight, bank(0, 0, SEQ), ACT.Copy, scale=-1.0).then_inc(chosen_ready, 1)
            a.wait_ge(chosen_ready, 3)

            def distances(token, g):
                for u in act_tokens(g):
                    ins = a.activation(distance[2 * (g % 2) + u - 2], iota, ACT.Abs, scale=-1.0,
                                       bias=at(chosen, token + (2 * SEQ + u), 1))
                ins.then_inc(distance_ready, 1)

            def act_one_hots(token, g, n):
                a.wait_ge(distance_ready, n)
                for u in act_tokens(g):
                    ins = a.activation(one_hot_w[g % 2][:, u * PARTS:(u + 1) * PARTS], distance[2 * (g % 2) + u - 2], ACT.Relu,
                                       scale=at(minus_weight, token + u, 1), bias=at(chosen, token + u, 1))
                ins.then_inc(act_one_hots_ready, 1)

            def scatter_round(it, last=False):
                for g in range(4):
                    if not (last and g >= 2):
                        distances(it * 16 + (4 * g + 8), g)
                    a.wait_ge(scat_done, it * 4 + (g + 1))
                    a.activation(weights_of(it * 16 + 4 * g, 0, LATE), scattered(g)[:, :, 0:LATE], ACT.Copy).then_inc(w_written, 1)
                    if not (last and g >= 2):
                        act_one_hots(it * 16 + (4 * g + 8), g, it * 4 + (g + 3))

            a.wait_ge(h_kept, 16)
            for g in range(2):
                distances(4 * g, g)
                act_one_hots(4 * g, g, g + 1)
            with a.Fori(0, SEQ // 16 - 1) as it:
                scatter_round(it)
            scatter_round(SEQ // 16 - 1, last=True)

            def gelu_block(j, it=0, first=False):
                p = piece_u(j, it)
                a.wait_ge(slot_done[p.slot], p.count)
                if not first:
                    a.wait_ge(coef_low, it * 4 + (j - 1))
                a.activation(coef[j % 2], bank(4 + j % 4, 0, SEQ), ACT.Gelu_apprx_tanh).then_inc(gelu_ready, 1)

            def coef_high_part(j, it=0, first=False):
                if j < LATE:
                    a.wait_ge(coef_ready, it * 4 + (j + 1))
                if not first:
                    p = piece_v(j - 2, it)
                    a.wait_ge(slot_done[p.slot], p.count)
                a.activation(chunk_of(yh, j % 2), coefficients(j, it), ACT.Copy).then_inc(coef_high, 1)

            def expert_step(j, it):
                if j + 2 < LATE:
                    gelu_block(j + 2, it)
                if j < LATE - 2:
                    ahead(piece_v(j, it))
                if j + 2 < NKEYS:
                    coef_high_part(j + 2, it)
                if j >= LATE - 2:
                    ahead(piece_v(j, it))
                if j + 3 < LATE:
                    ahead(piece_u(j + 3, it))

            a.wait_ge(scat_done, SEQ // 4)
            gelu_block(0, first=True)
            gelu_block(1, first=True)
            coef_high_part(0, first=True)
            coef_high_part(1, first=True)
            for j in (1, 2):
                ahead(piece_u(j))
            expert_steps(a, expert_step)
            load_rows(0, 1)
            a.dma_start(fbias[0:16, :], forget_bias_in).then_inc(bias_loaded, 16)

            sum_squares(2, False)
            evacuate_turned(2)
            load_rows(1, 2)
            a.wait_ge(angle_ready, 1)
            a.activation(rope, angles, ACT.Sin).then_inc(rope_ready, 1)

            def turned_group_high(k, g):
                a.wait_ge(turned, 4 * k + g + 1)
                a.activation(xh[:, g * HALF:(g + 1) * HALF], bank(GROUP_BANKS[g]), ACT.Copy).then_inc(turned_high, 1)

            def attention(kind, s, k_turn):
                if kind == "fox":
                    ahead(Piece("fox_f", 0))
                    a.wait_ge(fz_ready, 1)
                    a.activation(fz_e, fz_e, ACT.Exp, scale=-1.0).then_inc(fexp_ready, 1)
                for k in range(KC):
                    ahead(Piece(f"{kind}_v", k))
                for b in range(4):
                    ins = a.activation(v_tok[:, b * HALF:(b + 1) * HALF], bank(b), ACT.Copy)
                ins.then_inc(s["v_ready"], 1)

                def qk_out(it, e):
                    k_piece = Piece(f"{kind}_qk", 2 * e + 1, it, 4)
                    a.wait_ge(slot_done[k_piece.slot], k_piece.count)
                    if not opening(it):
                        a.wait_ge(s["rope_done" if kind == "diff" else "scores_done"], it * 2 + (e - 1))
                    a.activation(qk[e], bank(4), ACT.Copy).then_inc(s["qk_ready"], 1)

                def exponentials(it, e):
                    a.wait_ge(s["max_ready"], it * 2 + (e + 1))
                    for m in range(4):
                        ins = a.activation(pr[:, m * SEQ:(m + 1) * SEQ], sm[:, m * SEQ:(m + 1) * SEQ], ACT.Exp,
                                           scale=SCALE, bias=nb4[:, m:m + 1], accum_out=l4[:, m:m + 1])
                    ins.then_inc(s["probs_ready"], 1)

                def pair(it, e, last=False):
                    n1 = it * 2 + (e + 1)
                    q_piece = Piece(f"{kind}_qk", 2 * e, it, 4).later(4)
                    if two_left(it):
                        ahead(q_piece)
                    a.wait_ge(s["turned"], n1)
                    if kind == "diff":
                        a.activation(pT[:, 0:384], bank(6, 0, 384), ACT.Copy).then_inc(s["turned_ready"], 1)
                    else:
                        for m in range(2):
                            ins = a.activation(pT[:, m * 384:m * 384 + 384], bank(5 + m, 0, 384), ACT.Copy)
                        ins.then_inc(s["turned_ready"], 1)
                    if last:
                        ahead(Piece(f"{kind}_out", 0))
                    if two_left(it):
                        qk_out(it + 1, e)
                    if not last:
                        exponentials(*following(it, e))
                    if kind == "diff":
                        a.wait_ge(s["pv_done"], n1)
                        for b in range(TB):
                            ins = a.activation(squares[:, b * PARTS:(b + 1) * PARTS], bank(7, b * PARTS, PARTS), ACT.Square, accum_out=osq[:, b:b + 1])
                        ins.then_inc(s["osq_ready"], 1)
                    if two_left(it):
                        ahead(q_piece.later(1))
                    elif e == 0:
                        for g in range(3):
                            turned_group_high(k_turn, g)
                    else:
                        for k in range(1, 4):
                            ahead(Piece(f"{kind}_out", k))
                        turned_group_high(k_turn, 3)
                        for k in range(4, KC):
                            ahead(Piece(f"{kind}_out", k))

                qk_out(0, 0)
                for n in range(2):
                    ahead(Piece(f"{kind}_qk", n))
                qk_out(0, 1)
                for n in range(2, 4):
                    ahead(Piece(f"{kind}_qk", n))
                exponentials(0, 0)
                all_pairs(a, pair)

            def ffn(l):
                s = ffn_sems[l]

                def hidden(n, it=0, first=False):
                    ahead(piece_gate(l, n, it))
                    a.wait_ge(s["conv_ready"], it * 4 + (n + 1))
                    a.activation(act[n % 2], conv[n % 2], ACT.Silu).then_inc(s["silu_ready"], 1)
                    ahead(piece_up(l, n, it))
                    a.wait_ge(s["hid_ready"], it * 4 + (n + 1))
                    if not first:
                        p = piece_out(l, n - 2, it)
                        a.wait_ge(slot_done[p.slot], p.count)
                    a.activation(chunk_of(yh, n % 2), hid[n % 2], ACT.Copy).then_inc(s["hid_high"], 1)

                def step(n, it):
                    if n + 1 < FF_CHUNKS:
                        hidden(n + 1, it, first=(opening(it) and n == 0))
                    ahead(piece_out(l, n, it))

                hidden(0, first=True)
                ffn_steps(a, step)

            attention("diff", att_sems[0], 3)
            sum_squares(3, True)
            evacuate_turned(4)
            load_rows(3, 2)
            ffn(0)
            sum_squares(4, True)
            evacuate_turned(5)
            load_rows(5, 2)
            attention("fox", att_sems[1], 6)
            sum_squares(5, True)
            evacuate_turned(7)
            load_rows(7, 2)
            ffn(1)
            sum_squares(6, True)

        @block.tensor
        def _(pe):
            def turn(k, src, norm=None):
                for n in range(4):
                    t = n // 2
                    if norm is not None:
                        pe.wait_ge(normed, TB * norm + t + 1)
                    for i in range(4):
                        c = 4 * (n % 2) + i
                        ins = pe.transpose(bank(n, i * PARTS, PARTS), src[:, t * D + c * PARTS:t * D + (c + 1) * PARTS], ident)
                    ins.then_inc(turned, 1)

            def products(dst, left, right, start, stop):
                pe.matmul(dst, left[1], right[0], start=start, stop=False)
                pe.matmul(dst, left[0], right[1], start=False, stop=False)
                return pe.matmul(dst, left[0], right[0], start=False, stop=stop)

            def project_in(p, dst):
                pe.wait_ge(slot_low[p.slot], p.count)
                for k in range(KC):
                    ins = products(dst, (cols(high, p, k * PARTS, PARTS), cols(low, p, k * PARTS, PARTS)),
                                   (chunk_of(xh, k), chunk_of(xl, k)), k == 0, k == KC - 1)
                ins.then_inc(slot_done[p.slot], 1)

            def project_out(p, src_high, src_low, k, first, last, norm_next=False):
                pe.wait_ge(slot_low[p.slot], p.count)
                for t in range(TB):
                    xs = slice(k * SEQ + t * PARTS, k * SEQ + (t + 1) * PARTS)
                    for half in range(2):
                        pe.matmul(bank(2 * t + half), src_low[:, xs], cols(high, p, half * HALF, HALF), start=first, stop=False)
                    for half in range(2):
                        pe.matmul(bank(2 * t + half), src_high[:, xs], cols(low, p, half * HALF, HALF), start=False, stop=False)
                    for half in range(2):
                        ins = pe.matmul(bank(2 * t + half), src_high[:, xs], cols(high, p, half * HALF, HALF), start=False, stop=last)
                    if norm_next and last and t == 0:
                        ins.then_inc(first_tile_done, 1)
                ins.then_inc(slot_done[p.slot], 1)

            pe.wait_ge(consts_loaded, 16)
            turn(0, tmp, 0)
            pe.wait_ge(xT_ready, 4)

            def mix_round(c):
                later = not isinstance(c, int)
                dsts = [(bank(0, 0, SEQ), xc_ready), (bank(1, 0, SEQ), cv_done), (bank(1, SEQ, SEQ), None),
                        (bank(2, 0, SEQ), bb_used), (bank(3, 0, SEQ), ga_used), (bank(4, 0, SEQ), tm_ready),
                        (bank(4, SEQ, SEQ), None)]
                for g, (dst, free) in enumerate(dsts):
                    if later and free is not None:
                        pe.wait_ge(free, c)
                    project_in(Piece("mix", g, c, 8), dst)
                gate = Piece("mix", 7, c, 8)
                pe.wait_ge(xc_low, c + 1)
                pe.wait_ge(slot_low[gate.slot], gate.count)
                if later:
                    pe.wait_ge(ri_ready, c)
                for n in range(2):
                    ins = products(bank(5, n * SEQ, SEQ), (cols(high, gate, n * PARTS, PARTS), cols(low, gate, n * PARTS, PARTS)),
                                   (chunk_of(yh, 0), chunk_of(yl, 0)), True, True)
                ins.then_inc(slot_done[gate.slot], 1)

            rounds(pe, KC, mix_round)
            for k in range(KC):
                pe.wait_ge(merged_low, k + 1)
                project_out(Piece("mix_out", k), xh, xl, k, k == 0, k == KC - 1, norm_next=True)

            turn(1, tmp, 1)
            pe.wait_ge(xT_ready, 8)
            pe.wait_ge(keys_loaded, 16)
            early = 0
            for it in range(4):
                for q in range(4):
                    if it >= 1:
                        pe.wait_ge(early_gelu, early - 4 + q + 1)
                    project_in(Piece("query", 4 * it + q), bank(4 + q, 0, SEQ))
                if it >= 2:
                    pe.wait_ge(sc_ready, it - 1)
                for q in range(4):
                    pe.wait_ge(q_ready, 4 * it + q + 1)
                    for t in range(TB):
                        ins = pe.matmul(bank(2 * (it % 2) + t, q * PARTS, PARTS),
                                        qs[:, q * SEQ + t * PARTS:q * SEQ + (t + 1) * PARTS],
                                        keysT[:, (4 * it + q) * PARTS:(4 * it + q + 1) * PARTS], start=True, stop=True)
                ins.then_inc(score_done, 1)
                if it == 0:
                    pe.wait_ge(xf_ready, 1)
                for early in range(early, early + EARLY_OF_ROUND[it]):
                    pe.wait_ge(early_loaded[early % 4], 16 * (early // 4 + 1))
                    if early >= 4:
                        pe.wait_ge(early_gelu, early - 3)
                    for k in range(KC):
                        ins = pe.matmul(bank(4 + early % 4, 0, SEQ), early_u[early % 4][:, k * PARTS:(k + 1) * PARTS],
                                        chunk_of(xf, k), start=(k == 0), stop=(k == KC - 1))
                    ins.then_inc(early_done, 1)
                early += 1
            pe.wait_ge(early_gelu, EARLY)
            project_in(piece_u(0), bank(4, 0, SEQ))
            pe.wait_ge(sel_ready, 1)
            for n in range(3):
                for t in range(TB):
                    ins = pe.transpose(bank(n // 2, (n % 2) * SEQ + t * PARTS, PARTS),
                                       sel[:, n * SEQ + t * PARTS:n * SEQ + (t + 1) * PARTS], ident)
                if n != 0:
                    ins.then_inc(sel_turned, 1)
            for j in (1, 2):
                project_in(piece_u(j), bank(4 + j, 0, SEQ))

            def scatter_round(it):
                for g in range(4):
                    pe.wait_ge(one_hots_ready, it * 4 + (g + 1))
                    pe.wait_ge(act_one_hots_ready, it * 4 + (g + 1))
                    if not opening(it):
                        pe.wait_ge(early_weighed, it * 4 + (g - 3))
                    for u in range(4):
                        ins = pe.matmul(bank(g, u * PARTS, PARTS), one_hot[g % 2][:, u * PARTS:(u + 1) * PARTS],
                                        one_hot_w[g % 2][:, u * PARTS:(u + 1) * PARTS], start=True, stop=True)
                    ins.then_inc(scat_done, 1)

            rounds(pe, SEQ // 16, scatter_round)

            def expert_step(j, it):
                pe.wait_ge(coef_low, it * 4 + (j + 1))
                project_out(piece_v(j, it), chunk_of(yh, j % 2), chunk_of(yl, j % 2), 0,
                            first=(opening(it) and j == 0), last=(j == NKEYS - 1), norm_next=True)
                if j + 3 < LATE:
                    if not (opening(it) and j == 0):
                        pe.wait_ge(gelu_ready, it * 4 + j)
                    project_in(piece_u(j + 3, it), bank(4 + (j + 3) % 4, 0, SEQ))

            pe.wait_ge(early_weighed, SEQ // 4)
            expert_steps(pe, expert_step)

            turn(2, h_tok, 2)

            def attention(kind, s, k_turn):
                pe.wait_ge(xT_ready, 4 * k_turn)
                if kind == "fox":
                    project_in(Piece("fox_f", 0), bank(7, 0, SEQ))
                for k in range(KC):
                    project_out(Piece(f"{kind}_v", k), xh, xl, k, k == 0, k == KC - 1)

                def project(it, e, n):
                    project_in(Piece(f"{kind}_qk", 2 * e + n, it, 4), bank(4, n * SEQ, SEQ))

                def rotate(it, e):
                    pe.wait_ge(s["qk_ready"], it * 2 + (e + 1))
                    pe.matmul(bank(5), perm, qk[e], start=True, stop=True).then_inc(s["rotated"], 1)

                def scores(it, e):
                    src = (qkr if kind == "diff" else qk)[e]
                    pe.wait_ge(s["rope_done" if kind == "diff" else "qk_ready"], it * 2 + (e + 1))
                    if not opening(it):
                        pe.wait_ge(s["max_ready"], it * 2 + (e - 1))
                    elif e == 0:
                        pe.wait_ge(s["v_ready"], 1)
                        if kind == "fox":
                            pe.wait_ge(bias_ready, 1)
                    for t in range(TB):
                        if kind == "fox":
                            for m in range(2):
                                pe.matmul(bank(2 * e + m, t * SEQ, SEQ), ones,
                                          at(bias_rows, it * 4 * SEQ + (2 * e + m) * SEQ, SEQ), start=True, stop=False)
                        for m in range(2):
                            ins = pe.matmul(bank(2 * e + m, t * SEQ, SEQ), src[64 * m:64 * m + 64, t * PARTS:(t + 1) * PARTS],
                                            src[64 * m:64 * m + 64, SEQ:2 * SEQ], start=(kind == "diff"), stop=True)
                    ins.then_inc(s["scores_done"], 1)

                def turn_group(g):
                    pe.wait_ge(s["o_ready"], 2 * g + 2)
                    for i in range(2):
                        for t in range(TB):
                            lo = t * D + (2 * g + i) * PARTS
                            ins = pe.transpose(bank(GROUP_BANKS[g], i * SEQ + t * PARTS, PARTS), o_tok[:, lo:lo + PARTS], ident)
                    ins.then_inc(turned, 1)

                def output(k):
                    project_out(Piece(f"{kind}_out", k), xh, xl, k, k == 0, k == KC - 1, norm_next=True)

                def pair(it, e, last=False):
                    n1 = it * 2 + (e + 1)
                    if not last and kind == "diff":
                        rotate(*following(it, e))
                    if two_left(it):
                        pe.wait_ge(s["qk_ready"], it * 2 + (e + 2))
                        project(it + 1, e, 0)
                    if not last:
                        scores(*following(it, e))
                    if kind == "diff":
                        pe.wait_ge(s["mixed_ready"], n1)
                        for n, (t, k) in enumerate(((0, 0), (1, 0), (1, 1))):
                            ins = pe.transpose(bank(6, n * PARTS, PARTS), att[:, t * SEQ + k * PARTS:t * SEQ + (k + 1) * PARTS], ident)
                        ins.then_inc(s["turned"], 1)
                    else:
                        pe.wait_ge(s["probs_ready"], n1)
                        for m in range(2):
                            for n, (t, k) in enumerate(((0, 0), (1, 0), (1, 1))):
                                lo = m * HALF + t * SEQ + k * PARTS
                                ins = pe.transpose(bank(5 + m, n * PARTS, PARTS), pr[:, lo:lo + PARTS], ident)
                        ins.then_inc(s["turned"], 1)
                    if two_left(it):
                        project(it + 1, e, 1)
                    if last:
                        pe.wait_ge(s["max_ready"], HEADS)
                        pe.wait_ge(xT_ready, 4 * k_turn + 3)
                        output(0)
                    pe.wait_ge(s["turned_ready"], n1)
                    if not (opening(it) and e == 0):
                        pe.wait_ge(s["o_ready"], it * 2 + e)
                    if kind == "diff":
                        for t, terms in enumerate((((0, 0),), ((1, 0), (2, 1)))):
                            for n, k in terms:
                                ins = pe.matmul(bank(7, t * PARTS, PARTS), pT[:, n * PARTS:(n + 1) * PARTS],
                                                at(v_tok, it * 2 * PARTS + (k * D + e * PARTS), PARTS),
                                                start=(n < 2), stop=(n != 1))
                    else:
                        for m in range(2):
                            for t, terms in enumerate((((0, 0),), ((1, 0), (2, 1)))):
                                for n, k in terms:
                                    ins = pe.matmul(bank(7, (2 * m + t) * 64, 64), pT[:, m * 384 + n * PARTS:m * 384 + (n + 1) * PARTS],
                                                    at(v_tok, it * 4 * 64 + (k * D + (2 * e + m) * 64), 64),
                                                    start=(n < 2), stop=(n != 1))
                    ins.then_inc(s["pv_done"], 1)
                    if not two_left(it) and e == 0:
                        pe.wait_ge(s["max_ready"], HEADS - 1)
                        for g in range(3):
                            turn_group(g)

                project(0, 0, 0)
                project(0, 0, 1)
                if kind == "diff":
                    rotate(0, 0)
                pe.wait_ge(s["qk_ready"], 1)
                project(0, 1, 0)
                scores(0, 0)
                project(0, 1, 1)
                all_pairs(pe, pair)
                for k in range(1, 4):
                    output(k)
                turn_group(3)
                for k in range(4, 6):
                    output(k)
                pe.wait_ge(xT_ready, 4 * k_turn + 4)
                for k in range(6, KC):
                    output(k)

            def ffn(l, k_turn):
                s = ffn_sems[l]
                turn(k_turn, h_tok, 3 + 2 * l)
                pe.wait_ge(xT_ready, 4 * k_turn + 4)

                def gate_and_up(n, it=0):
                    project_in(piece_gate(l, n, it), bank(4 + 2 * (n % 2), 0, SEQ))
                    project_in(piece_up(l, n, it), bank(5 + 2 * (n % 2), 0, SEQ))

                def step(n, it):
                    if n + 1 < FF_CHUNKS:
                        if not (opening(it) and n == 0):
                            pe.wait_ge(s["hid_ready"], it * 4 + n)
                        gate_and_up(n + 1, it)
                    pe.wait_ge(s["hid_low"], it * 4 + (n + 1))
                    project_out(piece_out(l, n, it), chunk_of(yh, n % 2), chunk_of(yl, n % 2), 0,
                                first=(opening(it) and n == 0), last=(n == FF_CHUNKS - 1), norm_next=True)

                gate_and_up(0)
                ffn_steps(pe, step)

            attention("diff", att_sems[0], 3)
            ffn(0, 4)
            turn(5, h_tok, 4)
            attention("fox", att_sems[1], 6)
            ffn(1, 7)

        @block.vector
        def _(v):
            chain = Chain(v, dve_steps)
            link = chain.link

            def take_low(p, n=D):
                v.wait_ge(slot_high[p.slot], p.count)
                v.tensor_tensor(cols(low, p, 0, n), cols(raw, p, 0, n), cols(high, p, 0, n).bitcast(F32), ALU.subtract
                                ).then_inc(slot_low[p.slot], 1)

            def ahead(p, n=D):
                if p.n + RING < TOTAL:
                    take_low(p.later(RING), n)

            def low_of(dst, src, src_high):
                return v.tensor_tensor(dst, src, src_high.bitcast(F32), ALU.subtract)

            def evacuate_turned(k, gain=None):
                for n in range(4):
                    v.wait_ge(turned_high, 4 * k + n + 1)
                    if gain is None:
                        ins = low_of(turned_part(xl, n), bank(n).rearrange("p (c t) -> p c t", c=4), turned_part(xh, n))
                    else:
                        for i in range(4):
                            c = 4 * (n % 2) + i
                            ins = v.scalar_tensor_tensor(out=turned_part(xl, n)[:, i], in0=bank(n, i * PARTS, PARTS),
                                                         scalar=params[:, c * NP + gain:c * NP + gain + 1],
                                                         in1=turned_part(xh, n)[:, i].bitcast(F32), op0=ALU.mult, op1=ALU.subtract)
                    ins.then_inc(xT_ready, 1)

            def log1p_of_exp(dst, e, t):
                z, z2 = t
                link(v.tensor_scalar(z, e, 2.0, None, ALU.add))
                link(v.reciprocal(z, z))
                link(v.tensor_tensor(z, z, e, ALU.mult))
                link(v.tensor_tensor(z2, z, z, ALU.mult))
                link(v.tensor_scalar(dst, z2, 1.0 / 15.0, None, ALU.mult))
                for n in (13, 11, 9, 7, 5, 3):
                    link(v.scalar_tensor_tensor(out=dst, in0=dst, scalar=1.0 / n, in1=z2, op0=ALU.add, op1=ALU.mult))
                link(v.scalar_tensor_tensor(out=dst, in0=dst, scalar=1.0, in1=z, op0=ALU.add, op1=ALU.mult))
                link(v.tensor_scalar(dst, dst, 2.0, None, ALU.mult))

            def variance(k, b, eps):
                v.wait_ge(sumsq_ready, TB * k + b + 1)
                v.tensor_scalar(var[:, b:b + 1], sumsq[:, b:b + 1], 1.0 / D, eps, ALU.mult, ALU.add).then_inc(var_ready, 1)

            def tile(t, b):
                return t[:, b * D:(b + 1) * D]

            def rms(k):
                for b in range(TB):
                    variance(k, b, EPS_RMS)
                for b in range(TB):
                    v.wait_ge(rstd_ready, TB * k + b + 1)
                    v.tensor_scalar(tile(tmp, b), tile(h_tok, b), rstd[:, b:b + 1], None, ALU.mult).then_inc(normed, 1)

            def wait_for_tile(k, b, last):
                if b == 0:
                    v.wait_ge(first_tile_done, k)
                else:
                    v.wait_ge(slot_done[last.slot], last.count)

            def layer_norm(k, last):
                for b in range(TB):
                    wait_for_tile(k, b, last)
                    for n in (2 * b, 2 * b + 1):
                        h = h_tok[:, n * HALF:(n + 1) * HALF]
                        ins = v.scalar_tensor_tensor(out=h, in0=h, scalar=ALPHA, in1=bank(n), op0=ALU.mult, op1=ALU.add,
                                                     accum_out=sum4[:, n:n + 1])
                    link(ins)
                    mean = negmean[:, b:b + 1]
                    v.tensor_scalar(mean, sum4[:, 2 * b:2 * b + 1], sum4[:, 2 * b + 1:2 * b + 2], -1.0 / D, ALU.add, ALU.mult
                                    ).then_inc(h_ready, 1)
                v.wait_ge(rows_loaded, 16 + 32 * (k - 2))
                for b in range(TB):
                    v.wait_ge(h_ready, TB * (k - 1) + b + 1)
                    ins = v.scalar_tensor_tensor(out=tile(tmp, b), in0=tile(h_tok, b), scalar=negmean[:, b:b + 1],
                                                 in1=rows[:, 0:D], op0=ALU.add, op1=ALU.mult)
                    chain.step(ins)
                    variance(k, b, EPS_LN)
                chain.wait()
                for b in range(TB):
                    v.wait_ge(rstd_ready, TB * k + b + 1)
                    v.scalar_tensor_tensor(out=tile(h_tok, b), in0=tile(tmp, b), scalar=rstd[:, b:b + 1], in1=rows[:, D:],
                                           op0=ALU.mult, op1=ALU.add).then_inc(normed, 1)

            for b in range(TB):
                v.wait_ge(x_loaded[b], 16)
            v.wait_ge(pool_ready, 1)
            rms(0)
            take_low(Piece("mix", 0))
            v.wait_ge(small_loaded, 16 * 3)
            evacuate_turned(0, G1)
            for n in range(1, RING):
                take_low(Piece("mix", n))
            p3 = params[:, :].rearrange("p (c n) -> p c n", n=NP)
            lam, small = p3[:, :, LAM], [part(mx + 4200 + 8 * n, KC) for n in range(5)]
            link(v.tensor_scalar(small[1], lam, -1.0, None, ALU.mult))
            v.tensor_tensor(small[0], small[1], lam, ALU.max).then_inc(lam_neg, 1)
            l4v = lambdas.rearrange("p (n w d) -> p n w d", n=2, w=2)
            pairs = lam_prod.rearrange("p (n d) -> p n d", n=2)
            link(v.tensor_tensor(pairs, l4v[:, :, 0, :], l4v[:, :, 1, :], ALU.mult))
            v.tensor_reduce(lam2, pairs, AX.X, ALU.add).then_inc(lamdot_ready, 1)
            v.wait_ge(lam_exp, 1)
            log1p_of_exp(small[2], small[0], small[3:5])
            link(v.tensor_scalar(small[1], small[1], 0.0, None, ALU.max))
            link(v.tensor_tensor(small[2], small[2], small[1], ALU.add))
            v.tensor_scalar(p3[:, :, SP4], small[2], 4.0, None, ALU.mult)
            v.tensor_scalar(p3[:, :, NSP4], small[2], -4.0, None, ALU.mult)
            v.tensor_scalar(p3[:, :, HBA], p3[:, :, BA], 0.5, None, ALU.mult)
            link(v.tensor_scalar(p3[:, :, HBX], p3[:, :, BX], 0.5, None, ALU.mult))
            v.wait_ge(lamexp_ready, 1)
            link(v.tensor_tensor(nlam, lam2[:, 1:2], lam2[:, 0:1], ALU.subtract))
            link(v.tensor_scalar(nlam, nlam, -LAMBDA_INIT, None, ALU.add))
            link(v.tensor_scalar(subln[:, :], subln[:, :], 1.0 - LAMBDA_INIT, None, ALU.mult))

            def finish(c, n):
                v.wait_ge(root_ready, n)
                v.wait_ge(decay_ready, n)
                link(v.tensor_tensor(ix, ix, root, ALU.mult))
                link(v.tensor_tensor_scan(msq, decay, ix, 0.0, ALU.mult, ALU.add))
                link(v.tensor_tensor(gate_a, gate_a, msq, ALU.mult))
                v.scalar_tensor_tensor(out=at(arena, c, SEQ), in0=gate_a, scalar=0.5, in1=gate_b,
                                       op0=ALU.mult, op1=ALU.add).then_inc(merged_ready, 1)

            def merged_low_part(c):
                v.wait_ge(merged_high, c + 1)
                low_of(chunk_of(xl, c), part(M_OUT + c * SEQ, SEQ), chunk_of(xh, c)).then_inc(merged_low, 1)

            def mix_round(c, last=False):
                later = not opening(c)
                if later:
                    v.wait_ge(decay_ready, c)
                v.tensor_copy(pst, at(params, c * NP, NP)).then_inc(pst_ready, 1)
                v.wait_ge(pst_ready, c + 1)
                piece = [Piece("mix", g, c, 8) for g in range(8)]
                v.wait_ge(slot_done[0], piece[0].count)
                xa = bank(0, 0, SEQ)
                link(v.tensor_scalar(xc, xa, pst[:, CA + 3:CA + 4], pst[:, CAB:CAB + 1], ALU.mult, ALU.add))
                for k in (1, 2, 3):
                    ins = v.scalar_tensor_tensor(out=xc[:, k:], in0=xa[:, :SEQ - k], scalar=pst[:, CA + 3 - k:CA + 4 - k],
                                                 in1=xc[:, k:], op0=ALU.mult, op1=ALU.add)
                    if k < 3:
                        link(ins)
                ins.then_inc(xc_ready, 1)
                for g in range(3):
                    ahead(piece[g])
                v.wait_ge(xc_high, c + 1)
                low_of(chunk_of(yl, 0), xc, chunk_of(yh, 0)).then_inc(xc_low, 1)
                if later:
                    finish(c * SEQ + (M_OUT - SEQ), c)
                v.wait_ge(vb_ready, c + 1)
                v.tensor_tensor(cv, bank(1, SEQ, SEQ), vb_sb, ALU.mult).then_inc(cv_done, 1)
                v.wait_ge(cv_done, c + 1)
                link(v.tensor_scalar(yb, cv, pst[:, CB + 2:CB + 3], None, ALU.mult))
                for k in (1, 2):
                    link(v.scalar_tensor_tensor(out=yb[:, k:], in0=cv[:, :SEQ - k], scalar=pst[:, CB + 2 - k:CB + 3 - k],
                                                in1=yb[:, k:], op0=ALU.mult, op1=ALU.add))
                ahead(piece[3], 2 * PARTS)
                v.wait_ge(slot_done[3], piece[3].count)
                v.tensor_tensor(ybb, bank(2, 0, SEQ), yb, ALU.mult).then_inc(bb_used, 1)
                ahead(piece[4])
                v.wait_ge(sq_ready, c + 1)
                ga = bank(3, 0, SEQ)
                link(v.tensor_scalar(inner, sq, GELU_A, 1.0, ALU.mult, ALU.add))
                v.tensor_tensor(inner, ga, inner, ALU.mult).then_inc(inner_ready, 1)
                ahead(piece[5])
                v.wait_ge(tg_ready, c + 1)
                v.scalar_tensor_tensor(out=gg, in0=tg, scalar=1.0, in1=ga, op0=ALU.add, op1=ALU.mult).then_inc(ga_used, 1)
                ahead(piece[6])
                v.wait_ge(ga_used, c + 1)
                v.wait_ge(bb_used, c + 1)
                v.wait_ge(tm_ready, c + 1)
                v.scalar_tensor_tensor(out=gate_a, in0=tm[:, 0:SEQ], scalar=1.0, in1=gg,
                                       op0=ALU.add, op1=ALU.mult)
                v.scalar_tensor_tensor(out=gate_b, in0=tm[:, SEQ:], scalar=1.0, in1=ybb,
                                       op0=ALU.add, op1=ALU.mult).then_inc(tm_used, 1)
                if last:
                    for k in range(KC - 1):
                        merged_low_part(k)
                ahead(piece[7])
                v.wait_ge(ri_ready, c + 1)
                v.scalar_tensor_tensor(out=ix, in0=ti, scalar=1.0, in1=xc,
                                       op0=ALU.add, op1=ALU.mult)
                v.wait_ge(tt_ready, c + 1)
                v.wait_ge(decay_ready, c + 1)
                link(v.tensor_tensor(t1, decay, decay, ALU.mult))
                v.scalar_tensor_tensor(out=msq, in0=t1, scalar=1.0, in1=tt, op0=ALU.add, op1=ALU.mult).then_inc(m_ready, 1)

            mix_round(0)
            with v.Fori(1, KC - 1) as it:
                chain.enter(it, 11, 1)
                mix_round(it)
            chain.leave(KC - 2)
            mix_round(KC - 1, last=True)
            finish(M_OUT + (KC - 1) * SEQ, KC)
            merged_low_part(KC - 1)
            for c in range(KC - 1):
                ahead(Piece("mix_out", c))
            last = Piece("mix_out", KC - 1)
            for b in range(TB):
                wait_for_tile(1, b, last)
                for n in (2 * b, 2 * b + 1):
                    h = h_tok[:, n * HALF:(n + 1) * HALF]
                    ins = v.scalar_tensor_tensor(out=h, in0=bank(n), scalar=0.5, in1=h, op0=ALU.mult, op1=ALU.add)
                ins.then_inc(h_ready, 1)
            rms(1)
            evacuate_turned(1, G2)
            ahead(Piece("mix_out", KC - 1))
            v.wait_ge(xT_ready, 8)
            v.tensor_tensor(xf, xh[:, :].bitcast(F32), xl[:, :].bitcast(F32), ALU.add).then_inc(xf_ready, 1)

            top4 = top1.rearrange("p (b q k) -> p b q k", b=TB, q=4)
            idx4 = idxf.rearrange("p (b q k) -> p b q k", b=TB, q=4)
            for it in range(4):
                v.wait_ge(sc_ready, it + 1)
                for q in range(4 * it, min(4 * it + 4, 15)):
                    ahead(Piece("query", q))
                tiles = [(b, q) for b in range(TB) for q in range(4)]

                def scores(b, q):
                    return sc[it % 2][:, b * HALF + q * PARTS:b * HALF + (q + 1) * PARTS]

                def places(t, b, q, n):
                    return t[:, (b * 4 + q) * 16 + 8 * n:(b * 4 + q) * 16 + 8 * n + 8]

                for b, q in tiles:
                    ins = v.max(places(top1, b, q, 0), scores(b, q))
                link(ins)
                for b, q in tiles:
                    v.max_index(places(idxu, b, q, 0), places(top1, b, q, 0), scores(b, q))
                    ins = v.match_replace(rest[:, (b * 4 + q) * PARTS:(b * 4 + q + 1) * PARTS], places(top1, b, q, 0),
                                          scores(b, q), -3e38)
                ins.then_inc(sc_used, 1)
                v.wait_ge(sc_used, it + 1)
                for b, q in tiles:
                    ins = v.max(places(top1, b, q, 1), rest[:, (b * 4 + q) * PARTS:(b * 4 + q + 1) * PARTS])
                link(ins)
                for b, q in tiles:
                    ins = v.max_index(places(idxu, b, q, 1), places(top1, b, q, 1),
                                      rest[:, (b * 4 + q) * PARTS:(b * 4 + q + 1) * PARTS])
                chain.step(ins)
                c4 = cand.rearrange("p (m a b) -> p m a b", m=4, a=16)
                t4 = top1.rearrange("p (m h k) -> p m h k", m=4, h=2)
                v.tensor_tensor(c4, t4[:, :, 0, :].unsqueeze(3).to_broadcast([PARTS, 4, 16, 16]),
                                t4[:, :, 1, :].unsqueeze(2).to_broadcast([PARTS, 4, 16, 16]), ALU.add)
                chain.wait()
                link(v.tensor_copy(idxf, idxu))

                def cd(t, m):
                    return t[:, m * 256:(m + 1) * 256]

                def bp(t, m, n):
                    return t[:, m * 16 + 8 * n:m * 16 + 8 * n + 8]

                for m in range(4):
                    ins = v.max(bp(best, m, 0), cd(cand, m))
                link(ins)
                for m in range(4):
                    v.max_index(bp(posu, m, 0), bp(best, m, 0), cd(cand, m))
                    ins = v.match_replace(cd(cand2, m), bp(best, m, 0), cd(cand, m), -3e38)
                link(ins)
                for m in range(4):
                    ins = v.max(bp(best, m, 1), cd(cand2, m))
                link(ins)
                for m in range(4):
                    ins = v.max_index(bp(posu, m, 1), bp(best, m, 1), cd(cand2, m))
                link(ins)
                b3 = best.rearrange("p (m k) -> p m k", m=4)
                heads = slice(32 * it, 32 * it + 32)
                sel3 = sel.rearrange("p (n b k) -> p n b k", n=3, b=TB)

                def chosen_of(n):
                    return sel3[:, n, :, heads].rearrange("p b (h k) -> p b h k", h=2)

                b4 = best.rearrange("p (b h k) -> p b h k", b=TB, h=2)
                for b in range(TB):
                    ins = v.tensor_tensor(chosen_of(0)[:, b], b4[:, b], b4[:, b, :, 0:1].to_broadcast([PARTS, 2, 16]), ALU.subtract)
                if it == 3:
                    ins.then_inc(shifted_ready, 1)
                for n, (by, op) in enumerate(((4, ALU.logical_shift_right), (15, ALU.bitwise_and))):
                    link(v.tensor_single_scalar(digit, posu, by, op))
                    link(v.tensor_copy(digitf, digit))
                    e4 = eqs.rearrange("p (m k a) -> p m k a", m=4, k=16)
                    d3 = digitf.rearrange("p (m k) -> p m k", m=4)
                    i4 = idxf.rearrange("p (m h a) -> p m h a", m=4, h=2)
                    link(v.tensor_tensor(e4, d3.unsqueeze(3).to_broadcast([PARTS, 4, 16, 16]),
                                         iota[:, 0:16].unsqueeze(1).unsqueeze(1).to_broadcast([PARTS, 4, 16, 16]), ALU.is_equal))
                    link(v.tensor_tensor(e4, e4, i4[:, :, n, :].unsqueeze(2).to_broadcast([PARTS, 4, 16, 16]), ALU.mult))
                    for b in range(TB):
                        ins = v.tensor_reduce(chosen_of(1 + n)[:, b], e4[:, 2 * b:2 * b + 2], AX.X, ALU.add)
                    chain.step(ins)
            v.wait_ge(exp_ready, 1)
            w3 = sel[:, 0:SEQ].rearrange("p (g k) -> p g k", k=16)
            s16 = expsum[:, 0:16]
            link(v.tensor_reduce(s16, w3, AX.X, ALU.add))
            link(v.reciprocal(s16, s16))
            chain.wait()
            v.tensor_tensor(w3, w3, s16.unsqueeze(2).to_broadcast([PARTS, 16, 16]), ALU.mult).then_inc(sel_ready, 1)

            take_low(piece_v(0))
            ahead(piece_u(0))

            v.wait_ge(chosen_ready, 2)
            v.wait_ge(h_kept, 16)
            weight, sel_i, sel_j = (chosen[:, n * SEQ:(n + 1) * SEQ] for n in range(3))
            iota4 = iota.unsqueeze(1).to_broadcast([PARTS, 4, PARTS])

            def weigh_early(n, token, g):
                v.wait_ge(w_written, n)
                w = weights_of(token, LATE, NKEYS)
                v.tensor_tensor(w, w, scattered(g)[:, :, LATE:], ALU.mult).then_inc(early_weighed, 1)

            def one_hot_round(it):
                for g in range(4):
                    if not (opening(it) and g < 2):
                        v.wait_ge(scat_done, it * 4 + (g - 1))
                    v.tensor_tensor(one_hot[g % 2].rearrange("p (t i) -> p t i", t=4),
                                    at(sel_i, it * 16 + 4 * g, 4).unsqueeze(2).to_broadcast([PARTS, 4, PARTS]),
                                    iota4, ALU.is_equal)
                    for u in range(act_tokens(g)[0]):
                        ins = v.tensor_scalar(one_hot_w[g % 2][:, u * PARTS:(u + 1) * PARTS], iota,
                                              at(sel_j, it * 16 + (4 * g + u), 1), at(weight, it * 16 + (4 * g + u), 1),
                                              ALU.is_equal, ALU.mult)
                    ins.then_inc(one_hots_ready, 1)
                    if not (opening(it) and g < 2):
                        weigh_early(it * 4 + (g - 1), it * 16 + (4 * g - 8), (g - 2) % 4)

            rounds(v, SEQ // 16, one_hot_round)
            for n in (SEQ // 4 - 1, SEQ // 4):
                weigh_early(n, 4 * n - 4, (n - 1) % 4)

            def weigh(j, it=0):
                v.wait_ge(gelu_ready, it * 4 + (j + 1))
                v.tensor_tensor(coef[j % 2], coef[j % 2], at(arena, it * 4 * SEQ + j * SEQ, SEQ), ALU.mult).then_inc(coef_ready, 1)

            def coef_low_part(j, it=0):
                v.wait_ge(coef_high, it * 4 + (j + 1))
                low_of(chunk_of(yl, j % 2), coefficients(j, it), chunk_of(yh, j % 2)).then_inc(coef_low, 1)

            def expert_step(j, it):
                if j + 2 < LATE:
                    weigh(j + 2, it)
                if j < LATE - 2:
                    ahead(piece_v(j, it))
                if j + 2 < NKEYS:
                    coef_low_part(j + 2, it)
                if LATE - 2 <= j < NKEYS - 1:
                    ahead(piece_v(j, it))
                if j + 3 < LATE:
                    ahead(piece_u(j + 3, it))

            weigh(0)
            weigh(1)
            coef_low_part(0)
            coef_low_part(1)
            for j in (1, 2):
                ahead(piece_u(j))
            expert_steps(v, expert_step)
            last = piece_v(NKEYS - 1)
            v.wait_ge(h_back_loaded, 16)
            for b in range(TB):
                wait_for_tile(2, b, last)
                for n in (2 * b, 2 * b + 1):
                    cs = slice(n * HALF, (n + 1) * HALF)
                    ins = v.tensor_tensor(h_tok[:, cs], h_back[:, cs], bank(n), ALU.add)
                ins.then_inc(h_ready, 1)
            for b in range(TB):
                variance(2, b, EPS_RMS)
            v.wait_ge(rows_loaded, 16)
            for b in range(TB):
                h = tile(h_tok, b)
                v.wait_ge(rstd_ready, TB * 2 + b + 1)
                v.scalar_tensor_tensor(out=h, in0=h, scalar=rstd[:, b:b + 1], in1=rows[:, 0:D], op0=ALU.mult, op1=ALU.mult
                                       ).then_inc(normed, 1)
            evacuate_turned(2)
            ahead(piece_v(NKEYS - 1))
            v.wait_ge(pos_loaded, 16)
            v.wait_ge(consts_loaded, 16)
            ang, flip = angles[:, SEQ:], angles[:, 0:SEQ]
            link(v.tensor_copy(ang, rope[:, 0:SEQ].bitcast(I32)))
            link(v.tensor_scalar(ang, ang, freq, None, ALU.mult))
            link(v.tensor_scalar(turns, ang, 1.0 / (2.0 * math.pi), ROUND, ALU.mult, ALU.add))
            link(v.tensor_scalar(turns, turns, -ROUND, None, ALU.add))
            for c in TWO_PI_PARTS:
                link(v.scalar_tensor_tensor(out=ang, in0=turns, scalar=-c, in1=ang, op0=ALU.mult, op1=ALU.add))
            link(v.tensor_scalar(ang, ang, 3.1415925, -3.1415925, ALU.min, ALU.max))
            link(v.scalar_tensor_tensor(out=flip, in0=ang, scalar=-1.0, in1=ang, op0=ALU.mult, op1=ALU.max))
            v.tensor_scalar(flip, flip, -1.0, math.pi / 2.0, ALU.mult, ALU.add).then_inc(angle_ready, 1)

            rope2 = [rope[:, n * SEQ:(n + 1) * SEQ].unsqueeze(1).to_broadcast([PARTS, 2, SEQ]) for n in range(2)]

            def attention(kind, s, k_turn):
                v_done = 0
                if kind == "diff":
                    v.wait_ge(mask_loaded, 16)
                else:
                    ahead(Piece("fox_f", 0))
                    fz, t2, c16 = (part(14592 + 256 * n, SEQ)[0:16, :] for n in range(3))
                    t3 = part(15360, SEQ)[0:16, :]
                    v.wait_ge(slot_done[Piece("fox_f", 0).slot], Piece("fox_f", 0).count)
                    v.wait_ge(bias_loaded, 16)
                    v.wait_ge(pool_ready, 3)
                    link(v.tensor_scalar(fz, bank(7, 0, SEQ)[0:16, :], fbias[0:16, :], None, ALU.add))
                    v.scalar_tensor_tensor(out=fz_e, in0=fz, scalar=-1.0, in1=fz, op0=ALU.mult, op1=ALU.max).then_inc(fz_ready, 1)
                    for v_done in range(2):
                        ahead(Piece("fox_v", v_done))
                    v.wait_ge(fexp_ready, 1)
                    log1p_of_exp(c16, fz_e, (t2, t3))
                    link(v.tensor_scalar(fz, fz, 0.0, None, ALU.min))
                    link(v.tensor_tensor(fz, fz, c16, ALU.subtract))
                    link(v.tensor_tensor_scan(c16, ones256[0:16, :], fz, 0.0, ALU.mult, ALU.add))
                    link(v.tensor_scalar(c16, c16, -1.0 / SCALE, None, ALU.mult))
                    for v_done in range(2, 6):
                        ahead(Piece("fox_v", v_done))
                    b3 = bias_rows[0:16, :].rearrange("p (h t) -> p h t", h=16)
                    v.tensor_tensor(b3, c16.unsqueeze(1).to_broadcast([16, 16, SEQ]),
                                    head_sel[0:16, :].unsqueeze(2).to_broadcast([16, 16, SEQ]), ALU.mult).then_inc(bias_ready, 1)
                    v_done = 6
                for k in range(v_done, KC):
                    ahead(Piece(f"{kind}_v", k))

                def turned_group_low(g):
                    v.wait_ge(turned_high, 4 * k_turn + g + 1)
                    cs = slice(g * HALF, (g + 1) * HALF)
                    low_of(xl[:, cs], bank(GROUP_BANKS[g]), xh[:, cs]).then_inc(xT_ready, 1)

                def rotary(it, e):
                    v.wait_ge(s["rotated"], it * 2 + (e + 1))
                    if not opening(it):
                        v.wait_ge(s["scores_done"], it * 2 + (e - 1))
                    three = lambda t: t.rearrange("p (n t) -> p n t", n=2)
                    v.tensor_tensor(three(rot), three(bank(5)), rope2[1], ALU.mult)
                    link(v.tensor_tensor(three(qkr[e]), three(qk[e]), rope2[0], ALU.mult))
                    v.tensor_tensor(qkr[e], qkr[e], rot, ALU.add).then_inc(s["rope_done"], 1)

                def result_before(it, e):
                    n = it * 2 + e
                    place = lambda t, m: it * 256 + (t * D + e * 128 - 128 + m)
                    if kind == "diff":
                        v.wait_ge(s["osq_ready"], n)
                        v.tensor_scalar(ovar, osq, 1.0 / PARTS, EPS_RMS, ALU.mult, ALU.add).then_inc(s["ovar_ready"], 1)
                        v.wait_ge(s["orstd_ready"], n)
                        for t in range(TB):
                            ins = v.scalar_tensor_tensor(out=at(o_tok, place(t, 0), PARTS), in0=bank(7, t * PARTS, PARTS),
                                                         scalar=orstd[:, t:t + 1], in1=subln[:, :], op0=ALU.mult, op1=ALU.mult)
                    else:
                        v.wait_ge(s["pv_done"], n)
                        for m in range(2):
                            for t in range(TB):
                                ins = v.tensor_scalar(at(o_tok, place(t, 64 * m), 64), bank(7, (2 * m + t) * 64, 64),
                                                      rl4[:, 2 * m + t:2 * m + t + 1], None, ALU.mult)
                    ins.then_inc(s["o_ready"], 1)

                def maxima(it, e):
                    v.wait_ge(s["scores_done"], it * 2 + (e + 1))
                    for m in range(2):
                        ins = v.tensor_tensor(sm[:, m * HALF:(m + 1) * HALF], bank(2 * e + m), mask, ALU.add)
                    link(ins)
                    link(v.tensor_reduce(mx4, sm.rearrange("p (m k) -> p m k", m=4), AX.X, ALU.max))
                    v.tensor_scalar(nb4, mx4, -SCALE, None, ALU.mult).then_inc(s["max_ready"], 1)

                def pair(it, e, last=False):
                    n1 = it * 2 + (e + 1)
                    first = opening(it) and e == 0
                    q_piece = Piece(f"{kind}_qk", 2 * e, it, 4).later(4)
                    if kind == "diff":
                        if not last:
                            rotary(*following(it, e))
                        v.wait_ge(s["probs_ready"], n1)
                        link(v.reciprocal(rl4, l4))
                        if not first:
                            v.wait_ge(s["turned"], it * 2 + e)
                        v.tensor_scalar(rl2, rl4[:, 2:4], nlam, None, ALU.mult)
                        for t in range(TB):
                            ins = v.tensor_scalar(att[:, t * SEQ:(t + 1) * SEQ], pr[:, t * SEQ:(t + 1) * SEQ],
                                                  rl4[:, t:t + 1], None, ALU.mult)
                        link(ins)
                        for t in range(TB):
                            a_t = att[:, t * SEQ:(t + 1) * SEQ]
                            ins = v.scalar_tensor_tensor(out=a_t, in0=pr[:, HALF + t * SEQ:HALF + (t + 1) * SEQ],
                                                         scalar=rl2[:, t:t + 1], in1=a_t, op0=ALU.mult, op1=ALU.add)
                        ins.then_inc(s["mixed_ready"], 1)
                    if not first:
                        result_before(it, e)
                    if kind == "fox":
                        v.wait_ge(s["probs_ready"], n1)
                        if not first:
                            v.wait_ge(s["o_ready"], it * 2 + e)
                        link(v.reciprocal(rl4, l4))
                    if not (first or last):
                        ahead(q_piece.later(-1))
                    if two_left(it):
                        ahead(q_piece)
                    if not last:
                        maxima(*following(it, e))

                steps = 2 * (5 if kind == "diff" else 3)
                if kind == "diff":
                    v.wait_ge(rope_ready, 1)
                    rotary(0, 0)
                for n in range(2):
                    ahead(Piece(f"{kind}_qk", n))
                maxima(0, 0)
                for n in range(2, 4):
                    ahead(Piece(f"{kind}_qk", n))
                all_pairs(v, pair, chain=chain, steps=steps)
                for g in range(3):
                    turned_group_low(g)
                ahead(Piece(f"{kind}_out", 0))
                result_before(4, 0)
                for k in range(1, 4):
                    ahead(Piece(f"{kind}_out", k))
                turned_group_low(3)
                for k in range(4, KC - 1):
                    ahead(Piece(f"{kind}_out", k))

            def ffn(l):
                s = ffn_sems[l]

                def hidden(n, it=0):
                    e = n % 2
                    gate = bank(4 + 2 * e, 0, SEQ)
                    p = fpst[e]
                    link(v.tensor_copy(p, at(ffn_params, it * 16 + (l * FF_CHUNKS + n) * 4, 4)))
                    v.wait_ge(slot_done[piece_gate(l, n, it).slot], piece_gate(l, n, it).count)
                    link(v.tensor_scalar(conv[e], gate, p[:, 2:3], p[:, 3:4], ALU.mult, ALU.add))
                    for k in (1, 2):
                        ins = v.scalar_tensor_tensor(out=conv[e][:, k:], in0=gate[:, :SEQ - k], scalar=p[:, 2 - k:3 - k],
                                                     in1=conv[e][:, k:], op0=ALU.mult, op1=ALU.add)
                        if k == 1:
                            link(ins)
                    ins.then_inc(s["conv_ready"], 1)
                    ahead(piece_gate(l, n, it))
                    v.wait_ge(s["silu_ready"], it * 4 + (n + 1))
                    v.wait_ge(slot_done[piece_up(l, n, it).slot], piece_up(l, n, it).count)
                    v.tensor_tensor(hid[e], act[e], bank(5 + 2 * e, 0, SEQ), ALU.mult).then_inc(s["hid_ready"], 1)
                    ahead(piece_up(l, n, it))
                    v.wait_ge(s["hid_high"], it * 4 + (n + 1))
                    low_of(chunk_of(yl, e), hid[e], chunk_of(yh, e)).then_inc(s["hid_low"], 1)

                def step(n, it):
                    if n + 1 < FF_CHUNKS:
                        hidden(n + 1, it)
                        ahead(piece_out(l, n, it))

                v.wait_ge(ffn_params_loaded, 16)
                hidden(0)
                ffn_steps(v, step, chain, 3)

            attention("diff", att_sems[0], 3)
            layer_norm(3, Piece("diff_out", KC - 1))
            evacuate_turned(4)
            ahead(Piece("diff_out", KC - 1))
            ffn(0)
            layer_norm(4, piece_out(0, FF_CHUNKS - 1))
            evacuate_turned(5)
            ahead(piece_out(0, FF_CHUNKS - 1))
            attention("fox", att_sems[1], 6)
            layer_norm(5, Piece("fox_out", KC - 1))
            evacuate_turned(7)
            ahead(Piece("fox_out", KC - 1))
            ffn(1)
            layer_norm(6, piece_out(1, FF_CHUNKS - 1))


def _in_pieces(w):
    n = w.shape[1] // PARTS
    return w.reshape(KC, PARTS, n, PARTS).transpose(2, 1, 0, 3).reshape(n, PARTS, D)


def _by_feature(v):
    v = v.reshape(-1, v.shape[-1] // PARTS, PARTS)
    return v.transpose(2, 1, 0)


def _constants():
    c = np.zeros((PARTS, NCONST), np.float32)
    c[:, IDENT:IDENT + PARTS] = np.eye(PARTS)
    for m in range(PARTS):
        d = m % 64
        if d < 8:
            c[m + 8, PERM + m] = -1.0
        elif d < 16:
            c[m - 8, PERM + m] = 1.0
    c[:, IOTA:IOTA + PARTS] = np.arange(PARTS)
    inv = np.float32(500000.0) ** (-np.arange(0, 16, 2, dtype=np.float32) / np.float32(16))
    d = np.arange(PARTS) % 64
    c[:, FREQ] = np.where(d < 16, inv[d % 8], 0.0)
    c[:16, HSEL:HSEL + 16] = np.eye(16)
    return c


def _causal_mask():
    q, k = np.arange(PARTS)[:, None], np.arange(SEQ)[None]
    return np.concatenate([np.where(k <= q + b * PARTS, 0.0, MASKED) for b in range(TB)], 1).astype(np.float32)


def kernel(**inputs):
    import concourse.bacc as bacc
    from concourse.bass_utils import run_bass_kernel_spmd

    g = {k: np.asarray(v) for k, v in inputs.items()}
    f = np.ascontiguousarray
    w_in = g["w_in"][0].reshape(KC, PARTS, 7, KC, PARTS).transpose(2, 3, 1, 0, 4).reshape(7, KC, PARTS, D)
    w_in = w_in[[0, 2, 4, 3, 1, 5, 6]]
    params = np.zeros((PARTS, KC, NP), np.float32)
    for lo, name in ((G1, "norm1_g"), (CA, "conv_a_w"), (CAB, "conv_a_b"), (BA, "b_a"), (BX, "b_x"),
                     (LAM, "lru_lambda"), (CB, "conv_b_w"), (G2, "norm2_g")):
        v = _by_feature(g[name][0])
        params[:, :, lo:lo + v.shape[2]] = v
    ffn_params = np.stack([_by_feature(np.concatenate([g["ffn_conv_w_2"][l], g["ffn_conv_b_2"][l][None]]))
                           for l in range(2)], 1)
    diff, fox = g["diff_w_qkv_2"][0], g["fox_w_in_2"][0]

    def qk_pieces(w):
        p = _in_pieces(w[:, :2 * D])
        return p.reshape(2, 8, PARTS, D).transpose(1, 0, 2, 3).reshape(16, PARTS, D)

    ffn_in = []
    for l in range(2):
        p = _in_pieces(g["ffn_w_in_2"][l])
        ffn_in.append(p.reshape(2, FF_CHUNKS, PARTS, D).transpose(1, 0, 2, 3).reshape(2 * FF_CHUNKS, PARTS, D))
    arrays = {
        "x": g["x"][0].reshape(TB, PARTS, D).transpose(1, 0, 2),
        "w_mix": w_in,
        "w_gate": np.concatenate([g["w_a"][0], g["w_x"][0]], axis=2),
        "w_out": g["w_out"][0].reshape(KC, PARTS, D),
        "w_query": _in_pieces(g["peer_wq"][0]),
        "keys": g["peer_subkeys"][0].transpose(3, 0, 1, 2).reshape(PARTS, 16 * PARTS),
        "u_tab": g["peer_u"][0].reshape(PARTS, PARTS, KC, PARTS).transpose(1, 3, 2, 0).reshape(PARTS, PARTS, D),
        "v_tab": g["peer_v"][0].reshape(PARTS, PARTS, D).transpose(1, 0, 2),
        "diff_qk": qk_pieces(diff),
        "diff_v": diff[:, 2 * D:].reshape(KC, PARTS, D),
        "diff_out": g["diff_w_o_2"][0].reshape(KC, PARTS, D),
        "fox_qk": qk_pieces(fox),
        "fox_v": fox[:, 2 * D:3 * D].reshape(KC, PARTS, D),
        "fox_f": _in_pieces(np.pad(fox[:, 3 * D:], ((0, 0), (0, PARTS - 16))))[0],
        "fox_out": g["fox_w_o_2"][0].reshape(KC, PARTS, D),
        "mask": _causal_mask(),
        "ffn_in": np.stack(ffn_in),
        "ffn_out": g["ffn_w_out_2"].reshape(2, FF_CHUNKS, PARTS, D),
        "consts": _constants(),
        "params": params.reshape(PARTS, KC * NP),
        "ffn_params": ffn_params.reshape(PARTS, 2 * FF_CHUNKS * 4),
        "rows": np.stack([g["final_g"]] + [g[f"{n}_2"][l] for l in range(2) for n in ("ln1_g", "ln1_b", "ln2_g", "ln2_b")]),
        "subln": g["diff_subln_g_2"],
        "lambdas": np.stack([g[f"diff_lambda_{n}_2"][0] for n in ("q1", "k1", "q2", "k2")]).reshape(1, 256),
        "forget_bias": g["fox_b_f_2"].reshape(16, 1),
        "positions": g["positions_2"].astype(np.int32),
    }
    nc = bacc.Bacc("TRN2", target_bir_lowering=False, num_devices=1)
    arrays = {f"in_{k}": f(v) for k, v in arrays.items()}
    args = [nc.dram_tensor(k, v.shape, mybir.dt.from_np(v.dtype), kind="ExternalInput").ap() for k, v in arrays.items()]
    out = nc.dram_tensor("out", (PARTS, TB, D), F32, kind="ExternalOutput").ap()
    h_saved = nc.dram_tensor("h_saved", (PARTS, TB * D), F32, kind="Internal").ap()
    build(nc, *args, h_saved, out)
    r = run_bass_kernel_spmd(nc, [arrays], core_ids=[0])
    got = r.results[0]["out"]
    return np.ascontiguousarray(got.transpose(1, 0, 2).reshape(1, SEQ, D))
```
